# Optimizing a Trainium2 kernel written in Bass

```python
import math
import jax, jax.numpy as jnp
from jax import lax
import numpy as np

D_MODEL = 1024
BATCH = 1
SEQ = 128
DEPTH = 2
DEC_BATCH = 1
DEC_SEQ = 512
PAST_LEN = 128

GRID_W = 64
N_HEADS = 8
HEAD_DIM = 64
W_ATT = N_HEADS * HEAD_DIM
NA_ROWS = 8
NA_COLS = 16
NA_SPAN = 2 * NA_COLS
ROPE_BASE = 10000.0
Q_BLOCK = 128
W_CONV = 512
CONV_K = 31
W_POOL = 512
POOL_WINDOWS = (2, 4, 8, 16)
POOL_GROUP = W_POOL // len(POOL_WINDOWS)
W_SGU = 512
SGU_GROUPS = 4
SGU_GROUP_W = W_SGU // SGU_GROUPS
SGU_CHUNK = 128
N_BRANCH = 4
BRANCH_W = 512
N_EXPERTS = 16
EC_CAPACITY = 2
D_EXPERT = 1024
EPS = 1e-6
NEG_INF = -1e30

IN_SIZES = (W_ATT, W_ATT, W_ATT, 2 * W_CONV, W_POOL, W_SGU, W_SGU, N_BRANCH * D_MODEL)
D_IN = sum(IN_SIZES)
IN_SPLITS = tuple(int(s) for s in np.cumsum(IN_SIZES)[:-1])

kernel_name = "hybrid_diffusion_parallel_mixer_step"

def rmsnorm(x, g):
    xf = x.astype(jnp.float32)
    y = xf * lax.rsqrt(jnp.mean(xf * xf, axis=-1, keepdims=True) + EPS)
    return (y * g.astype(jnp.float32)).astype(x.dtype)

def layernorm(x, g, b):
    xf = x.astype(jnp.float32)
    mu = jnp.mean(xf, axis=-1, keepdims=True)
    var = jnp.mean(jnp.square(xf - mu), axis=-1, keepdims=True)
    y = (xf - mu) * lax.rsqrt(var + EPS)
    return (y * g.astype(jnp.float32) + b.astype(jnp.float32)).astype(x.dtype)

def modulate(h, shift, scale):
    return h * (1 + scale[:, None, :]) + shift[:, None, :]

def adaln(cond, w, b):
    return jax.nn.silu(cond) @ w + b

def axial_rope(x):
    L = x.shape[1]
    t = np.arange(L)
    half = HEAD_DIM // 2
    nf = half // 2
    inv = (1.0 / (ROPE_BASE ** (np.arange(nf) / nf))).astype(np.float32)

    def rot(xa, pos):
        ang = (pos[:, None].astype(np.float32) * inv[None, :]).astype(np.float32)
        cos = jnp.asarray(np.cos(ang))[None, :, None, :]
        sin = jnp.asarray(np.sin(ang))[None, :, None, :]
        x1, x2 = xa[..., :nf], xa[..., nf:]
        return jnp.concatenate([x1 * cos - x2 * sin, x1 * sin + x2 * cos], axis=-1)

    xf = x.astype(jnp.float32)
    out = jnp.concatenate([rot(xf[..., :half], t // GRID_W), rot(xf[..., half:], t % GRID_W)], axis=-1)
    return out.astype(x.dtype)

def dense_context_attention(q, ck, cv):
    B, Lc, H, hd = q.shape
    nb = Lc // Q_BLOCK
    qb = q.reshape(B, nb, Q_BLOCK, H, hd).transpose(1, 0, 2, 3, 4)

    def one(qblk):
        s = jnp.einsum('bqhd,bhkd->bhqk', qblk, ck).astype(jnp.float32)
        p = jax.nn.softmax(s, axis=-1).astype(cv.dtype)
        return jnp.einsum('bhqk,bhkd->bqhd', p, cv)

    o = lax.map(one, qb)
    return o.transpose(1, 0, 2, 3, 4).reshape(B, Lc, H, hd)

def neighbourhood_attention(q_rot, q_plain, k_rot, v, ck, cv, rpb):
    B, L, H, hd = q_rot.shape
    rows = L // GRID_W
    kh = min(NA_ROWS, rows)
    ncb = GRID_W // NA_COLS
    r = np.arange(rows)
    row_idx = np.clip(r - kh // 2, 0, rows - kh)[:, None] + np.arange(kh)[None, :]
    d_row = row_idx - r[:, None] + (NA_ROWS - 1)
    cb = np.arange(ncb)
    span_idx = np.clip(cb * NA_COLS - NA_COLS // 2, 0, GRID_W - NA_SPAN)[:, None] + np.arange(NA_SPAN)[None, :]
    qcol = np.arange(GRID_W).reshape(ncb, NA_COLS)
    col_start = np.clip(qcol - NA_COLS // 2, 0, GRID_W - NA_COLS)
    keycol = span_idx[:, None, :]
    col_valid = (keycol >= col_start[..., None]) & (keycol < col_start[..., None] + NA_COLS)
    d_col = np.clip(keycol - qcol[..., None], -(NA_COLS - 1), NA_COLS - 1) + (NA_COLS - 1)
    bias = rpb.astype(jnp.float32)[:, d_row[:, None, None, :, None], d_col[None, :, :, None, :]]
    bias = jnp.where(jnp.asarray(col_valid)[None, None, :, :, None, :], bias, NEG_INF)
    bias = bias.transpose(1, 2, 0, 3, 4, 5)

    kg = k_rot.reshape(B, rows, GRID_W, H, hd)
    vg = v.reshape(B, rows, GRID_W, H, hd)
    to_rows = lambda a: a.reshape(B, rows, ncb, NA_COLS, H, hd).transpose(1, 0, 2, 3, 4, 5)
    n_loc = kh * NA_SPAN

    def one_row(args):
        qr, qp, ridx, brow = args
        kb = kg[:, ridx][:, :, span_idx]
        vb = vg[:, ridx][:, :, span_idx]
        s_loc = jnp.einsum('bnqhd,bknshd->bnhqks', qr, kb).astype(jnp.float32) + brow[None]
        s_ctx = jnp.einsum('bnqhd,bhcd->bnhqc', qp, ck).astype(jnp.float32)
        s = jnp.concatenate([s_loc.reshape(B, ncb, H, NA_COLS, n_loc), s_ctx], axis=-1)
        p = jax.nn.softmax(s, axis=-1).astype(v.dtype)
        p_loc = p[..., :n_loc].reshape(B, ncb, H, NA_COLS, kh, NA_SPAN)
        p_ctx = p[..., n_loc:]
        return (jnp.einsum('bnhqks,bknshd->bnqhd', p_loc, vb)
                + jnp.einsum('bnhqc,bhcd->bnqhd', p_ctx, cv))

    o = lax.map(one_row, (to_rows(q_rot), to_rows(q_plain), jnp.asarray(row_idx, jnp.int32), bias))
    return o.transpose(1, 0, 2, 3, 4, 5).reshape(B, L, H, hd)

def context_attention_branch(q, k, v):
    B, L = q.shape[:2]
    ck, cv = k.transpose(0, 2, 1, 3), v.transpose(0, 2, 1, 3)
    o = dense_context_attention(q * (HEAD_DIM ** -0.5), ck, cv)
    return o.reshape(B, L, W_ATT), (ck, cv)

def latent_attention_branch(q, k, v, ck, cv, rpb):
    B, L = q.shape[:2]
    scale = HEAD_DIM ** -0.5
    o = neighbourhood_attention(axial_rope(q) * scale, q * scale, axial_rope(k), v, ck, cv, rpb)
    return o.reshape(B, L, W_ATT), None

def conformer_conv(z, conv_w, conv_b, ln_g, ln_b):
    a, g = jnp.split(z, 2, axis=-1)
    y = a * jax.nn.sigmoid(g)
    y = lax.conv_general_dilated(y, conv_w[:, None, :], window_strides=(1,),
                                 padding=[(CONV_K // 2, CONV_K // 2)],
                                 dimension_numbers=('NWC', 'WIO', 'NWC'),
                                 feature_group_count=W_CONV) + conv_b
    return jax.nn.silu(layernorm(y, ln_g, ln_b))

def multiscale_pool(z, pool_w, pool_scale):
    B, L, _ = z.shape
    ng = len(POOL_WINDOWS)
    zg = z.reshape(B, L, ng, POOL_GROUP)
    zf = zg.astype(jnp.float32)
    csum = jnp.concatenate([jnp.zeros((B, 1, ng, POOL_GROUP), jnp.float32), jnp.cumsum(zf, axis=1)], axis=1)
    t = np.arange(L)
    means = []
    for gi, w in enumerate(POOL_WINDOWS):
        lo = np.clip(t - w // 2, 0, L - 1)
        hi = np.clip(t + w - w // 2 - 1, 0, L - 1)
        cnt = jnp.asarray((hi - lo + 1).astype(np.float32))
        means.append((csum[:, hi + 1, gi] - csum[:, lo, gi]) / cnt[None, :, None])
    d = (jnp.stack(means, axis=2) - zf).astype(z.dtype)
    y = jnp.einsum('blgc,gce->blge', d, pool_w).reshape(B, L, W_POOL)
    return y * pool_scale

def spatial_gating(u, v, ln_g, ln_b, sgu_w, sgu_b):
    B, L, _ = u.shape
    nc = L // SGU_CHUNK
    vg = layernorm(v, ln_g, ln_b).reshape(B, nc, SGU_CHUNK, SGU_GROUPS, SGU_GROUP_W)
    mixed = jnp.einsum('gpq,bnqgc->bnpgc', sgu_w, vg) + sgu_b.T[None, None, :, :, None]
    return u * mixed.reshape(B, L, W_SGU)

def expert_choice_ffn(h, w_router, w1, w3, w2):
    B, L, D = h.shape
    cap = EC_CAPACITY * L // N_EXPERTS
    aff = jax.nn.softmax((h @ w_router).astype(jnp.float32), axis=-1)
    gate, idx = lax.top_k(aff.transpose(0, 2, 1), cap)
    xs = jax.vmap(lambda hb, ib: hb[ib])(h, idx)
    a = jnp.einsum('becd,edf->becf', xs, w1)
    b = jnp.einsum('becd,edf->becf', xs, w3)
    y = jnp.einsum('becf,efd->becd', jax.nn.silu(a) * b, w2) * gate[..., None].astype(h.dtype)
    return jax.vmap(lambda yb, ib: jnp.zeros((L, D), yb.dtype).at[ib.reshape(-1)].add(yb.reshape(-1, D)))(y, idx)

def token_mixers(h, attn_fn, lp):
    B, L, _ = h.shape
    proj = h @ lp['w_in']
    q, k, v, z_conv, z_pool, z_u, z_v, z_gate = jnp.split(proj, IN_SPLITS, axis=-1)
    shp = (B, L, N_HEADS, HEAD_DIM)
    o_att, kv = attn_fn(q.reshape(shp), k.reshape(shp), v.reshape(shp))
    o_conv = conformer_conv(z_conv, lp['conv_w'], lp['conv_b'], lp['conv_ln_g'], lp['conv_ln_b'])
    o_pool = multiscale_pool(z_pool, lp['pool_w'], lp['pool_scale'])
    o_sgu = spatial_gating(jax.nn.gelu(z_u), jax.nn.gelu(z_v), lp['sgu_ln_g'], lp['sgu_ln_b'], lp['sgu_w'], lp['sgu_b'])
    branches = jnp.stack([o_att, o_conv, o_pool, o_sgu], axis=2)
    proj_b = jnp.einsum('blnc,ncd->blnd', branches, lp['w_branch'])
    gates = jax.nn.sigmoid(z_gate.reshape(B, L, N_BRANCH, D_MODEL))
    merged = jnp.sum(gates * proj_b, axis=2)
    return merged @ lp['w_out'], kv

def run_layer(x, mod, attn_fn, lp):
    shift1, scale1, gate1, shift2, scale2, gate2 = jnp.split(mod, 6, axis=-1)
    h = modulate(rmsnorm(x, lp['norm1_g']), shift1, scale1)
    mix, kv = token_mixers(h, attn_fn, lp)
    x = x + gate1[:, None, :] * mix
    h2 = modulate(rmsnorm(x, lp['norm2_g']), shift2, scale2)
    x = x + gate2[:, None, :] * expert_choice_ffn(h2, lp['w_router'], lp['w1'], lp['w3'], lp['w2'])
    return x, kv

def setup_inputs(seed: int = 0) -> dict:
    key = jax.random.key(seed)
    ks = iter(jax.random.split(key, 40))
    nrm = lambda shape, s: jax.random.normal(next(ks), shape, jnp.float32) * s
    D = D_MODEL
    return {
        'x_prompt': nrm((BATCH, SEQ, D), 1.0),
        'x_sample': nrm((DEC_BATCH, DEC_SEQ, D), 1.0),
        'cache_k': nrm((DEC_BATCH, DEPTH, N_HEADS, PAST_LEN, HEAD_DIM), 1.0),
        'cache_v': nrm((DEC_BATCH, DEPTH, N_HEADS, PAST_LEN, HEAD_DIM), 1.0),
        'c': nrm((DEC_BATCH, D), 1.0),
        'c_ctx': nrm((D,), 1.0),
        'w_ada': nrm((DEPTH, D, 6 * D), 0.5 * D ** -0.5),
        'b_ada': nrm((DEPTH, 6 * D), 0.02),
        'norm1_g': 1.0 + nrm((DEPTH, D), 0.02),
        'w_in': nrm((DEPTH, D, D_IN), D ** -0.5),
        'rpb': nrm((DEPTH, N_HEADS, 2 * NA_ROWS - 1, 2 * NA_COLS - 1), 0.1),
        'conv_w': nrm((DEPTH, CONV_K, W_CONV), CONV_K ** -0.5),
        'conv_b': nrm((DEPTH, W_CONV), 0.02),
        'conv_ln_g': 1.0 + nrm((DEPTH, W_CONV), 0.02),
        'conv_ln_b': nrm((DEPTH, W_CONV), 0.02),
        'pool_w': nrm((DEPTH, len(POOL_WINDOWS), POOL_GROUP, POOL_GROUP), POOL_GROUP ** -0.5),
        'pool_scale': 1.0 + nrm((DEPTH, W_POOL), 0.02),
        'sgu_ln_g': 1.0 + nrm((DEPTH, W_SGU), 0.02),
        'sgu_ln_b': nrm((DEPTH, W_SGU), 0.02),
        'sgu_w': nrm((DEPTH, SGU_GROUPS, SGU_CHUNK, SGU_CHUNK), SGU_CHUNK ** -0.5),
        'sgu_b': 1.0 + nrm((DEPTH, SGU_GROUPS, SGU_CHUNK), 0.02),
        'w_branch': nrm((DEPTH, N_BRANCH, BRANCH_W, D), BRANCH_W ** -0.5),
        'w_out': nrm((DEPTH, D, D), D ** -0.5),
        'norm2_g': 1.0 + nrm((DEPTH, D), 0.02),
        'w_router': nrm((DEPTH, D, N_EXPERTS), D ** -0.5),
        'w1': nrm((DEPTH, N_EXPERTS, D, D_EXPERT), D ** -0.5),
        'w3': nrm((DEPTH, N_EXPERTS, D, D_EXPERT), D ** -0.5),
        'w2': nrm((DEPTH, N_EXPERTS, D_EXPERT, D), D_EXPERT ** -0.5),
        'final_g': 1.0 + nrm((D,), 0.02),
    }

def reference(x_prompt, x_sample, cache_k, cache_v, c, c_ctx, w_ada, b_ada, norm1_g, w_in, rpb,
              conv_w, conv_b, conv_ln_g, conv_ln_b, pool_w, pool_scale, sgu_ln_g, sgu_ln_b, sgu_w, sgu_b,
              w_branch, w_out, norm2_g, w_router, w1, w3, w2, final_g):
    xp, xs = x_prompt, x_sample
    new_k, new_v = [], []
    for l in range(DEPTH):
        lp = {
            'norm1_g': norm1_g[l], 'w_in': w_in[l],
            'conv_w': conv_w[l], 'conv_b': conv_b[l], 'conv_ln_g': conv_ln_g[l], 'conv_ln_b': conv_ln_b[l],
            'pool_w': pool_w[l], 'pool_scale': pool_scale[l],
            'sgu_ln_g': sgu_ln_g[l], 'sgu_ln_b': sgu_ln_b[l], 'sgu_w': sgu_w[l], 'sgu_b': sgu_b[l],
            'w_branch': w_branch[l], 'w_out': w_out[l], 'norm2_g': norm2_g[l],
            'w_router': w_router[l], 'w1': w1[l], 'w3': w3[l], 'w2': w2[l],
        }
        mod_ctx = adaln(c_ctx[None, :], w_ada[l], b_ada[l])
        xp, (k_l, v_l) = run_layer(xp, mod_ctx, context_attention_branch, lp)
        new_k.append(k_l)
        new_v.append(v_l)
        mod_lat = adaln(c, w_ada[l], b_ada[l])
        ck, cv, rpb_l = cache_k[:, l], cache_v[:, l], rpb[l]
        attn_lat = lambda q, k, v, ck=ck, cv=cv, rpb_l=rpb_l: latent_attention_branch(q, k, v, ck, cv, rpb_l)
        xs, _ = run_layer(xs, mod_lat, attn_lat, lp)
    y_prompt = rmsnorm(xp, final_g)
    y_sample = rmsnorm(xs, final_g)
    new_cache_k = jnp.stack(new_k, axis=1)
    new_cache_v = jnp.stack(new_v, axis=1)
    return (y_prompt, y_sample, new_cache_k, new_cache_v)


_drawn_inputs = setup_inputs


def setup_inputs(seed=0):
    import zlib

    import numpy as np

    out = dict(_drawn_inputs(seed))
    spreads = {}
    factors = {'cache_k': 3.915,
     'cache_v': 3.288,
     'norm1_g': 2.902,
     'rpb': 8.0,
     'conv_b': 7.116,
     'conv_ln_g': 8.0,
     'conv_ln_b': 21.395,
     'pool_scale': 8.0,
     'sgu_ln_g': 8.0,
     'sgu_ln_b': 8.0,
     'sgu_b': 8.0,
     'norm2_g': 6.863,
     'final_g': 7.448}
    for name, (base, spread) in spreads.items():
        noise = np.random.default_rng([zlib.crc32(name.encode()), seed]).standard_normal(out[name].shape)
        drawn = base * np.exp(spread * noise) if base else spread * noise
        out[name] = __import__('jax').numpy.asarray(drawn.astype(out[name].dtype))
    for name, factor in factors.items():
        out[name] = (out[name] * factor).astype(out[name].dtype)
    return out
```

```python
from contextlib import ExitStack

import numpy as np

import concourse.bass as bass
from concourse import mybir

F32 = mybir.dt.float32
ALU = mybir.AluOpType
ACT = mybir.ActivationFunctionType
AX = mybir.AxisListType.X

P = 128
LAYERS = 2
D = 1024
KC = D // P
LAT, CTX = 512, 128
TOK = LAT + CTX
HALF = TOK // 2
TT = TOK // P
HEADS, HD = 8, 64
PAIRS = HEADS // 2
GRID_W, ROWS, COLS = 64, LAT // 64, 16
BW = 512
BC = BW // P
TAPS = 31
CPAD = TAPS // 2
CLEN = LAT + CPAD + CTX
CCTX = LAT + CPAD
PPAD = 8
PLEN = PPAD + LAT + PPAD + CTX + PPAD
PCTX = PPAD + LAT + PPAD
NE = 16
CAPL, CAPC = 2 * LAT // NE, 2 * CTX // NE
CAP = CAPL + CAPC
EPAIRS = NE // 2
EPS = 1e-6
NEG = -1e30
SLOTS = 3
WIDE = 48

ADA_BLOCKS = 12
IN_CONV, IN_POOL, IN_U, IN_V, IN_Q, IN_K, IN_VAL = 12, 14, 15, 16, 17, 18, 19
GATE_ORDER = (2, 3, 1, 0)
OUT_BLOCK = 32
MIX_BLOCKS = 34
EXP_BLOCKS = 6


def first_in_slot(n):
    return n // SLOTS


def per_layer(s):
    mixer = len(range(s, MIX_BLOCKS, SLOTS))
    return mixer + EXP_BLOCKS * NE // SLOTS


def _layout(parts):
    at, out = 0, {}
    for name, n in parts:
        out[name] = at
        at += n
    return out, at


PAR, NPAR = _layout([("b_ada", 48), ("g1", KC), ("g2", KC), ("conv_b", BC), ("conv_g", BC),
                     ("conv_beta", BC), ("pool_scale", BC), ("conv_w", BC * TAPS), ("router", KC * NE),
                     ("pool_w", BW), ("sgu_w", BW), ("sgu_g", BW), ("sgu_beta", BW), ("sgu_b", BW)])
CON, NCON = _layout([("cos", LAT), ("sin", LAT), ("ident", P), ("ones", P), ("perm", P),
                     ("mask", 3 * 32), ("edge", 4 * 2 * 8), ("iota", CAPL), ("row64", 1), ("row16", 1),
                     ("final_g", KC)])


def group_major(ap):
    return ap.rearrange("p (g r j) -> p r g j", g=8, r=ROWS)


def in_rows(ap):
    return ap.rearrange("p (r g j) -> p r g j", g=8, r=ROWS)


def step_kernel(nc, a):
    with ExitStack() as ctx:
        def sb(name, n):
            return ctx.enter_context(nc.sbuf_tensor(name, [P, n], F32))

        def sem(name):
            return ctx.enter_context(nc.semaphore(name))

        ring = sb("ring", SLOTS * 4096)
        xT = sb("xT", KC * TOK)
        hT = sb("hT", KC * TOK)
        region_m = sb("region_m", 5120)
        region_b = sb("region_b", 3 * BC * TOK + BC * 656)
        region_r = sb("region_r", 7168)
        params = sb("params", NPAR)
        consts = sb("consts", NCON)
        sq = sb("sq", 2 * 656)
        sig = sb("sig", 2 * TOK)
        rstd = sb("rstd", 656)
        mod = sb("mod", 96)
        mscale = sb("mscale", 2 * 2 * KC)
        cond = sb("cond", 2 * KC)
        small = sb("small", 96)
        PS = [ctx.enter_context(nc.psum_tensor(f"ps{i}", [P, 2, 512], F32)) for i in range(4)]

        def par(name, n):
            return params[:, PAR[name]:PAR[name] + n]

        def con(name, n):
            return consts[:, CON[name]:CON[name] + n]

        x = xT[:, :].rearrange("p (k t) -> p k t", k=KC)
        h = hT[:, :].rearrange("p (k t) -> p k t", k=KC)
        ones, ident, perm = con("ones", P), con("ident", P), con("perm", P)
        cosT, sinT = con("cos", LAT), con("sin", LAT)
        mod3 = mod[:, :].rearrange("p (c g) -> p c g", g=2)
        msc = mscale[:, :].rearrange("p (n k g) -> p n k g", n=2, g=2)
        sq2 = sq[:, :].rearrange("p (b t) -> p b t", b=2)
        sig2 = sig[:, :].rearrange("p (b t) -> p b t", b=2)
        br_att = region_b[:, 0:2560].rearrange("p (c t) -> p c t", c=BC)
        br_pool = region_b[:, 2560:5120].rearrange("p (c t) -> p c t", c=BC)
        br_sgu = region_b[:, 5120:7680].rearrange("p (c t) -> p c t", c=BC)
        br_conv = region_b[:, 7680:7680 + BC * 656].rearrange("p (c t) -> p c t", c=BC)
        YP = CPAD + LAT + CPAD + CTX + CPAD
        ypad = region_b[:, 0:2 * YP].rearrange("p (b t) -> p b t", b=2)
        vT = br_att
        zp = region_m[:, 0:4 * PLEN].rearrange("p (c t) -> p c t", c=BC)
        psum_a = region_m[:, 4 * PLEN:5 * PLEN]
        psum_b = region_m[:, 5 * PLEN:6 * PLEN]
        qs = region_m[:, 0:2560].rearrange("p (c t) -> p c t", c=PAIRS)
        q_rot = region_m[:, 2560:4608].rearrange("p (c t) -> p c t", c=PAIRS)
        kctx = region_m[:, 4608:5120].rearrange("p (c t) -> p c t", c=PAIRS)
        k_rot = region_r[:, 0:2048].rearrange("p (c t) -> p c t", c=PAIRS)
        val = region_r[:, 2048:4608].rearrange("p (t c) -> p t c", t=TT)
        ck = region_r[:, 4608:5120].rearrange("p (c t) -> p c t", c=PAIRS)
        cv = region_r[:, 5120:5632]
        bias_m = region_r[:, 5632:7168].rearrange("p (b v s) -> p b v s", b=2, v=3)
        bias_w = rstd[:, 0:ROWS * WIDE].rearrange("p (r s) -> p r s", r=ROWS)
        prob = sq[:, 0:2 * 448].rearrange("p (b s) -> p b s", b=2)
        prob_t = sig[:, 0:1024].rearrange("p (b s) -> p b s", b=2)
        gv = region_r[:, 0:2560].rearrange("p (t c) -> p t c", t=TT)
        nmax, rsum, rinv = small[:, 0:2], small[:, 2:4], small[:, 4:6]
        stats6 = small[:, 8:38].rearrange("p (t s) -> p t s", t=TT)
        stats2 = small[:, 38:48].rearrange("p (t s) -> p t s", t=TT)
        vroot = small[:, 48:53]
        merged = region_m[:, :].rearrange("p (k t) -> p k t", k=KC)
        h_tok = region_m[:, :].rearrange("p (t d) -> p t d", t=TT)
        pick_l = region_b[:, 0:4096].rearrange("p (t e c) -> p t e c", t=4, e=NE)
        pick_c = region_b[:, 4096:4352].rearrange("p (e c) -> p e c", e=NE)
        put_l = region_b[:, 4352:8448].rearrange("p (q t) -> p q t", q=EPAIRS)
        put_c = region_b[:, 8448:9472].rearrange("p (q t) -> p q t", q=EPAIRS)
        xs = region_r[:, 0:2 * KC * CAP].rearrange("p (b k c) -> p b k c", b=2, k=KC)
        sil = region_r[:, 1280:1920].rearrange("p (k c) -> p k c", k=KC)
        act = region_r[:, 1920:2560].rearrange("p (k c) -> p k c", k=KC)
        yt_l = region_r[:, 2560:3584].rearrange("p (k c) -> p k c", k=KC)
        yt_c = region_r[:, 3584:3840].rearrange("p (k c) -> p k c", k=KC)
        y_l = region_r[:, 3840:4864]
        y_c = region_r[:, 4864:5888]
        spread = region_r[:, 5888:7168]
        affT = region_r[0:NE, 0:640]
        affW = region_r[0:NE, 640:1280]
        selT = region_r[0:NE, 1280:1920]
        cumT = region_r[0:NE, 1920:2560]
        slotT = sig[0:NE, 0:TOK]
        aff = rstd[:, 0:80].rearrange("p (t e) -> p t e", t=TT)
        slot_tok = rstd[:, 80:160].rearrange("p (t e) -> p t e", t=TT)
        rt_max, rt_sum = small[:, 56:61], small[:, 61:66]

        slot_loaded = [sem(f"slot_loaded{i}") for i in range(SLOTS)]
        slot_used = [sem(f"slot_used{i}") for i in range(SLOTS)]
        start_in, cond_ready = sem("start_in"), sem("cond_ready")
        layer_done, all_idle, layer_go = sem("layer_done"), sem("all_idle"), sem("layer_go")
        stored, kv_stored, bias_in = sem("stored"), sem("kv_stored"), sem("bias_in")
        out_ready, final_sq, final_sum, final_root, final_xr = (
            sem(n) for n in ("out_ready", "final_sq", "final_sum", "final_root", "final_xr"))
        names = """params_in cache_in spread_in dve_step pool_step
            squared square_used norm_sum var_ready root_ready xr_ready h_ready ada_done mod_ready
            tile_done conv_sig conv_in pool_in u_ready zv_ready q_in k_in v_in
            pads_zero conv_acc conv_mean conv_centred conv_var conv_norm conv_ready
            pool_d poolw_done pool_ready sgu_norm sgu_mixed sgu_ready turned roped
            v_turned v_tok prob_pad bias_built bias_read
            s_done s_ready p_exp p_norm p_turned pt_ready o_done o_ready
            gate_done gate_sig br_done br_used out_done x_mixed
            logits logit_sub aff_exp aff_ready aff_turned aff_copied slot_ready slot_turned slot_copied spread_done
            spread_aff put_ready h2_turned h2_tok_a h2_tok_d pick_ready
            gathered xs_ready a_done b_done sil_ready act_ready y_done yl_ready yc_ready
            t_done ytok_ready yctok_ready c_done c_used""".split()
        S = {n: sem(n) for n in names}
        cleared = [S[n].num for n in names]
        assert cleared == list(range(cleared[0], cleared[0] + len(cleared)))

        block = ctx.enter_context(nc.Block())

        def linker(eng, own):
            n = {}

            def link(ins, name=own):
                n[name] = n.get(name, 0) + 1
                ins.then_inc(S[name], 1)
                eng.wait_ge(S[name], n[name])
            return link

        @block.sync
        def _(sp):
            def load(slot, before, src):
                sp.wait_ge(slot_used[slot], before)
                sp.dma_start(ring[:, slot * 4096:(slot + 1) * 4096], src).then_inc(slot_loaded[slot], 16)

            sp.dma_start(xT[:, :], a["x0"]).then_inc(start_in, 16)
            sp.dma_start(consts[:, :], a["consts"]).then_inc(start_in, 16)
            with sp.Fori(0, LAYERS) as l:
                for n in range(MIX_BLOCKS):
                    s = n % SLOTS
                    load(s, l * per_layer(s) + first_in_slot(n), a["w_mix"][l, n])
                with sp.Fori(0, EPAIRS) as q:
                    for b in range(2 * EXP_BLOCKS):
                        s = (MIX_BLOCKS + b) % SLOTS
                        load(s, l * per_layer(s) + q * (2 * EXP_BLOCKS // SLOTS)
                             + first_in_slot(MIX_BLOCKS + b),
                             a["w_exp"][l, q, b])
            for k in range(KC):
                sp.wait_ge(out_ready, 2 * (k + 1))
                sp.dma_start(a["y"][:, k, :], h[:, k, :]).then_inc(stored, 16)
            sp.wait_ge(stored, 16 * KC)
            sp.wait_ge(kv_stored, 2 * 16 * LAYERS)

        @block.tensor
        def _(pe):
            pending = []

            def mm(*args, **kw):
                ins = pe.matmul(*args, **kw)
                if pending:
                    ins.then_inc(slot_used[pending.pop(0)], 1)
                return ins

            def weights(l, n, more=0):
                s = n % SLOTS
                pe.wait_ge(slot_loaded[s], (l * per_layer(s) + more) * 16 + 16 * (first_in_slot(n) + 1))
                return ring[:, s * 4096:(s + 1) * 4096].rearrange("p (k n) -> p k n", k=KC)

            def read(n):
                pending.append(n % SLOTS)

            evac = []
            for c in range(BC):
                evac += [("conv_sig", 2 * (c + 1)), ("conv_in", 2 * (c + 1))]
            evac += [("pool_in", 2 * (g + 1)) for g in range(BC)]
            evac += [("u_ready", g + 1) for g in range(BC)]
            evac += [("zv_ready", t + 1) for t in range(TT)]
            for name in ("q_in", "k_in", "v_in"):
                evac += [(name, 2 * (g + 1)) for g in range(BC)]
            tile = [0]

            def tile_slot():
                n = tile[0]
                tile[0] += 1
                if n >= 3:
                    name, v = evac[n - 3]
                    pe.wait_ge(S[name], v)
                return PS[n % 3]

            def columns(split):
                return ((0, 0, HALF), (1, HALF, TOK)) if split == "half" else ((0, 0, LAT), (1, LAT, TOK))

            def project(w, m, split):
                ps = tile_slot()
                for k in range(KC):
                    if tile[0] == 1:
                        pe.wait_ge(S["h_ready"], 2 * (k + 1))
                    for b, t0, t1 in columns(split):
                        args = dict(start=k == 0, stop=k == KC - 1)
                        at = (ps[:, b, 0:t1 - t0], w[:, k, m * P:(m + 1) * P], h[:, k, t0:t1])
                        last = (pe.matmul if (k, b) == (KC - 1, 1) else mm)(*at, **args)
                last.then_inc(S["tile_done"], 1)

            def norm_sum(ps, base, signal):
                for k in range(KC):
                    pe.wait_ge(S["squared"], base + k + 1)
                    for b, t0, t1 in columns("half"):
                        last = pe.matmul(ps[:, b, 0:HALF], ones, sq2[:, k % 2, t0:t1], start=k == 0, stop=k == KC - 1)
                    last.then_inc(S["square_used" if k < KC - 1 else signal], 1)

            pe.wait_ge(start_in, 16 * 3)
            pe.wait_ge(cond_ready, 1)
            with pe.Fori(0, LAYERS) as l:
                tile[0] = 0
                cnd = cond[:, :].rearrange("p (k g) -> p k g", g=2)
                for n in range(ADA_BLOCKS):
                    w = weights(l, n)
                    for m in range(4):
                        at = PS[3][:, 0, (4 * n + m) * 2:(4 * n + m) * 2 + 2]
                        for k in range(KC):
                            end = (n, m, k) == (ADA_BLOCKS - 1, 3, KC - 1)
                            last = (pe.matmul if end else mm)(at, w[:, k, m * P:(m + 1) * P], cnd[:, k, :],
                                                              start=k == 0, stop=k == KC - 1)
                    read(n)
                    if n == 3:
                        norm_sum(PS[2], 0, "norm_sum")
                last.then_inc(S["ada_done"], 1)
                for c in range(BC):
                    w = weights(l, IN_CONV + c // 2)
                    for j in range(2):
                        project(w, 2 * (c % 2) + j, "group")
                    if c % 2:
                        read(IN_CONV + c // 2)
                w = weights(l, IN_POOL)
                for g in range(BC):
                    project(w, g, "group")
                read(IN_POOL)
                w = weights(l, IN_U)
                for g in range(BC):
                    project(w, g, "half")
                read(IN_U)

                def over_channels(source, ready, done):
                    pe.wait_ge(*ready)
                    for c in range(BC):
                        if source is sq2:
                            pe.wait_ge(S["squared"], KC + 2 * (c + 1))
                        for b, t0, t1 in ((0, 0, LAT), (1, CCTX, CLEN)):
                            src = source[:, c % 2, t0:t1] if source is sq2 else source[:, c, t0:t1]
                            last = (pe.matmul if b else mm)(PS[3][:, b, 0:t1 - t0], ones, src,
                                                            start=c == 0, stop=c == BC - 1)
                        if source is sq2 and c < BC - 1:
                            last.then_inc(S["square_used"], 1)
                    last.then_inc(S[done], 1)

                pe.wait_ge(S["mod_ready"], 1)
                over_channels(br_conv, (S["conv_acc"], BC), "conv_mean")
                w = weights(l, IN_V)
                for t in range(TT):
                    ps = tile_slot()
                    for k in range(KC):
                        last = (pe.matmul if k == KC - 1 else mm)(
                            ps[:, 0, :], h[:, k, t * P:(t + 1) * P], w[:, k, :], start=k == 0, stop=k == KC - 1)
                    last.then_inc(S["tile_done"], 1)
                read(IN_V)
                over_channels(sq2, (S["conv_centred"], 8), "conv_var")
                for g in range(BC):
                    pe.wait_ge(S["pool_d"], g + 1)
                    if g:
                        pe.wait_ge(S["pool_ready"], 2 * g)
                    else:
                        pe.wait_ge(S["conv_norm"], 2)
                    pw = par("pool_w", BW)[:, g * P:(g + 1) * P]
                    pe.matmul(PS[3][:, 0, :], pw, zp[:, g, PPAD:PPAD + LAT], start=True, stop=True)
                    pe.matmul(PS[3][:, 1, 0:CTX], pw, zp[:, g, PCTX:PCTX + CTX], start=True,
                              stop=True).then_inc(S["poolw_done"], 1)

                def turn(name, src, m, n):
                    pe.wait_ge(S[name], 2 * (m + 1))
                    if n >= 2:
                        pe.wait_ge(S["roped"], n - 1)
                    pe.matmul(PS[3][:, n % 2, :], perm, src[:, m, 0:LAT], start=True,
                              stop=True).then_inc(S["turned"], 1)

                w = weights(l, IN_Q)
                for m in range(PAIRS):
                    project(w, m, "group")
                    if m == 0:
                        pe.wait_ge(S["pool_ready"], 2 * BC)
                    if m:
                        turn("q_in", qs, m - 1, m - 1)
                read(IN_Q)
                for g in range(BC):
                    if g == 0:
                        turn("q_in", qs, 3, 3)
                        pe.wait_ge(S["roped"], 4)
                        pe.wait_ge(S["sgu_norm"], TT)
                    else:
                        pe.wait_ge(S["sgu_ready"], g)
                    for t in range(TT):
                        last = pe.matmul(PS[3][:, t // 4, (t % 4) * P:(t % 4 + 1) * P],
                                         gv[:, t, g * P:(g + 1) * P], par("sgu_w", BW)[:, g * P:(g + 1) * P],
                                         start=True, stop=True)
                    last.then_inc(S["sgu_mixed"], 1)
                w = weights(l, IN_K)
                for m in range(PAIRS):
                    project(w, m, "group")
                    if m == 1:
                        pe.wait_ge(S["sgu_ready"], BC)
                    if m:
                        turn("k_in", k_rot, m - 1, 4 + m - 1)
                read(IN_K)
                w = weights(l, IN_VAL)
                for m in range(PAIRS):
                    project(w, m, "group")
                    if m == 0:
                        turn("k_in", k_rot, 3, 7)
                read(IN_VAL)
                for t in range(TT):
                    pe.wait_ge(S["v_in"], 2 * PAIRS)
                    if t < 2:
                        pe.wait_ge(S["roped"], 8)
                    else:
                        pe.wait_ge(S["v_tok"], t - 1)
                    for m in range(PAIRS):
                        last = pe.transpose(PS[3][:, t % 2, m * P:(m + 1) * P], vT[:, m, t * P:(t + 1) * P], ident)
                    last.then_inc(S["v_turned"], 1)

                units = attention_units()
                pe.wait_ge(S["v_tok"], TT)
                pe.wait_ge(S["v_in"], 2 * PAIRS)
                pe.wait_ge(S["roped"], 8)
                pe.wait_ge(S["cache_in"], 32)

                def scores(u):
                    head, cb = units[u]
                    hb, m = (head % 2) * HD, head // 2
                    if u >= 2:
                        pe.wait_ge(S["s_ready"], u - 1)
                    ps = PS[0][:, u % 2, :]
                    if cb is None:
                        pe.matmul(ps[:, 256:384], qs[hb:hb + HD, m, LAT:TOK], kctx[hb:hb + HD, m, :],
                                  start=True, stop=True).then_inc(S["s_done"], 1)
                        return
                    s0 = span_start(cb) * ROWS
                    pe.matmul(ps[:, 0:256], q_rot[hb:hb + HD, m, cb * P:(cb + 1) * P],
                              k_rot[hb:hb + HD, m, s0:s0 + 256], start=True, stop=True)
                    pe.matmul(ps[:, 256:384], qs[hb:hb + HD, m, cb * P:(cb + 1) * P], ck[hb:hb + HD, m, :],
                              start=True, stop=True).then_inc(S["s_done"], 1)

                def turn_probs(u):
                    pe.wait_ge(S["p_norm"], u + 1)
                    if u >= 2:
                        pe.wait_ge(S["pt_ready"], u - 1)
                    for i, (c0, _, _) in enumerate(key_chunks(units[u][1])):
                        last = pe.transpose(PS[1][:, u % 2, i * P:(i + 1) * P], prob[:, u % 2, c0:c0 + P], ident)
                    last.then_inc(S["p_turned"], 1)

                def weigh_values(u):
                    head, cb = units[u]
                    hb = (head % 2) * HD
                    pe.wait_ge(S["pt_ready"], u + 1)
                    m = head // 2
                    if hb == 0 and (cb == 0) and m >= 2:
                        pe.wait_ge(S["o_ready"], 2 * (m - 1))
                    chunks = key_chunks(cb)
                    out = PS[3][hb:hb + HD, m % 2, 0:P] if cb is None else \
                        PS[2][hb:hb + HD, m % 2, cb * P:(cb + 1) * P]
                    for i, (_, n, src) in enumerate(chunks):
                        v = val[0:n, src, head * HD:(head + 1) * HD] if src != "cache" else \
                            cv[:, head * HD:(head + 1) * HD]
                        last = pe.matmul(out, v, prob_t[0:n, u % 2, i * P:(i + 1) * P], start=i == 0,
                                         stop=i == len(chunks) - 1)
                    last.then_inc(S["o_done"], 1)

                for u in range(len(units) + 2):
                    if u < len(units):
                        scores(u)
                    if 1 <= u <= len(units):
                        turn_probs(u - 1)
                    if u >= 2:
                        weigh_values(u - 2)

                pe.wait_ge(S["o_ready"], 2 * PAIRS)
                pe.wait_ge(S["conv_ready"], BC)
                i = 0
                for o, n in enumerate(GATE_ORDER):
                    base = 20 + 3 * o
                    split = "group" if n == 1 else "half"
                    src = {0: br_att, 1: br_conv, 2: br_pool, 3: br_sgu}[n]
                    for m in range(KC):
                        if m % 4 == 0:
                            wg = weights(l, base + (2 if m else 0))
                        if i >= 2:
                            pe.wait_ge(S["gate_sig"], 2 * (i - 1))
                        for k in range(KC):
                            for b, t0, t1 in columns(split):
                                last = (pe.matmul if (k, b) == (KC - 1, 1) else mm)(
                                    PS[2 * (i % 2)][:, b, 0:t1 - t0], wg[:, k, (m % 4) * P:(m % 4 + 1) * P],
                                    h[:, k, t0:t1], start=k == 0, stop=k == KC - 1)
                        last.then_inc(S["gate_done"], 1)
                        if m == 0:
                            weights(l, base + 1)
                            s = (base + 1) % SLOTS
                            wb = ring[:, s * 4096:(s + 1) * 4096].rearrange("p (k n) -> p k n", k=BC)
                        if i >= 2:
                            pe.wait_ge(S["br_used"], i - 1)
                        for k in range(BC):
                            for b, t0, t1 in columns(split):
                                rhs = src[:, k, CCTX:CLEN] if n == 1 and b else src[:, k, t0:t1]
                                last = (pe.matmul if (k, b) == (BC - 1, 1) else mm)(
                                    PS[2 * (i % 2) + 1][:, b, 0:t1 - t0], wb[:, k, m * P:(m + 1) * P],
                                    rhs, start=k == 0, stop=k == BC - 1)
                        last.then_inc(S["br_done"], 1)
                        i += 1
                        if m == 3:
                            read(base)
                    read(base + 1)
                    read(base + 2)
                pe.wait_ge(S["br_used"], i)
                for m in range(KC):
                    w = weights(l, OUT_BLOCK + m // 4)
                    if m >= 2:
                        pe.wait_ge(S["x_mixed"], 2 * (m - 1))
                    for k in range(KC):
                        for b, t0, t1 in columns("group"):
                            last = (pe.matmul if (k, b) == (KC - 1, 1) else mm)(
                                PS[m % 2][:, b, 0:t1 - t0], w[:, k, (m % 4) * P:(m % 4 + 1) * P],
                                merged[:, k, t0:t1], start=k == 0, stop=k == KC - 1)
                    last.then_inc(S["out_done"], 1)
                    if m % 4 == 3:
                        read(OUT_BLOCK + m // 4)
                norm_sum(PS[2], KC + 2 * BC, "norm_sum")

                for t in range(TT):
                    for k in range(KC):
                        pe.wait_ge(S["h_ready"], 2 * (KC + k + 1))
                        last = (mm if k < KC - 1 else pe.matmul)(
                            PS[3][:, 0, t * NE:(t + 1) * NE], h[:, k, t * P:(t + 1) * P],
                            par("router", KC * NE)[:, k * NE:(k + 1) * NE], start=k == 0, stop=k == KC - 1)
                last.then_inc(S["logits"], 1)
                for t in range(TT):
                    if t >= 2:
                        name = "h2_tok_a" if t % 2 == 0 else "h2_tok_d"
                        pe.wait_ge(S[name], t // 2)
                    for k in range(KC):
                        last = pe.transpose(PS[t % 2][:, k // 4, (k % 4) * P:(k % 4 + 1) * P],
                                            h[:, k, t * P:(t + 1) * P], ident)
                    last.then_inc(S["h2_turned"], 1)
                pe.wait_ge(S["aff_ready"], 1)
                for t in range(TT):
                    last = pe.transpose(PS[2][0:NE, t // 4, (t % 4) * P:(t % 4 + 1) * P], aff[:, t, :], ident)
                last.then_inc(S["aff_turned"], 1)
                pe.wait_ge(S["slot_ready"], 1)
                for t in range(TT):
                    last = pe.transpose(PS[3][:, 0, t * NE:(t + 1) * NE], slotT[:, t * P:(t + 1) * P],
                                        ident[0:NE, 0:NE])
                last.then_inc(S["slot_turned"], 1)
                pe.wait_ge(S["spread_in"], 16)
                pe.wait_ge(S["h2_tok_a"], 3)
                pe.wait_ge(S["h2_tok_d"], 2)
                for q in range(EPAIRS):
                    if q:
                        pe.wait_ge(S["put_ready"], 2 * q)
                    el = spread[0:NE, q * P:(q + 1) * P]
                    ec = spread[0:NE, D + q * 32:D + (q + 1) * 32]
                    pe.matmul(PS[0][:, 0, :], el, slotT[:, 0:LAT], start=True, stop=True)
                    pe.matmul(PS[0][0:32, 1, 0:CTX], ec, slotT[:, LAT:TOK], start=True, stop=True)
                    pe.matmul(PS[1][:, 0, :], el, affT[:, 0:LAT], start=True, stop=True)
                    pe.matmul(PS[1][0:32, 1, 0:CTX], ec, affT[:, LAT:TOK], start=True,
                              stop=True).then_inc(S["spread_done"], 1)
                pe.wait_ge(S["put_ready"], 2 * EPAIRS)
                pe.wait_ge(S["pick_ready"], TT)

                with pe.Fori(0, EPAIRS) as q:
                    for j in range(2):
                        if j:
                            pe.wait_ge(S["xs_ready"], q * 2 + 1)
                        else:
                            pe.wait_ge(S["ytok_ready"], q)
                        for k in range(KC):
                            at = PS[0][:, k // 4, (k % 4) * CAP:(k % 4 + 1) * CAP]
                            for t in range(4):
                                mm(at[:, 0:CAPL], h_tok[:, t, k * P:(k + 1) * P], pick_l[:, t, q * 2 + j, :],
                                   start=t == 0, stop=t == 3)
                            last = pe.matmul(at[:, CAPL:CAP], h_tok[:, 4, k * P:(k + 1) * P],
                                             pick_c[:, q * 2 + j, :], start=True, stop=True)
                        last.then_inc(S["gathered"], 1)
                        pe.wait_ge(S["xs_ready"], q * 2 + j + 1)
                        for i, (ps, done) in enumerate(((PS[1], "a_done"), (PS[2], "b_done"), (PS[3], "y_done"))):
                            if i == 0:
                                if j:
                                    pe.wait_ge(S["sil_ready"], q * 2 + 1)
                                else:
                                    pe.wait_ge(S["yctok_ready"], q)
                            elif i == 1:
                                if j:
                                    pe.wait_ge(S["act_ready"], q * 2 + 1)
                                else:
                                    pe.wait_ge(S["c_used"], q * 8)
                            else:
                                pe.wait_ge(S["act_ready"], q * 2 + j + 1)
                                if j:
                                    pe.wait_ge(S["yl_ready"], q * 2 + 1)
                                    pe.wait_ge(S["yc_ready"], q * 2 + 1)
                            for m in range(KC):
                                n = MIX_BLOCKS + EXP_BLOCKS * j + 2 * i + m // 4
                                if m % 4 == 0:
                                    w = weights(l, n, q * (2 * EXP_BLOCKS // SLOTS))
                                for k in range(KC):
                                    rhs = act[:, k, :] if i == 2 else xs[:, j, k, :]
                                    last = (pe.matmul if (m, k) == (KC - 1, KC - 1) else mm)(
                                        ps[:, m // 4, (m % 4) * CAP:(m % 4 + 1) * CAP],
                                        w[:, k, (m % 4) * P:(m % 4 + 1) * P], rhs,
                                        start=k == 0, stop=k == KC - 1)
                                if m % 4 == 3:
                                    read(n)
                            last.then_inc(S[done], 1)
                    pe.wait_ge(S["yl_ready"], q * 2 + 2)
                    for k in range(KC):
                        last = pe.transpose(PS[0][:, k // 4, (k % 4) * P:(k % 4 + 1) * P], yt_l[:, k, :], ident)
                        if pending:
                            last.then_inc(slot_used[pending.pop(0)], 1)
                    last.then_inc(S["t_done"], 1)
                    pe.wait_ge(S["yc_ready"], q * 2 + 2)
                    for k in range(KC):
                        last = pe.transpose(PS[1][0:32, k // 4, (k % 4) * P:(k % 4 + 1) * P], yt_c[:, k, :], ident)
                    last.then_inc(S["t_done"], 1)
                    pe.wait_ge(S["ytok_ready"], q + 1)
                    pe.wait_ge(S["yctok_ready"], q + 1)
                    for k in range(KC):
                        if k >= 2:
                            pe.wait_ge(S["c_used"], q * 8 + k - 1)
                        ps = PS[2 + k % 2]
                        pe.matmul(ps[:, 0, :], y_l[:, k * P:(k + 1) * P], put_l[:, q, :], start=True, stop=True)
                        pe.matmul(ps[:, 1, 0:CTX], y_c[0:32, k * P:(k + 1) * P], put_c[0:32, q, :], start=True,
                                  stop=True).then_inc(S["c_done"], 1)
                assert not pending
                pe.drain().then_inc(layer_done, 1)
                pe.wait_ge(layer_go, l + 1)
            for k in range(KC):
                pe.wait_ge(final_sq, k + 1)
                for b, t0, t1 in columns("half"):
                    last = pe.matmul(PS[0][:, b, 0:HALF], ones, h[:, k, t0:t1], start=k == 0, stop=k == KC - 1)
            last.then_inc(final_sum, 1)

        @block.scalar
        def _(sc):
            sc.dma_start(cond[:, :], a["cond"]).then_inc(start_in, 16)
            sc.wait_ge(start_in, 16 * 3)
            sc.activation(cond[:, :], cond[:, :], ACT.Silu).then_inc(cond_ready, 1)

            def squares(base):
                for k in range(KC):
                    if k >= 2:
                        sc.wait_ge(S["square_used"], base + k - 1)
                    sc.activation(sq2[:, k % 2, 0:TOK], x[:, k, :], ACT.Square).then_inc(S["squared"], 1)

            def root(name, n, ap):
                sc.wait_ge(S[name], n)
                sc.activation(ap, ap, ACT.Sqrt).then_inc(S["root_ready"], 1)

            def modulate(norm):
                sc.wait_ge(S["mod_ready"], 3)
                for k in range(KC):
                    sc.wait_ge(S["xr_ready"], KC * norm + k + 1)
                    for g, (t0, t1) in enumerate(((0, LAT), (LAT, TOK))):
                        sc.activation(h[:, k, t0:t1], h[:, k, t0:t1], ACT.Identity,
                                      scale=msc[:, norm, k, g:g + 1],
                                      bias=mod3[:, 24 * norm + k, g:g + 1]).then_inc(S["h_ready"], 1)

            def tile_of(n):
                sc.wait_ge(S["tile_done"], n + 1)
                return PS[n % 3]

            with sc.Fori(0, LAYERS) as l:
                sc.dma_start(params[:, :], a["params"][l]).then_inc(S["params_in"], 16)
                squares(0)
                root("var_ready", 1, rstd[:, 0:TOK])
                modulate(0)
                sc.wait_ge(S["params_in"], 16)
                for c in range(BC):
                    ps = tile_of(2 * c)
                    if c >= 2:
                        sc.wait_ge(S["conv_in"], 2 * (c - 1))
                    for b, t0, t1 in ((0, 0, LAT), (1, LAT, TOK)):
                        sc.activation(sig2[:, c % 2, t0:t1], ps[:, b, 0:t1 - t0], ACT.Sigmoid).then_inc(S["conv_sig"], 1)
                sc.wait_ge(S["pads_zero"], 1)
                for g in range(BC):
                    ps = tile_of(8 + g)
                    sc.activation(zp[:, g, PPAD:PPAD + LAT], ps[:, 0, :], ACT.Copy).then_inc(S["pool_in"], 1)
                    sc.activation(zp[:, g, PCTX:PCTX + CTX], ps[:, 1, 0:CTX], ACT.Copy).then_inc(S["pool_in"], 1)
                for g in range(BC):
                    ps = tile_of(12 + g)
                    sc.activation(br_sgu[:, g, :].rearrange("p (b t) -> p b t", b=2), ps[:, :, 0:HALF],
                                  ACT.Gelu_apprx_tanh).then_inc(S["u_ready"], 1)
                for t in range(TT):
                    ps = tile_of(16 + t)
                    sc.activation(gv[:, t, :], ps[:, 0, :], ACT.Gelu_apprx_tanh).then_inc(S["zv_ready"], 1)
                for c in range(BC):
                    sc.wait_ge(S["conv_centred"], 2 * (c + 1))
                    if c >= 2:
                        sc.wait_ge(S["square_used"], KC - 1 + c - 1)
                    for t0, t1 in ((0, LAT), (CCTX, CLEN)):
                        sc.activation(sq2[:, c % 2, t0:t1], br_conv[:, c, t0:t1],
                                      ACT.Square).then_inc(S["squared"], 1)
                sc.dma_start(ck, a["ck"][l]).then_inc(S["cache_in"], 16)
                sc.dma_start(cv, a["cv"][l]).then_inc(S["cache_in"], 16)
                root("conv_norm", 2, rstd[:, 0:CLEN])
                root("var_ready", 2, vroot)
                for c in range(BC):
                    sc.wait_ge(S["conv_norm"], 2 + c + 1)
                    sc.activation(br_conv[:, c, 0:CLEN], br_conv[:, c, 0:CLEN], ACT.Silu,
                                  scale=par("conv_g", BC)[:, c:c + 1],
                                  bias=par("conv_beta", BC)[:, c:c + 1]).then_inc(S["conv_ready"], 1)
                for g in range(BC):
                    sc.wait_ge(S["poolw_done"], g + 1)
                    for b, t0, t1 in ((0, 0, LAT), (1, LAT, TOK)):
                        sc.activation(br_pool[:, g, t0:t1], PS[3][:, b, 0:t1 - t0], ACT.Copy,
                                      scale=par("pool_scale", BC)[:, g:g + 1]).then_inc(S["pool_ready"], 1)

                def by_group(n, dst, ctx_dst, scale, name):
                    ps = tile_of(n)
                    sc.activation(group_major(dst), in_rows(ps[:, 0, :]), ACT.Copy, scale=scale).then_inc(S[name], 1)
                    sc.activation(ctx_dst, ps[:, 1, 0:CTX], ACT.Copy, scale=scale).then_inc(S[name], 1)

                for m in range(PAIRS):
                    by_group(21 + m, qs[:, m, 0:LAT], qs[:, m, LAT:TOK], HD ** -0.5, "q_in")
                sc.wait_ge(S["sgu_mixed"], BC)
                for m in range(PAIRS):
                    by_group(25 + m, k_rot[:, m, :], kctx[:, m, :], 1.0, "k_in")
                for m in range(PAIRS):
                    by_group(29 + m, vT[:, m, 0:LAT], vT[:, m, LAT:TOK], 1.0, "v_in")
                sc.wait_ge(S["k_in"], 2 * PAIRS)
                sc.dma_start(a["new_k"][l], kctx).then_inc(kv_stored, 16)
                sc.wait_ge(S["v_tok"], TT)
                sc.dma_start(a["new_v"][l], val[:, 4, :]).then_inc(kv_stored, 16)

                units = attention_units()

                def exp_scores(u):
                    sc.wait_ge(S["s_ready"], u + 1)
                    lo = 320 if units[u][1] is None else 64
                    sc.activation(prob[:, u % 2, lo:448], prob[:, u % 2, lo:448], ACT.Exp,
                                  bias=nmax[:, u % 2:u % 2 + 1], accum_out=rsum[:, u % 2:u % 2 + 1]).then_inc(S["p_exp"], 1)

                def copy_turned(u):
                    chunks = key_chunks(units[u][1])
                    sc.wait_ge(S["p_turned"], u + 1)
                    if u >= 2:
                        sc.wait_ge(S["o_done"], u - 1)
                    sc.activation(prob_t[:, u % 2, 0:len(chunks) * P], PS[1][:, u % 2, 0:len(chunks) * P],
                                  ACT.Copy).then_inc(S["pt_ready"], 1)

                for u in range(len(units) + 1):
                    if u < len(units):
                        exp_scores(u)
                    if u >= 1:
                        copy_turned(u - 1)

                i = 0
                for n in GATE_ORDER:
                    for m in range(KC):
                        sc.wait_ge(S["gate_done"], i + 1)
                        if i >= 2:
                            sc.wait_ge(S["br_used"], i - 1)
                        ps = PS[2 * (i % 2)]
                        if n == 1:
                            for b, t0, t1 in ((0, 0, LAT), (1, LAT, TOK)):
                                sc.activation(sig2[:, i % 2, t0:t1], ps[:, b, 0:t1 - t0],
                                              ACT.Sigmoid).then_inc(S["gate_sig"], 1)
                        else:
                            sc.activation(sig2[:, i % 2, :].rearrange("p (b t) -> p b t", b=2), ps[:, :, 0:HALF],
                                          ACT.Sigmoid).then_inc(S["gate_sig"], 2)
                        i += 1
                for k in range(KC):
                    sc.wait_ge(S["x_mixed"], 2 * (k + 1))
                    if k >= 2:
                        sc.wait_ge(S["square_used"], KC - 1 + BC - 1 + k - 1)
                    sc.activation(sq2[:, k % 2, 0:TOK], x[:, k, :], ACT.Square).then_inc(S["squared"], 1)
                sc.dma_start(spread[0:NE, :], a["spread"]).then_inc(S["spread_in"], 16)
                root("var_ready", 3, rstd[:, 0:TOK])
                modulate(1)
                sc.wait_ge(S["logit_sub"], 1)
                sc.activation(aff, aff, ACT.Exp).then_inc(S["aff_exp"], 1)
                for t in range(0, TT, 2):
                    sc.wait_ge(S["h2_turned"], t + 1)
                    sc.activation(h_tok[:, t, :].rearrange("p (b d) -> p b d", b=2), PS[t % 2][:, :, :],
                                  ACT.Copy).then_inc(S["h2_tok_a"], 1)
                sc.wait_ge(S["aff_turned"], 1)
                sc.activation(affT[:, 0:LAT], PS[2][0:NE, 0, :], ACT.Copy).then_inc(S["aff_copied"], 1)
                sc.activation(affT[:, LAT:TOK], PS[2][0:NE, 1, 0:CTX], ACT.Copy).then_inc(S["aff_copied"], 1)
                for q in range(EPAIRS):
                    sc.wait_ge(S["spread_done"], q + 1)
                    if q >= 2:
                        sc.wait_ge(S["put_ready"], 2 * (q - 1))
                    sc.activation(sq2[:, q % 2, 0:LAT], PS[1][:, 0, :], ACT.Copy).then_inc(S["spread_aff"], 1)
                    sc.activation(sq2[0:32, q % 2, LAT:TOK], PS[1][0:32, 1, 0:CTX], ACT.Copy).then_inc(S["spread_aff"], 1)
                with sc.Fori(0, EPAIRS) as q:
                    for j in range(2):
                        sc.wait_ge(S["gathered"], q * 2 + j + 1)
                        sc.activation(xs[:, j].rearrange("p (b k) c -> p b (k c)", b=2), PS[0][:, :, 0:4 * CAP],
                                      ACT.Copy).then_inc(S["xs_ready"], 1)
                        sc.wait_ge(S["a_done"], q * 2 + j + 1)
                        sc.wait_ge(S["act_ready"], q * 2 + j)
                        sc.activation(sil.rearrange("p (b k) c -> p b (k c)", b=2), PS[1][:, :, 0:4 * CAP],
                                      ACT.Silu).then_inc(S["sil_ready"], 1)
                        sc.wait_ge(S["y_done"], q * 2 + j + 1)
                        sc.activation(yt_l[:, :, j * CAPL:(j + 1) * CAPL].rearrange("p (b k) c -> p b k c", b=2),
                                      PS[3][:, :, 0:4 * CAP].rearrange("p b (k c) -> p b k c", k=4)[:, :, :, 0:CAPL],
                                      ACT.Copy).then_inc(S["yl_ready"], 1)
                        sc.activation(yt_c[:, :, j * CAPC:(j + 1) * CAPC].rearrange("p (b k) c -> p b k c", b=2),
                                      PS[3][:, :, 0:4 * CAP].rearrange("p b (k c) -> p b k c", k=4)[:, :, :, CAPL:CAP],
                                      ACT.Copy).then_inc(S["yc_ready"], 1)
                    sc.wait_ge(S["t_done"], q * 2 + 1)
                    sc.activation(y_l.rearrange("p (b d) -> p b d", b=2), PS[0][:, :, :], ACT.Copy).then_inc(S["ytok_ready"], 1)
                sc.drain().then_inc(layer_done, 1)
                sc.wait_ge(layer_go, l + 1)
            for k in range(KC):
                sc.activation(h[:, k, :], x[:, k, :], ACT.Square).then_inc(final_sq, 1)
            sc.wait_ge(final_root, 1)
            sc.activation(rstd[:, 0:TOK], rstd[:, 0:TOK], ACT.Sqrt).then_inc(final_root, 1)

        @block.vector
        def _(v):
            def layer_body(l):
                link = linker(v, "dve_step")
                v.wait_ge(S["params_in"], 16)

                def normalise(norm, n):
                    v.wait_ge(S["norm_sum"], norm + 1)
                    v.tensor_scalar(rstd[:, 0:TOK].rearrange("p (b t) -> p b t", b=2), PS[2][:, :, 0:HALF],
                                    1.0 / D, EPS, ALU.mult, ALU.add).then_inc(S["var_ready"], 1)
                    v.wait_ge(S["root_ready"], n)
                    link(v.reciprocal(rstd[:, 0:TOK], rstd[:, 0:TOK]))
                    for k in range(KC):
                        v.tensor_tensor(h[:, k, :], x[:, k, :], rstd[:, 0:TOK], ALU.mult).then_inc(S["xr_ready"], 1)

                normalise(0, 1)
                v.wait_ge(S["ada_done"], 1)
                link(v.tensor_tensor(mod3, PS[3][:, 0, 0:96].rearrange("p (c g) -> p c g", g=2),
                                     par("b_ada", 48).unsqueeze(2).broadcast_to([P, 48, 2]), ALU.add), "mod_ready")
                for norm, g in enumerate(("g1", "g2")):
                    link(v.scalar_tensor_tensor(msc[:, norm], mod3[:, 24 * norm + 8:24 * norm + 16, :], 1.0,
                                                par(g, KC).unsqueeze(2).broadcast_to([P, KC, 2]), ALU.add, ALU.mult),
                         "mod_ready")
                v.wait_ge(S["pads_zero"], 1)
                for c in range(BC):
                    v.wait_ge(S["conv_sig"], 2 * (c + 1))
                    v.wait_ge(S["tile_done"], 2 * c + 2)
                    ps, yp = PS[(2 * c + 1) % 3], ypad[:, c % 2, :]
                    v.tensor_tensor(yp[:, CPAD:CPAD + LAT], ps[:, 0, :], sig2[:, c % 2, 0:LAT], ALU.mult)\
                        .then_inc(S["conv_in"], 1)
                    v.tensor_tensor(yp[:, 2 * CPAD + LAT:2 * CPAD + TOK], ps[:, 1, 0:CTX], sig2[:, c % 2, LAT:TOK],
                                    ALU.mult).then_inc(S["conv_in"], 1)
                    v.wait_ge(S["conv_in"], 2 * (c + 1))
                    cw = par("conv_w", BC * TAPS)[:, c * TAPS:(c + 1) * TAPS]
                    acc = br_conv[:, c, 0:CLEN]
                    link(v.tensor_scalar(acc, yp[:, 0:CLEN], cw[:, 0:1], par("conv_b", BC)[:, c:c + 1], ALU.mult, ALU.add))
                    for tap in range(1, TAPS):
                        link(v.scalar_tensor_tensor(acc, yp[:, tap:tap + CLEN], cw[:, tap:tap + 1], acc, ALU.mult, ALU.add),
                             "dve_step" if tap < TAPS - 1 else "conv_acc")
                v.wait_ge(S["conv_mean"], 1)
                for c in range(BC):
                    for b, t0, t1 in ((0, 0, LAT), (1, CCTX, CLEN)):
                        v.scalar_tensor_tensor(br_conv[:, c, t0:t1], PS[3][:, b, 0:t1 - t0], -1.0 / BW,
                                               br_conv[:, c, t0:t1], ALU.mult, ALU.add).then_inc(S["conv_centred"], 1)
                v.wait_ge(S["h_ready"], 2 * KC)
                link(v.memset(rstd[:, LAT:CCTX], 1.0))
                v.wait_ge(S["conv_var"], 1)
                for b, t0, t1 in ((0, 0, LAT), (1, CCTX, CLEN)):
                    link(v.tensor_scalar(rstd[:, t0:t1], PS[3][:, b, 0:t1 - t0], 1.0 / BW, EPS, ALU.mult, ALU.add),
                         "conv_norm")
                v.wait_ge(S["root_ready"], 2)
                link(v.reciprocal(rstd[:, 0:CLEN], rstd[:, 0:CLEN]))
                v.wait_ge(S["conv_centred"], 2 * BC)
                for c in range(BC):
                    v.tensor_tensor(br_conv[:, c, 0:CLEN], br_conv[:, c, 0:CLEN], rstd[:, 0:CLEN], ALU.mult)\
                        .then_inc(S["conv_norm"], 1)
                for t in range(TT):
                    v.wait_ge(S["zv_ready"], t + 1)
                    link(v.bn_stats(stats6[:, t, :], gv[:, t, :]))
                    link(v.bn_aggr(stats2[:, t, :], stats6[:, t, :]))
                link(v.tensor_scalar(vroot, stats2[:, :, 1], EPS, None, ALU.add), "var_ready")
                v.wait_ge(S["root_ready"], 3)
                link(v.reciprocal(vroot, vroot))
                for t in range(TT):
                    link(v.tensor_scalar(gv[:, t, :], gv[:, t, :], stats2[:, t, 0:1], vroot[:, t:t + 1],
                                         ALU.subtract, ALU.mult))
                    link(v.tensor_tensor(gv[:, t, :], gv[:, t, :], par("sgu_g", BW), ALU.mult))
                    link(v.tensor_tensor(gv[:, t, :], gv[:, t, :], par("sgu_beta", BW), ALU.add), "sgu_norm")

                def rope(n, src, dst, m, name):
                    v.wait_ge(S[name], 2 * (m + 1))
                    v.wait_ge(S["turned"], n + 1)
                    link(v.tensor_tensor(sig[:, 0:LAT], PS[3][:, n % 2, :], sinT, ALU.mult))
                    link(v.tensor_tensor(dst[:, m, :], src[:, m, 0:LAT], cosT, ALU.mult))
                    link(v.tensor_tensor(dst[:, m, :], dst[:, m, :], sig[:, 0:LAT], ALU.add), "roped")

                for m in range(PAIRS):
                    rope(m, qs, q_rot, m, "q_in")
                for g in range(BC):
                    v.wait_ge(S["sgu_mixed"], g + 1)
                    sb_row = par("sgu_b", BW)[:, g * P:(g + 1) * P]
                    v.wait_ge(S["u_ready"], g + 1)
                    link(v.tensor_tensor(sig[:, 0:LAT].rearrange("p (t q) -> p t q", t=4),
                                         PS[3][:, 0, :].rearrange("p (t q) -> p t q", t=4),
                                         sb_row.unsqueeze(1).broadcast_to([P, 4, P]), ALU.add))
                    link(v.tensor_tensor(sig[:, LAT:TOK], PS[3][:, 1, 0:CTX], sb_row, ALU.add))
                    link(v.tensor_tensor(br_sgu[:, g, :], br_sgu[:, g, :], sig[:, 0:TOK], ALU.mult), "sgu_ready")
                for m in range(PAIRS):
                    rope(4 + m, k_rot, k_rot, m, "k_in")
                for t in range(TT):
                    v.wait_ge(S["v_turned"], t + 1)
                    v.tensor_copy(val[:, t, :], PS[3][:, t % 2, :]).then_inc(S["v_tok"], 1)

                units = attention_units()
                v.wait_ge(S["prob_pad"], 1)

                def biased(u):
                    head, cb = units[u]
                    v.wait_ge(S["s_done"], u + 1)
                    ps, pr = PS[0][:, u % 2, :], prob[:, u % 2, :]
                    if u >= 2:
                        v.wait_ge(S["p_turned"], u - 1)
                    if cb is not None:
                        v.wait_ge(S["bias_built"], 3 * (head + 1))
                        var = bias_m[:, head % 2, (0, 1, 1, 2)[cb], :]
                        link(v.tensor_tensor(pr[:, 64:320], ps[:, 0:256], var, ALU.add))
                    link(v.tensor_copy(pr[:, 320:448], ps[:, 256:384]))
                    lo = 320 if cb is None else 64
                    v.tensor_reduce(nmax[:, u % 2:u % 2 + 1], pr[:, lo:448], AX, ALU.max, negate=True)\
                        .then_inc(S["s_ready"], 1)

                def normed(u):
                    lo = 320 if units[u][1] is None else 64
                    v.wait_ge(S["p_exp"], u + 1)
                    link(v.reciprocal(rinv[:, u % 2:u % 2 + 1], rsum[:, u % 2:u % 2 + 1]))
                    v.tensor_scalar(prob[:, u % 2, lo:448], prob[:, u % 2, lo:448], rinv[:, u % 2:u % 2 + 1], None,
                                    ALU.mult).then_inc(S["p_norm"], 1)

                def attended(m):
                    v.wait_ge(S["o_done"], 10 * (m + 1))
                    v.tensor_copy(in_rows(br_att[:, m, 0:LAT]), group_major(PS[2][:, m % 2, :])).then_inc(S["o_ready"], 1)
                    v.tensor_copy(br_att[:, m, LAT:TOK], PS[3][:, m % 2, 0:CTX]).then_inc(S["o_ready"], 1)

                for u in range(len(units) + 1):
                    if u < len(units):
                        biased(u)
                    if u >= 1:
                        normed(u - 1)
                    if u >= 12 and (u - 12) % 10 == 0:
                        attended((u - 12) // 10)
                attended(PAIRS - 1)

                v.wait_ge(kv_stored, l * 32 + 32)
                i = 0
                for o, n in enumerate(GATE_ORDER):
                    for m in range(KC):
                        v.wait_ge(S["gate_sig"], 2 * (i + 1))
                        v.wait_ge(S["br_done"], i + 1)
                        ps, sg = PS[2 * (i % 2) + 1], sig2[:, i % 2, :]
                        dst = merged[:, m, :] if o == 0 else sg
                        if n == 1:
                            link(v.tensor_tensor(dst[:, 0:LAT], ps[:, 0, :], sg[:, 0:LAT], ALU.mult))
                            link(v.tensor_tensor(dst[:, LAT:TOK], ps[:, 1, 0:CTX], sg[:, LAT:TOK], ALU.mult))
                        else:
                            link(v.tensor_tensor(dst.rearrange("p (b t) -> p b t", b=2), ps[:, :, 0:HALF],
                                                 sg.rearrange("p (b t) -> p b t", b=2), ALU.mult),
                                 "dve_step" if o else "br_used")
                        if o:
                            v.tensor_tensor(merged[:, m, :], merged[:, m, :], sg, ALU.add).then_inc(S["br_used"], 1)
                            v.wait_ge(S["br_used"], i + 1)
                        i += 1

                def add_gated(m, ps, gate):
                    for g, (b, t0, t1) in enumerate(((0, 0, LAT), (1, LAT, TOK))):
                        yield v.scalar_tensor_tensor(x[:, m, t0:t1], ps[:, b, 0:t1 - t0], mod3[:, gate + m, g:g + 1],
                                                     x[:, m, t0:t1], ALU.mult, ALU.add)

                for m in range(KC):
                    v.wait_ge(S["out_done"], m + 1)
                    for ins in add_gated(m, PS[m % 2], 16):
                        link(ins, "x_mixed")
                normalise(1, 4)

                v.wait_ge(S["logits"], 1)
                v.wait_ge(S["xr_ready"], 2 * KC)
                lg = PS[3][:, 0, 0:TT * NE].rearrange("p (t e) -> p t e", t=TT)
                link(v.tensor_reduce(rt_max, lg, AX, ALU.max))
                link(v.tensor_tensor(aff, lg, rt_max.unsqueeze(2).broadcast_to([P, TT, NE]), ALU.subtract), "logit_sub")
                v.wait_ge(S["aff_exp"], 1)
                link(v.tensor_reduce(rt_sum, aff, AX, ALU.add))
                link(v.reciprocal(rt_sum, rt_sum))
                link(v.tensor_tensor(aff, aff, rt_sum.unsqueeze(2).broadcast_to([P, TT, NE]), ALU.mult), "aff_ready")
                for t in range(1, TT, 2):
                    v.wait_ge(S["h2_turned"], t + 1)
                    v.tensor_copy(h_tok[:, t, :].rearrange("p (b d) -> p b d", b=2), PS[t % 2][:, :, :])\
                        .then_inc(S["h2_tok_d"], 1)
                v.wait_ge(S["aff_copied"], 2)
                link(v.tensor_copy(affW, affT))
                best = small[0:NE, 72:80]
                for t0, t1, cap in ((0, LAT, CAPL), (LAT, TOK, CAPC)):
                    for _ in range(cap // 8):
                        link(v.max(best, affW[:, t0:t1]))
                        link(v.match_replace(affW[:, t0:t1], best, affW[:, t0:t1], -1.0))
                link(v.tensor_scalar(selT, affW, 0.0, None, ALU.is_lt))
                for t0, t1 in ((0, LAT), (LAT, TOK)):
                    link(v.tensor_tensor_scan(cumT[:, t0:t1], selT[:, t0:t1], selT[:, t0:t1], 0.0, ALU.add, ALU.max))
                link(v.tensor_tensor(slotT, cumT, selT, ALU.mult))
                link(v.tensor_scalar(slotT, slotT, -1.0, None, ALU.add), "slot_ready")
                v.wait_ge(S["slot_turned"], 1)
                link(v.tensor_copy(slot_tok, PS[3][:, 0, 0:TT * NE].rearrange("p (t e) -> p t e", t=TT)))
                iota = con("iota", CAPL)
                for t in range(TT):
                    cap = CAPL if t < 4 else CAPC
                    v.tensor_tensor(pick_l[:, t, :, :] if t < 4 else pick_c[:, :, :],
                                    slot_tok[:, t, :].unsqueeze(2).broadcast_to([P, NE, cap]),
                                    iota[:, 0:cap].unsqueeze(1).broadcast_to([P, NE, cap]), ALU.is_equal)\
                        .then_inc(S["pick_ready"], 1)
                for q in range(EPAIRS):
                    v.wait_ge(S["spread_aff"], 2 * (q + 1))
                    link(v.scalar_tensor_tensor(put_l[:, q, :], PS[0][:, 0, :], con("row64", 1), sq2[:, q % 2, 0:LAT],
                                                ALU.is_equal, ALU.mult), "put_ready")
                    link(v.scalar_tensor_tensor(put_c[0:32, q, :], PS[0][0:32, 1, 0:CTX], con("row16", 1)[0:32],
                                                sq2[0:32, q % 2, LAT:TOK], ALU.is_equal, ALU.mult), "put_ready")
                with v.Fori(0, EPAIRS) as q:
                    for j in range(2):
                        v.wait_ge(S["sil_ready"], q * 2 + j + 1)
                        v.wait_ge(S["b_done"], q * 2 + j + 1)
                        v.tensor_tensor(act.rearrange("p (b k) c -> p b (k c)", b=2), PS[2][:, :, 0:4 * CAP],
                                        sil.rearrange("p (b k) c -> p b (k c)", b=2), ALU.mult).then_inc(S["act_ready"], 1)
                    v.wait_ge(S["t_done"], q * 2 + 2)
                    v.tensor_copy(y_c[0:32, :].rearrange("p (b d) -> p b d", b=2), PS[1][0:32, :, :])\
                        .then_inc(S["yctok_ready"], 1)
                    for k in range(KC):
                        v.wait_ge(S["c_done"], q * 8 + k + 1)
                        first, second = add_gated(k, PS[2 + k % 2], 40)
                        second.then_inc(S["c_used"], 1)
                    v.wait_ge(S["c_used"], q * 8 + 8)
                v.drain().then_inc(layer_done, 1)
                v.wait_ge(layer_go, l + 1)

            v.wait_ge(start_in, 16 * 3)
            with v.Fori(0, LAYERS) as l:
                layer_body(l)
            v.wait_ge(final_sum, 1)
            v.tensor_scalar(rstd[:, 0:TOK].rearrange("p (b t) -> p b t", b=2), PS[0][:, :, 0:HALF],
                            1.0 / D, EPS, ALU.mult, ALU.add).then_inc(final_root, 1)
            v.wait_ge(final_root, 2)
            v.reciprocal(rstd[:, 0:TOK], rstd[:, 0:TOK]).then_inc(final_xr, 1)
            v.wait_ge(final_xr, 1)
            for k in range(KC):
                v.tensor_tensor(h[:, k, :], x[:, k, :], rstd[:, 0:TOK], ALU.mult).then_inc(out_ready, 1)
                v.wait_ge(out_ready, 2 * k + 1)
                v.tensor_scalar(h[:, k, :], h[:, k, :], con("final_g", KC)[:, k:k + 1], None, ALU.mult)\
                    .then_inc(out_ready, 1)

        @block.gpsimd
        def _(g):
            g.wait_ge(start_in, 16 * 3)
            with g.Fori(0, LAYERS) as l:
                link = linker(g, "pool_step")
                link(g.memset(ypad, 0.0))
                g.memset(zp, 0.0).then_inc(S["pads_zero"], 1)
                for c in range(BC):
                    w = 2 << c
                    g.wait_ge(S["pool_in"], 2 * (c + 1))
                    g.wait_ge(S["pads_zero"], 1)
                    src, width = zp[:, c, :], PLEN
                    for d in range(c + 1):
                        dst = (psum_a, psum_b)[d % 2]
                        width -= 1 << d
                        link(g.tensor_tensor(dst[:, 0:width], src[:, 0:width], src[:, 1 << d:(1 << d) + width], ALU.add))
                        src = dst
                    off = PPAD - w // 2
                    edge = con("edge", 64)[:, c * 16:(c + 1) * 16]
                    for t0, n in ((0, LAT), (PCTX - PPAD, CTX)):
                        for e, at in enumerate((off + t0, off + t0 + n - 8)):
                            link(g.tensor_tensor(src[:, at:at + 8], src[:, at:at + 8], edge[:, e * 8:(e + 1) * 8], ALU.mult))
                    n = PLEN - 2 * PPAD
                    link(g.tensor_scalar(src[:, off:off + n], src[:, off:off + n], 1.0 / w, None, ALU.mult))
                    link(g.tensor_tensor(zp[:, c, PPAD:PPAD + n], src[:, off:off + n], zp[:, c, PPAD:PPAD + n],
                                         ALU.subtract), "pool_d")
                g.wait_ge(S["conv_norm"], 2 + BC)
                g.memset(prob[:, :, 0:64], 0.0).then_inc(S["prob_pad"], 1)
                mask = con("mask", 96).rearrange("p (v s) -> p v s", v=3)
                for head in range(HEADS):
                    if head:
                        g.wait_ge(S["bias_built"], 3 * head)
                    g.dma_start(bias_w, a["bias"][l, head]).then_inc(bias_in, 16)
                    g.wait_ge(bias_in, l * (16 * HEADS) + 16 * (head + 1))
                    if head >= 2:
                        g.wait_ge(S["s_ready"], 5 * (head - 1))
                    for var in range(3):
                        at = WIDE // 3 - 8 * var
                        g.tensor_tensor(
                            bias_m[:, head % 2, var, :].rearrange("p (g r j) -> p g r j", g=4, r=ROWS),
                            bias_w[:, :, at:at + 32].rearrange("p r (g j) -> p g r j", g=4),
                            mask[:, var, :].rearrange("p (g j) -> p g j", g=4).unsqueeze(2).broadcast_to([P, 4, ROWS, 8]),
                            ALU.add).then_inc(S["bias_built"], 1)
                g.drain().then_inc(layer_done, 1)
                g.wait_ge(layer_done, l * 4 + 4)
                g.sem_inc(all_idle, 1)
                g.sem_clear(range(cleared[0], cleared[-1] + 1))
                g.sem_inc(layer_go, 1)


def span_start(cb):
    return min(max(cb * COLS - COLS // 2, 0), GRID_W - 2 * COLS)


def attention_units():
    return [(head, cb) for head in range(HEADS) for cb in (0, 1, 2, 3, None)]


def key_chunks(cb):
    if cb is None:
        return [(320, P, 4)]
    if cb in (0, 3):
        first = span_start(cb) // COLS
        return [(64, P, first), (192, P, first + 1), (320, P, "cache")]
    first = (span_start(cb) - 8) // COLS
    return [(0, P, first), (128, P, first + 1), (320, P, "cache"), (256, 64, first + 2)]


def _constants():
    half, nf = HD // 2, HD // 4
    inv = (1.0 / (10000.0 ** (np.arange(nf) / nf))).astype(np.float32)
    tok = np.arange(LAT).reshape(ROWS, 8, 8).transpose(1, 0, 2).reshape(-1)
    out = np.zeros((P, NCON), np.float32)
    cos, sin = np.zeros((HD, LAT), np.float32), np.zeros((HD, LAT), np.float32)
    perm = np.zeros((P, P), np.float32)
    for part, pos in ((0, tok // GRID_W), (1, tok % GRID_W)):
        ang = (pos[:, None].astype(np.float32) * inv[None, :]).astype(np.float32)
        for s in range(2):
            rows = slice(part * half + s * nf, part * half + (s + 1) * nf)
            cos[rows] = np.cos(ang).T
            sin[rows] = np.sin(ang).T * (1 if s else -1)
    for i in range(P):
        perm[i ^ nf, i] = 1
    q = np.arange(P)
    qcol = (q // 64) * 8 + q % 8
    mask = np.zeros((P, 3, 32), np.float32)
    for var, cb in enumerate((0, 1, 3)):
        col = cb * COLS + qcol
        start = np.clip(col - COLS // 2, 0, GRID_W - COLS)
        key = span_start(cb) + np.arange(32)
        ok = (key[None] >= start[:, None]) & (key[None] < start[:, None] + COLS)
        mask[:, var] = np.where(ok, 0.0, NEG)
    edge = np.ones((4, 2, 8), np.float32)
    for g in range(4):
        w = 2 << g
        for t in range(8):
            edge[g, 0, t] = w / (w - max(0, w // 2 - t))
            edge[g, 1, t] = w / (w - max(0, w // 2 - 1 - (7 - t)))
    for name, value in (("cos", np.tile(cos, (2, 1))), ("sin", np.tile(sin, (2, 1))), ("ident", np.eye(P)),
                        ("ones", np.ones((P, P))), ("perm", perm), ("mask", mask.reshape(P, -1)),
                        ("edge", np.broadcast_to(edge.reshape(1, -1), (P, 64))),
                        ("iota", np.broadcast_to(np.arange(CAPL)[None], (P, CAPL))),
                        ("row64", (q % CAPL)[:, None]), ("row16", (q % CAPC)[:, None])):
        out[:, CON[name]:CON[name] + value.shape[1]] = value
    spread = np.zeros((NE, D + 256), np.float32)
    for e in range(NE):
        pair, j = e // 2, e % 2
        spread[e, pair * P + j * CAPL:pair * P + (j + 1) * CAPL] = 1
        spread[e, D + pair * 32 + j * CAPC:D + pair * 32 + (j + 1) * CAPC] = 1
    return out, spread


def _blocks(w, cols=512):
    *lead, k, n = w.shape
    w = w.reshape(*lead, k // P, P, n // cols, cols)
    a = len(lead)
    w = w.transpose(*range(a), a + 2, a + 1, a, a + 3)
    return w.reshape(*lead, n // cols, P, (k // P) * cols)


def _columns(v):
    return np.swapaxes(v.reshape(*v.shape[:-1], -1, P), -1, -2)


def kernel(**inputs):
    import concourse.bacc as bacc
    from concourse.bass_utils import run_bass_kernel_spmd as run

    i = {k: np.asarray(v) for k, v in inputs.items()}
    L = LAYERS
    tokens = np.concatenate([i["x_sample"][0], i["x_prompt"][0]], 0)
    w_in = i["w_in"]
    conv = w_in[:, :, 1536:2560].reshape(L, D, 2, BC, P)[:, :, ::-1].transpose(0, 1, 3, 2, 4).reshape(L, D, 1024)
    parts = [conv, w_in[:, :, 2560:3072], w_in[:, :, 3072:3584], w_in[:, :, 3584:4096], w_in[:, :, 0:1536]]
    blocks = [_blocks(i["w_ada"]), _blocks(np.concatenate(parts, -1))]
    for n in GATE_ORDER:
        gate = _blocks(w_in[:, :, 4096 + n * D:4096 + (n + 1) * D])
        branch = _blocks(i["w_branch"][:, n], D)
        blocks += [gate[:, 0:1], branch, gate[:, 1:2]]
    blocks.append(_blocks(i["w_out"]))
    w_mix = np.concatenate(blocks, 1)
    w_exp = np.concatenate([_blocks(i["w1"]), _blocks(i["w3"]), _blocks(i["w2"])], 2).reshape(L, EPAIRS, 12, P, 4096)

    params = np.zeros((L, P, NPAR), np.float32)
    row = lambda v: np.broadcast_to(v.reshape(L, 1, -1), (L, P, v[0].size))
    for name, value in (
            ("b_ada", _columns(i["b_ada"])), ("g1", _columns(i["norm1_g"])), ("g2", _columns(i["norm2_g"])),
            ("conv_b", _columns(i["conv_b"])), ("conv_g", _columns(i["conv_ln_g"])),
            ("conv_beta", _columns(i["conv_ln_b"])), ("pool_scale", _columns(i["pool_scale"])),
            ("conv_w", i["conv_w"].reshape(L, TAPS, BC, P).transpose(0, 3, 2, 1).reshape(L, P, -1)),
            ("router", i["w_router"].reshape(L, KC, P, NE).transpose(0, 2, 1, 3).reshape(L, P, -1)),
            ("pool_w", i["pool_w"].transpose(0, 2, 1, 3).reshape(L, P, -1)),
            ("sgu_w", i["sgu_w"].transpose(0, 3, 1, 2).reshape(L, P, -1)),
            ("sgu_g", row(i["sgu_ln_g"])), ("sgu_beta", row(i["sgu_ln_b"])), ("sgu_b", row(i["sgu_b"]))):
        params[:, :, PAR[name]:PAR[name] + value.shape[-1]] = value
    consts, spread = _constants()
    consts[:, CON["final_g"]:CON["final_g"] + KC] = _columns(i["final_g"])

    wide = np.zeros((L, HEADS, 15, 31 + 2 * 24), np.float32)
    wide[..., 24:55] = i["rpb"]
    q = np.arange(P)
    qrow, qcol = (q // 8) % 8, (q // 64) * 8 + q % 8
    at_row = np.arange(ROWS)[None, :] - qrow[:, None] + 7
    at_col = np.arange(WIDE)[None, :] - 16 - qcol[:, None] + 15 + 24
    bias = wide[:, :, at_row[:, :, None], at_col[:, None, :]]

    arrays = {
        "x0": tokens.T.reshape(KC, P, TOK).transpose(1, 0, 2).reshape(P, -1),
        "cond": np.stack([i["c"][0], i["c_ctx"]], -1).reshape(KC, P, 2).transpose(1, 0, 2).reshape(P, -1),
        "consts": consts, "spread": spread, "params": params, "bias": bias,
        "w_mix": w_mix, "w_exp": w_exp,
        "ck": i["cache_k"][0].reshape(L, PAIRS, 2, P, HD).transpose(0, 2, 4, 1, 3).reshape(L, P, PAIRS, P),
        "cv": i["cache_v"][0].transpose(0, 2, 1, 3).reshape(L, P, BW),
    }
    arrays = {k: np.ascontiguousarray(v) for k, v in arrays.items()}
    nc = bacc.Bacc("TRN2", target_bir_lowering=False, num_devices=1)
    a = {k: nc.dram_tensor(f"in_{k}", v.shape, F32, kind="ExternalInput").ap() for k, v in arrays.items()}
    for name, shape in (("y", (P, KC, TOK)), ("new_k", (L, P, PAIRS, CTX)), ("new_v", (L, CTX, BW))):
        a[name] = nc.dram_tensor(f"out_{name}", shape, F32, kind="ExternalOutput").ap()
    step_kernel(nc, a)
    r = run(nc, [{f"in_{k}": v for k, v in arrays.items()}], core_ids=[0]).results[0]
    y = r["out_y"].transpose(1, 0, 2).reshape(D, TOK).T
    new_k = r["out_new_k"].reshape(L, 2, HD, PAIRS, CTX).transpose(0, 3, 1, 4, 2).reshape(1, L, HEADS, CTX, HD)
    new_v = r["out_new_v"].reshape(L, CTX, HEADS, HD).transpose(0, 2, 1, 3)[None]
    return (np.ascontiguousarray(y[LAT:][None]), np.ascontiguousarray(y[:LAT][None]),
            np.ascontiguousarray(new_k), np.ascontiguousarray(new_v))
```

```python
from contextlib import ExitStack

import numpy as np

import concourse.bass as bass
from concourse import mybir

F32 = mybir.dt.float32
ALU = mybir.AluOpType
ACT = mybir.ActivationFunctionType
AX = mybir.AxisListType.X

P = 128
LAYERS = 2
D = 1024
KC = D // P
LAT, CTX = 512, 128
TOK = LAT + CTX
HALF = TOK // 2
TT = TOK // P
HEADS, HD = 8, 64
PAIRS = HEADS // 2
GRID_W, ROWS, COLS = 64, LAT // 64, 16
BW = 512
BC = BW // P
TAPS = 31
CPAD = TAPS // 2
CLEN = LAT + CPAD + CTX
CCTX = LAT + CPAD
PPAD = 8
PLEN = PPAD + LAT + PPAD + CTX + PPAD
PCTX = PPAD + LAT + PPAD
NE = 16
CAPL, CAPC = 2 * LAT // NE, 2 * CTX // NE
CAP = CAPL + CAPC
EPAIRS = NE // 2
CROWS = 32
EPS = 1e-6
NEG = -1e30
SLOTS = 3
WIDE = 48

ADA_BLOCKS, ADA_FIRST = 12, 4
PHASES = ("conv0", "conv1", "pool", "u", "v", "q", "k", "val")
IN_BLOCK = {name: ADA_FIRST + 2 * i for i, name in enumerate(PHASES)}


def ada_block(n):
    return n if n < ADA_FIRST else 2 * n - ADA_FIRST + 1


TILES = []
for _i, _name in enumerate(PHASES):
    TILES += [(_name, 0), ("ada", ADA_FIRST + _i)] + [(_name, _m) for _m in range(1, 5 if _name == "v" else 4)]
TILE_AT = {_t: _n for _n, _t in enumerate(TILES)}
GATE_ORDER = (2, 3, 1, 0)
OUT_BLOCK = 32
MIX_BLOCKS = 34
EXP_BLOCKS = 6


def tile_count(phase, m):
    return sum(name != "ada" for name, _ in TILES[:TILE_AT[phase, m] + 1])


def first_in_slot(n):
    return n // SLOTS


def per_layer(s):
    mixer = len(range(s, MIX_BLOCKS, SLOTS))
    return mixer + EXP_BLOCKS * NE // SLOTS


def _layout(parts):
    at, out = 0, {}
    for name, n in parts:
        out[name] = at
        at += n
    return out, at


PAR, NPAR = _layout([("b_ada", 48), ("g1", KC), ("g2", KC), ("conv_b", BC), ("conv_g", BC),
                     ("conv_beta", BC), ("pool_scale", BC), ("conv_w", BC * TAPS), ("router", KC * NE),
                     ("pool_w", BW), ("sgu_w", BW), ("sgu_g", BW), ("sgu_beta", BW), ("sgu_b", BW)])
CON, NCON = _layout([("cos", LAT), ("sin", LAT), ("ident", P), ("ones", P), ("perm", P),
                     ("mask", 3 * 32), ("edge", 4 * 2 * 8), ("iota", CAPL), ("row64", 1), ("row16", 1),
                     ("final_g", KC)])


def group_major(ap):
    return ap.rearrange("p (g r j) -> p r g j", g=8, r=ROWS)


def in_rows(ap):
    return ap.rearrange("p (r g j) -> p r g j", g=8, r=ROWS)


def step_kernel(nc, a):
    with ExitStack() as ctx:
        def sb(name, n):
            return ctx.enter_context(nc.sbuf_tensor(name, [P, n], F32))

        def sem(name):
            return ctx.enter_context(nc.semaphore(name))

        ring = sb("ring", SLOTS * 4096)
        region_x = sb("region_x", KC * TOK)
        hT = sb("hT", KC * TOK)
        region_m = sb("region_m", KC * TOK)
        region_b = sb("region_b", 3 * BC * TOK + BC * 656)
        region_r = sb("region_r", 7168)
        params = sb("params", NPAR)
        consts = sb("consts", NCON)
        sq = sb("sq", 2 * 656)
        sig = sb("sig", 2 * TOK)
        rstd = sb("rstd", 656)
        mod = sb("mod", 96)
        mscale = sb("mscale", 2 * 2 * KC)
        cond = sb("cond", 2 * KC + 30)
        small = sb("small", 112)
        PS = [ctx.enter_context(nc.psum_tensor(f"ps{i}", [P, 2, 512], F32)) for i in range(4)]

        def par(name, n):
            return params[:, PAR[name]:PAR[name] + n]

        def con(name, n):
            return consts[:, CON[name]:CON[name] + n]

        x = region_m[:, :].rearrange("p (k t) -> p k t", k=KC)
        h = hT[:, :].rearrange("p (k t) -> p k t", k=KC)
        ones, ident, perm = con("ones", P), con("ident", P), con("perm", P)
        cosT, sinT = con("cos", LAT), con("sin", LAT)
        mod3 = mod[:, :].rearrange("p (c g) -> p c g", g=2)
        msc = mscale[:, :].rearrange("p (n k g) -> p n k g", n=2, g=2)
        sq2 = sq[:, :].rearrange("p (b t) -> p b t", b=2)
        sig2 = sig[:, :].rearrange("p (b t) -> p b t", b=2)
        br_att = region_b[:, 0:2560].rearrange("p (c t) -> p c t", c=BC)
        br_pool = region_b[:, 2560:5120].rearrange("p (c t) -> p c t", c=BC)
        br_sgu = region_b[:, 5120:7680].rearrange("p (c t) -> p c t", c=BC)
        br_conv = region_b[:, 7680:7680 + BC * 656].rearrange("p (c t) -> p c t", c=BC)
        YP = CPAD + LAT + CPAD + CTX + CPAD
        ypad = region_b[:, 0:2 * YP].rearrange("p (b t) -> p b t", b=2)
        vT = br_att
        ada_row = region_b[:, 1536:2560].rearrange("p (b n) -> p b n", b=2)
        ada_part = small[:, 80:112].rearrange("p (m g c) -> p m g c", m=4, g=4)
        zp = region_r[:, 0:4 * PLEN].rearrange("p (c t) -> p c t", c=BC)
        psum_a = region_r[:, 4 * PLEN:5 * PLEN]
        psum_b = region_r[:, 5 * PLEN:6 * PLEN]
        qs = region_m[:, 0:2560].rearrange("p (c t) -> p c t", c=PAIRS)
        q_rot = region_m[:, 2560:4608].rearrange("p (c t) -> p c t", c=PAIRS)
        kctx = region_m[:, 4608:5120].rearrange("p (c t) -> p c t", c=PAIRS)
        k_rot = region_r[:, 0:2048].rearrange("p (c t) -> p c t", c=PAIRS)
        val = region_r[:, 2048:4608].rearrange("p (t c) -> p t c", t=TT)
        ck = region_r[:, 4608:5120].rearrange("p (c t) -> p c t", c=PAIRS)
        cv = region_r[:, 5120:5632]
        bias_m = region_r[:, 5632:7168].rearrange("p (b v s) -> p b v s", b=2, v=3)
        bias_w = rstd[:, 0:ROWS * WIDE].rearrange("p (r s) -> p r s", r=ROWS)
        prob = sq[:, 0:2 * 448].rearrange("p (b s) -> p b s", b=2)
        prob_t = sig[:, TOK:TOK + 512]
        gate = sig[:, 0:TOK]
        gv = region_x[:, 2560:5120].rearrange("p (t c) -> p t c", t=TT)
        mixed = region_x[:, 1920:2560]
        nmax, rsum, rinv = small[:, 0:2], small[:, 2:4], small[:, 4:6]
        stats6 = small[:, 8:38].rearrange("p (t s) -> p t s", t=TT)
        stats2 = small[:, 38:48].rearrange("p (t s) -> p t s", t=TT)
        vroot = small[:, 48:53]
        merged = region_x[:, :].rearrange("p (k t) -> p k t", k=KC)
        h_tok = region_x[:, :].rearrange("p (t d) -> p t d", t=TT)
        pick_l = region_b[:, 0:4096].rearrange("p (t e c) -> p t e c", t=4, e=NE)
        pick_c = region_b[:, 4096:4352].rearrange("p (e c) -> p e c", e=NE)
        put_l = region_b[:, 4352:8448].rearrange("p (q t) -> p q t", q=EPAIRS)
        put_c = region_b[:, 8448:9472].rearrange("p (q t) -> p q t", q=EPAIRS)
        xs = region_r[:, 0:2 * KC * CAP].rearrange("p (b k c) -> p b k c", b=2, k=KC)
        xs_ctx = region_r[:, 2560:4608].rearrange("p (k s) -> p k s", k=KC)
        act = region_r[0:CAP, 4608:5632].rearrange("p (h f) -> p h f", h=2)
        y_l = region_r[:, 5632:6656]
        spread = region_r[:, 5632:7168]
        y_c = sq[0:2 * CROWS, 0:D]
        act_t = sig[:, 0:KC * CAP].rearrange("p (k c) -> p k c", k=KC)
        affT = region_r[0:NE, 0:640]
        affW = region_r[0:NE, 640:1280]
        selT = region_r[0:NE, 1280:1920]
        cumT = region_r[0:NE, 1920:2560]
        slotT = sig[0:NE, 0:TOK]
        aff = rstd[:, 0:80].rearrange("p (t e) -> p t e", t=TT)
        slot_tok = rstd[:, 80:160].rearrange("p (t e) -> p t e", t=TT)
        rt_max, rt_sum = small[:, 56:61], small[:, 61:66]

        slot_loaded = [sem(f"slot_loaded{i}") for i in range(SLOTS)]
        slot_used = [sem(f"slot_used{i}") for i in range(SLOTS)]
        start_in, cond_ready = sem("start_in"), sem("cond_ready")
        layer_done, all_idle, layer_go = sem("layer_done"), sem("all_idle"), sem("layer_go")
        stored, kv_stored, bias_in = sem("stored"), sem("kv_stored"), sem("bias_in")
        out_ready, final_sq, final_sum, final_root, final_xr = (
            sem(n) for n in ("out_ready", "final_sq", "final_sum", "final_root", "final_xr"))
        names = """x_stored x_back params_in cache_in spread_in dve_step pool_step
            squared square_used norm_sum var_ready root_ready xr_ready h_ready ada_rows ada_row_in ada_turned ada_part_in ada_half mod_sum mod_ready
            tile_done conv_sig conv_in pool_in u_ready zv_ready q_in k_in v_in
            pads_zero conv_acc conv_mean conv_centred conv_var conv_norm conv_ready
            pool_d poolw_done pool_ready sgu_norm sgu_mixed sgu_ready turned roped
            v_turned v_tok prob_pad bias_built bias_read
            s_done s_ready p_exp p_norm p_turned pt_ready o_done o_ready
            gate_done gate_sig br_done br_used out_done x_mixed
            logits logit_sub aff_exp aff_ready aff_turned aff_copied slot_ready slot_turned slot_copied spread_done
            spread_aff put_ready h2_turned h2_tok_a h2_tok_d pick_ready
            ctx_gathered ctx_xs ctx_rows_zero gathered xs_ready xs_ctx_ready a_done b_done sil_ready act_ready
            act_turned act_t_ready y_done y_ready c_done c_used""".split()
        S = {n: sem(n) for n in names}
        cleared = [S[n].num for n in names]
        assert cleared == list(range(cleared[0], cleared[0] + len(cleared)))

        block = ctx.enter_context(nc.Block())

        def linker(eng, own):
            n = {}

            def link(ins, name=own):
                n[name] = n.get(name, 0) + 1
                ins.then_inc(S[name], 1)
                eng.wait_ge(S[name], n[name])
            return link

        @block.sync
        def _(sp):
            def load(slot, before, src):
                sp.wait_ge(slot_used[slot], before + 1)
                sp.dma_start(ring[:, slot * 4096:(slot + 1) * 4096], src).then_inc(slot_loaded[slot], 16)

            sp.dma_start(region_m[:, :], a["x0"]).then_inc(start_in, 16)
            sp.dma_start(consts[:, :], a["consts"]).then_inc(start_in, 16)
            for slot in range(SLOTS):
                sp.sem_inc(slot_used[slot], 1)
            with sp.Fori(0, LAYERS) as l:
                for n in range(MIX_BLOCKS):
                    s = n % SLOTS
                    load(s, l * per_layer(s) + first_in_slot(n), a["w_mix"][l, n])
                with sp.Fori(0, EPAIRS) as q:
                    for b in range(2 * EXP_BLOCKS):
                        s = (MIX_BLOCKS + b) % SLOTS
                        load(s, l * per_layer(s) + q * (2 * EXP_BLOCKS // SLOTS)
                             + first_in_slot(MIX_BLOCKS + b),
                             a["w_exp"][l, q, b])
            for k in range(KC):
                sp.wait_ge(out_ready, 2 * (k + 1))
                sp.dma_start(a["y"][:, k, :], h[:, k, :]).then_inc(stored, 16)
            sp.wait_ge(stored, 16 * KC)
            sp.wait_ge(kv_stored, 2 * 16 * LAYERS)

        @block.tensor
        def _(pe):
            pending = []

            def mm(*args, **kw):
                ins = pe.matmul(*args, **kw)
                if pending:
                    ins.then_inc(slot_used[pending.pop(0)], 1)
                return ins

            def weights(l, n, more=0):
                s = n % SLOTS
                pe.wait_ge(slot_loaded[s], (l * per_layer(s) + more) * 16 + 16 * (first_in_slot(n) + 1))
                return ring[:, s * 4096:(s + 1) * 4096].rearrange("p (k n) -> p k n", k=KC)

            def read(n):
                pending.append(n % SLOTS)

            def evacuated(name, m):
                if name == "ada":
                    return "ada_part_in", m + 1
                if name in ("conv0", "conv1"):
                    c = 2 * int(name[-1]) + m // 2
                    return ("conv_in" if m % 2 else "conv_sig"), 2 * (c + 1)
                signal, each = {"pool": ("pool_in", 2), "u": ("u_ready", 1), "v": ("zv_ready", 1), "q": ("q_in", 2),
                                "k": ("k_in", 2), "val": ("v_in", 2)}[name]
                return signal, each * (m + 1)

            tile = [0]

            def tile_slot():
                n = tile[0]
                tile[0] += 1
                if n >= 3:
                    name, v = evacuated(*TILES[n - 3])
                    pe.wait_ge(S[name], v)
                return PS[n % 3]

            def columns(split):
                return ((0, 0, HALF), (1, HALF, TOK)) if split == "half" else ((0, 0, LAT), (1, LAT, TOK))

            def project(w, m, split):
                ps = tile_slot()
                for k in range(KC):
                    if tile[0] == 1:
                        pe.wait_ge(S["h_ready"], 2 * (k + 1))
                    for b, t0, t1 in columns(split):
                        args = dict(start=k == 0, stop=k == KC - 1)
                        at = (ps[:, b, 0:t1 - t0], w[:, k, m * P:(m + 1) * P], h[:, k, t0:t1])
                        last = (pe.matmul if (k, b) == (KC - 1, 1) else mm)(*at, **args)
                last.then_inc(S["tile_done"], 1)

            def norm_sum(ps, base, signal):
                for k in range(KC):
                    pe.wait_ge(S["squared"], base + k + 1)
                    for b, t0, t1 in columns("half"):
                        last = pe.matmul(ps[:, b, 0:HALF], ones, sq2[:, k % 2, t0:t1], start=k == 0, stop=k == KC - 1)
                    last.then_inc(S["square_used" if k < KC - 1 else signal], 1)

            pe.wait_ge(start_in, 16 * 3)
            pe.wait_ge(cond_ready, 1)
            with pe.Fori(0, LAYERS) as l:
                tile[0] = 0

                def ada_rows(n, ps):
                    w = weights(l, ada_block(n))
                    if n >= 2:
                        pe.wait_ge(S["ada_part_in"], n - 1)
                    for k in range(KC):
                        g = k % 4
                        last = (pe.matmul if k == KC - 1 else mm)(
                            ps[32 * g:32 * (g + 1), 0, :], cond[:, 2 * k:2 * k + 32], w[:, k, :], start=k < 4,
                            stop=k >= 4, tile_position=(0, 32 * g))
                    last.then_inc(S["ada_rows"], 1)
                    read(ada_block(n))

                def ada_turn(n, ps):
                    pe.wait_ge(S["ada_row_in"], n + 1)
                    for m in range(4):
                        last = pe.transpose(ps[:, 1, m * P:(m + 1) * P], ada_row[:, n % 2, m * P:(m + 1) * P], ident)
                    last.then_inc(S["ada_turned"], 1)

                def ada_tile(phase):
                    n = ADA_FIRST + PHASES.index(phase)
                    ada_rows(n, tile_slot())

                def ada_tile_turn(phase):
                    n = ADA_FIRST + PHASES.index(phase)
                    ada_turn(n, PS[TILE_AT["ada", n] % 3])

                ada_rows(0, PS[0])
                ada_rows(1, PS[1])
                ada_turn(0, PS[0])
                ada_rows(2, PS[0])
                ada_turn(1, PS[1])
                ada_turn(2, PS[0])
                norm_sum(PS[2], 0, "norm_sum")
                ada_rows(3, PS[1])
                ada_turn(3, PS[1])
                pe.wait_ge(S["ada_part_in"], 4)
                for phase, split in (("conv0", "group"), ("conv1", "group"), ("pool", "group"), ("u", "half")):
                    w = weights(l, IN_BLOCK[phase])
                    for m in range(4):
                        project(w, m, split)
                        if m == 0:
                            ada_tile(phase)
                        if m == 1:
                            ada_tile_turn(phase)
                    read(IN_BLOCK[phase])

                def over_channels(source, ready, done):
                    pe.wait_ge(*ready)
                    for c in range(BC):
                        if source is sq2:
                            pe.wait_ge(S["squared"], KC + 2 * (c + 1))
                        for b, t0, t1 in ((0, 0, LAT), (1, CCTX, CLEN)):
                            src = source[:, c % 2, t0:t1] if source is sq2 else source[:, c, t0:t1]
                            last = (pe.matmul if b else mm)(PS[3][:, b, 0:t1 - t0], ones, src,
                                                            start=c == 0, stop=c == BC - 1)
                        if source is sq2 and c < BC - 1:
                            last.then_inc(S["square_used"], 1)
                    last.then_inc(S[done], 1)

                w = weights(l, IN_BLOCK["v"])
                for t in range(TT):
                    ps = tile_slot()
                    for k in range(KC):
                        last = (pe.matmul if k == KC - 1 else mm)(
                            ps[:, 0, :], h[:, k, t * P:(t + 1) * P], w[:, k, :], start=k == 0, stop=k == KC - 1)
                    last.then_inc(S["tile_done"], 1)
                    if t == 0:
                        ada_tile("v")
                    if t == 1:
                        ada_tile_turn("v")
                    if t == 2:
                        over_channels(br_conv, (S["conv_acc"], BC), "conv_mean")
                read(IN_BLOCK["v"])
                over_channels(sq2, (S["conv_centred"], 8), "conv_var")

                def pool_product(g):
                    pe.wait_ge(S["pool_d"], g + 1)
                    if g:
                        pe.wait_ge(S["pool_ready"], 2 * g)
                    else:
                        pe.wait_ge(S["conv_norm"], 2)
                    pw = par("pool_w", BW)[:, g * P:(g + 1) * P]
                    pe.matmul(PS[3][:, 0, :], pw, zp[:, g, PPAD:PPAD + LAT], start=True, stop=True)
                    pe.matmul(PS[3][:, 1, 0:CTX], pw, zp[:, g, PCTX:PCTX + CTX], start=True,
                              stop=True).then_inc(S["poolw_done"], 1)

                def turn(name, src, m, n):
                    pe.wait_ge(S[name], 2 * (m + 1))
                    if n >= 2:
                        pe.wait_ge(S["roped"], n - 1)
                    else:
                        pe.wait_ge(S["pool_ready"], 2 * BC)
                    pe.matmul(PS[3][:, n % 2, :], perm, src[:, m, 0:LAT], start=True,
                              stop=True).then_inc(S["turned"], 1)

                def turn_values():
                    pe.wait_ge(S["v_in"], 2 * PAIRS)
                    for t in range(TT):
                        if t < 2:
                            pe.wait_ge(S["roped"], 8)
                        else:
                            pe.wait_ge(S["v_tok"], t - 1)
                        for m in range(PAIRS):
                            last = pe.transpose(PS[3][:, t % 2, m * P:(m + 1) * P], vT[:, m, t * P:(t + 1) * P], ident)
                        last.then_inc(S["v_turned"], 1)

                def mix_tokens(g):
                    if g == 0:
                        pe.wait_ge(S["v_tok"], TT)
                        pe.wait_ge(S["sgu_norm"], TT)
                    else:
                        pe.wait_ge(S["sgu_ready"], g)
                    for t in range(TT):
                        last = pe.matmul(PS[3][:, t // 4, (t % 4) * P:(t % 4 + 1) * P],
                                         gv[:, t, g * P:(g + 1) * P], par("sgu_w", BW)[:, g * P:(g + 1) * P],
                                         start=True, stop=True)
                    last.then_inc(S["sgu_mixed"], 1)

                for phase in ("q", "k", "val"):
                    w = weights(l, IN_BLOCK[phase])
                    for m in range(PAIRS):
                        project(w, m, "group")
                        if m == 0:
                            ada_tile(phase)
                        if m == 1:
                            ada_tile_turn(phase)
                        if phase == "q":
                            pool_product(m)
                        elif phase == "k":
                            turn("q_in", qs, m, m)
                        else:
                            turn("k_in", k_rot, m, 4 + m)
                    read(IN_BLOCK[phase])

                units = attention_units()

                def scores(u):
                    head, cb = units[u]
                    hb, m = (head % 2) * HD, head // 2
                    if u:
                        pe.wait_ge(S["s_ready"], u)
                    else:
                        pe.wait_ge(S["cache_in"], 32)
                    ps = PS[2][:, 0, :]
                    if cb is None:
                        pe.matmul(ps[:, 256:384], qs[hb:hb + HD, m, LAT:TOK], kctx[hb:hb + HD, m, :],
                                  start=True, stop=True).then_inc(S["s_done"], 1)
                        return
                    s0 = span_start(cb) * ROWS
                    pe.matmul(ps[:, 0:256], q_rot[hb:hb + HD, m, cb * P:(cb + 1) * P],
                              k_rot[hb:hb + HD, m, s0:s0 + 256], start=True, stop=True)
                    pe.matmul(ps[:, 256:384], qs[hb:hb + HD, m, cb * P:(cb + 1) * P], ck[hb:hb + HD, m, :],
                              start=True, stop=True).then_inc(S["s_done"], 1)

                def turn_probs(u):
                    pe.wait_ge(S["p_norm"], u + 1)
                    if u:
                        pe.wait_ge(S["pt_ready"], u)
                    for i, (c0, _, _) in enumerate(key_chunks(units[u][1])):
                        last = pe.transpose(PS[2][:, 1, i * P:(i + 1) * P], prob[:, u % 2, c0:c0 + P], ident)
                    last.then_inc(S["p_turned"], 1)

                def weigh_values(u):
                    head, cb = units[u]
                    hb, m = (head % 2) * HD, head // 2
                    pe.wait_ge(S["pt_ready"], u + 1)
                    if u == 0:
                        pe.wait_ge(S["sgu_ready"], BC)
                    elif hb == 0 and cb == 0:
                        pe.wait_ge(S["o_ready"], 2 * m)
                    chunks = key_chunks(cb)
                    out = PS[3][hb:hb + HD, 1, 0:P] if cb is None else \
                        PS[3][hb:hb + HD, 0, cb * P:(cb + 1) * P]
                    for i, (_, n, src) in enumerate(chunks):
                        v = val[0:n, src, head * HD:(head + 1) * HD] if src != "cache" else \
                            cv[:, head * HD:(head + 1) * HD]
                        last = pe.matmul(out, v, prob_t[0:n, i * P:(i + 1) * P], start=i == 0,
                                         stop=i == len(chunks) - 1)
                    last.then_inc(S["o_done"], 1)

                def between(slot):
                    if slot == 0:
                        turn_values()
                    elif slot <= BC:
                        mix_tokens(slot - 1)
                    else:
                        u = slot - ATT_SLOT
                        if u < len(units):
                            scores(u)
                        if 2 <= u < len(units) + 2:
                            weigh_values(u - 2)
                        if 1 <= u < len(units) + 1:
                            turn_probs(u - 1)

                i = 0
                for o, n in enumerate(GATE_ORDER):
                    base = 20 + 3 * o
                    split = "group" if n == 1 else "half"
                    src = {0: br_att, 1: br_conv, 2: br_pool, 3: br_sgu}[n]
                    pe.wait_ge(*{0: (S["o_ready"], 2 * PAIRS), 1: (S["conv_ready"], BC),
                                 2: (S["pool_ready"], 2 * BC), 3: (S["sgu_ready"], BC)}[n])
                    for m in range(KC):
                        if m % 4 == 0:
                            wg = weights(l, base + (2 if m else 0))
                        if i:
                            pe.wait_ge(S["gate_sig"], 2 * i)
                        else:
                            pe.wait_ge(S["v_in"], 2 * PAIRS - 2)
                        for k in range(KC):
                            for b, t0, t1 in columns(split):
                                last = (pe.matmul if (k, b) == (KC - 1, 1) else mm)(
                                    PS[0][:, b, 0:t1 - t0], wg[:, k, (m % 4) * P:(m % 4 + 1) * P],
                                    h[:, k, t0:t1], start=k == 0, stop=k == KC - 1)
                        last.then_inc(S["gate_done"], 1)
                        if n:
                            between(2 * i)
                        if m == 0:
                            weights(l, base + 1)
                            s = (base + 1) % SLOTS
                            wb = ring[:, s * 4096:(s + 1) * 4096].rearrange("p (k n) -> p k n", k=BC)
                        if i:
                            pe.wait_ge(S["br_used"], i)
                        else:
                            pe.wait_ge(S["v_in"], 2 * PAIRS)
                        for k in range(BC):
                            for b, t0, t1 in columns(split):
                                rhs = src[:, k, CCTX:CLEN] if n == 1 and b else src[:, k, t0:t1]
                                last = (pe.matmul if (k, b) == (BC - 1, 1) else mm)(
                                    PS[1][:, b, 0:t1 - t0], wb[:, k, m * P:(m + 1) * P],
                                    rhs, start=k == 0, stop=k == BC - 1)
                        last.then_inc(S["br_done"], 1)
                        if n:
                            between(2 * i + 1)
                        i += 1
                        if m == 3:
                            read(base)
                    read(base + 1)
                    read(base + 2)
                pe.wait_ge(S["br_used"], i)
                for m in range(KC):
                    w = weights(l, OUT_BLOCK + m // 4)
                    if m >= 2:
                        pe.wait_ge(S["x_mixed"], 2 * (m - 1))
                    for k in range(KC):
                        for b, t0, t1 in columns("group"):
                            last = (pe.matmul if (k, b) == (KC - 1, 1) else mm)(
                                PS[m % 2][:, b, 0:t1 - t0], w[:, k, (m % 4) * P:(m % 4 + 1) * P],
                                merged[:, k, t0:t1], start=k == 0, stop=k == KC - 1)
                    last.then_inc(S["out_done"], 1)
                    if m % 4 == 3:
                        read(OUT_BLOCK + m // 4)
                norm_sum(PS[2], KC + 2 * BC, "norm_sum")

                for t in range(TT):
                    for k in range(KC):
                        pe.wait_ge(S["h_ready"], 2 * (KC + k + 1))
                        last = (mm if k < KC - 1 else pe.matmul)(
                            PS[3][:, 0, t * NE:(t + 1) * NE], h[:, k, t * P:(t + 1) * P],
                            par("router", KC * NE)[:, k * NE:(k + 1) * NE], start=k == 0, stop=k == KC - 1)
                last.then_inc(S["logits"], 1)
                for t in range(TT):
                    if t >= 2:
                        name = "h2_tok_a" if t % 2 == 0 else "h2_tok_d"
                        pe.wait_ge(S[name], t // 2)
                    for k in range(KC):
                        last = pe.transpose(PS[t % 2][:, k // 4, (k % 4) * P:(k % 4 + 1) * P],
                                            h[:, k, t * P:(t + 1) * P], ident)
                    last.then_inc(S["h2_turned"], 1)
                pe.wait_ge(S["aff_ready"], 1)
                for t in range(TT):
                    last = pe.transpose(PS[2][0:NE, t // 4, (t % 4) * P:(t % 4 + 1) * P], aff[:, t, :], ident)
                last.then_inc(S["aff_turned"], 1)
                pe.wait_ge(S["slot_ready"], 1)
                for t in range(TT):
                    last = pe.transpose(PS[3][:, 0, t * NE:(t + 1) * NE], slotT[:, t * P:(t + 1) * P],
                                        ident[0:NE, 0:NE])
                last.then_inc(S["slot_turned"], 1)
                pe.wait_ge(S["spread_in"], 16)
                pe.wait_ge(S["h2_tok_a"], 3)
                pe.wait_ge(S["h2_tok_d"], 2)
                for q in range(EPAIRS):
                    if q:
                        pe.wait_ge(S["put_ready"], 2 * q)
                    el = spread[0:NE, q * P:(q + 1) * P]
                    ec = spread[0:NE, D + q * 2 * CROWS:D + (q + 1) * 2 * CROWS]
                    pe.matmul(PS[0][:, 0, :], el, slotT[:, 0:LAT], start=True, stop=True)
                    pe.matmul(PS[0][0:2 * CROWS, 1, 0:CTX], ec, slotT[:, LAT:TOK], start=True, stop=True)
                    pe.matmul(PS[1][:, 0, :], el, affT[:, 0:LAT], start=True, stop=True)
                    pe.matmul(PS[1][0:2 * CROWS, 1, 0:CTX], ec, affT[:, LAT:TOK], start=True,
                              stop=True).then_inc(S["spread_done"], 1)
                pe.wait_ge(S["put_ready"], 2 * EPAIRS)
                pe.wait_ge(S["pick_ready"], TT)

                for k in range(KC):
                    last = pe.matmul(PS[k // 4][:, (k // 2) % 2, (k % 2) * 256:(k % 2 + 1) * 256],
                                     h_tok[:, 4, k * P:(k + 1) * P], pick_c.rearrange("p e c -> p (e c)"),
                                     start=True, stop=True)
                last.then_inc(S["ctx_gathered"], 1)
                pe.wait_ge(S["ctx_xs"], 2)

                def gather(q):
                    for k in range(KC):
                        for t in range(4):
                            last = pe.matmul(PS[0][:, k // 4, (k % 4) * P:(k % 4 + 1) * P],
                                             h_tok[:, t, k * P:(k + 1) * P],
                                             pick_l[:, t, :, :].rearrange("p e c -> p (e c)")[:, bass.ds(q * P, P)],
                                             start=t == 0, stop=t == 3)
                            if pending:
                                last.then_inc(slot_used[pending.pop(0)], 1)
                    last.then_inc(S["gathered"], 1)

                def expert_pair(q, final):
                    for j in range(2):
                        first = MIX_BLOCKS + EXP_BLOCKS * j
                        done = q * 4 + 2 * j

                        def product(n, ps, lhs, ks, signal):
                            w = weights(l, first + n, q * (2 * EXP_BLOCKS // SLOTS))
                            for k in ks:
                                last = (pe.matmul if k == KC - 1 else mm)(
                                    ps, lhs[:, k, :], w[:, k, :], start=k == 0, stop=k == KC - 1)
                            if ks[-1] == KC - 1:
                                last.then_inc(S[signal], 1)
                                read(first + n)

                        def turn_act(half):
                            pe.wait_ge(S["act_ready"], done + half + 1)
                            for k in range(4):
                                last = pe.transpose(PS[3][:, 0, k * CAP:(k + 1) * CAP],
                                                    act[:, half, k * P:(k + 1) * P], ident[0:CAP, 0:CAP])
                            last.then_inc(S["act_turned"], 1)

                        every, low, high = range(KC), range(4), range(4, KC)
                        pe.wait_ge(S["xs_ready"], q * 2 + 2)
                        pe.wait_ge(S["xs_ctx_ready"], q * 2 + 2)
                        product(0, PS[0][0:CAP, 0, :], xs[:, j], every, "a_done")
                        if j == 0:
                            pe.wait_ge(S["c_used"], q * KC + 1)
                        product(1, PS[1][0:CAP, 0, :], xs[:, j], every, "b_done")
                        product(2, PS[0][0:CAP, 1, :], xs[:, j], every, "a_done")
                        turn_act(0)
                        product(3, PS[1][0:CAP, 1, :], xs[:, j], every, "b_done")
                        if j:
                            if not final:
                                pe.wait_ge(S["sil_ready"], done + 2)
                                gather(q + 1)
                            pe.wait_ge(S["y_ready"], q * 8 + 4)
                        pe.wait_ge(S["act_t_ready"], done + 1)
                        if j:
                            turn_act(1)
                            product(4, PS[2][0:CAP, 0, :], act_t, low, "y_done")
                            pe.wait_ge(S["act_t_ready"], done + 2)
                            product(4, PS[2][0:CAP, 0, :], act_t, high, "y_done")
                            product(5, PS[2][0:CAP, 1, :], act_t, every, "y_done")
                        else:
                            product(4, PS[2][0:CAP, 0, :], act_t, low, "y_done")
                            turn_act(1)
                            product(5, PS[2][0:CAP, 1, :], act_t, low, "y_done")
                            pe.wait_ge(S["act_t_ready"], done + 2)
                            product(4, PS[2][0:CAP, 0, :], act_t, high, "y_done")
                            product(5, PS[2][0:CAP, 1, :], act_t, high, "y_done")
                    for k in range(KC):
                        if k % 4 == 0:
                            pe.wait_ge(S["y_ready"], q * 8 + 6 + 2 * (k // 4))
                        if k >= 2:
                            pe.wait_ge(S["c_used"], q * KC + k)
                        mm(PS[1][:, k % 2, :], y_l[:, k * P:(k + 1) * P], put_l[:, q, :], start=True, stop=True)
                        pe.matmul(PS[3][:, k % 2, 0:CTX], y_c[:, k * P:(k + 1) * P], put_c[0:2 * CROWS, q, :],
                                  start=True, stop=True).then_inc(S["c_done"], 1)

                gather(0)
                with pe.Fori(0, EPAIRS - 1) as q:
                    expert_pair(q, False)
                expert_pair(EPAIRS - 1, True)
                assert not pending
                pe.drain().then_inc(layer_done, 1)
                pe.wait_ge(layer_go, l + 1)
            for k in range(KC):
                pe.wait_ge(final_sq, k + 1)
                for b, t0, t1 in columns("half"):
                    last = pe.matmul(PS[0][:, b, 0:HALF], ones, h[:, k, t0:t1], start=k == 0, stop=k == KC - 1)
            last.then_inc(final_sum, 1)

        @block.scalar
        def _(sc):
            sc.dma_start(cond[:, :], a["cond"]).then_inc(start_in, 16)
            sc.wait_ge(start_in, 16 * 3)
            sc.activation(cond[:, :], cond[:, :], ACT.Silu).then_inc(cond_ready, 1)

            def squares(base, ks):
                for k in ks:
                    if k >= 2:
                        sc.wait_ge(S["square_used"], base + k - 1)
                    sc.activation(sq2[:, k % 2, 0:TOK], x[:, k, :], ACT.Square).then_inc(S["squared"], 1)

            def root(name, n, ap):
                sc.wait_ge(S[name], n)
                sc.activation(ap, ap, ACT.Sqrt).then_inc(S["root_ready"], 1)

            def modulate(norm):
                sc.wait_ge(S["mod_ready"], 2 if norm else 1)
                for k in range(KC):
                    sc.wait_ge(S["xr_ready"], KC * norm + k + 1)
                    for g, (t0, t1) in enumerate(((0, LAT), (LAT, TOK))):
                        sc.activation(h[:, k, t0:t1], h[:, k, t0:t1], ACT.Identity,
                                      scale=msc[:, norm, k, g:g + 1],
                                      bias=mod3[:, 24 * norm + k, g:g + 1]).then_inc(S["h_ready"], 1)

            def tile_of(phase, m):
                sc.wait_ge(S["tile_done"], tile_count(phase, m))
                return PS[TILE_AT[phase, m] % 3]

            def ada_rows_in(n, ps):
                sc.wait_ge(S["ada_rows"], n + 1)
                sc.activation(ada_row[:, n % 2, :], ps[:, 0, :], ACT.Copy).then_inc(S["ada_row_in"], 1)

            def ada_parts_in(n, ps):
                sc.wait_ge(S["ada_turned"], n + 1)
                if n:
                    sc.wait_ge(S["mod_sum"], n)
                sc.activation(ada_part, ps[:, 1, :].rearrange("p (m g c) -> p m g c", m=4, g=4)[:, :, :, 0:2],
                              ACT.Copy).then_inc(S["ada_part_in"], 1)

            def ada_between(phase, m):
                n = ADA_FIRST + PHASES.index(phase)
                if m < 2:
                    (ada_rows_in, ada_parts_in)[m](n, PS[TILE_AT["ada", n] % 3])

            with sc.Fori(0, LAYERS) as l:
                sc.dma_start(params[:, :], a["params"][l]).then_inc(S["params_in"], 16)
                sc.dma_start(a["x_store"], region_m[:, :]).then_inc(S["x_stored"], 16)
                squares(0, range(2))
                ada_rows_in(0, PS[0])
                ada_rows_in(1, PS[1])
                ada_parts_in(0, PS[0])
                ada_rows_in(2, PS[0])
                ada_parts_in(1, PS[1])
                ada_parts_in(2, PS[0])
                squares(0, range(2, KC))
                ada_rows_in(3, PS[1])
                ada_parts_in(3, PS[1])
                root("var_ready", 1, rstd[:, 0:TOK])
                modulate(0)
                sc.wait_ge(S["params_in"], 16)
                for c in range(BC):
                    ps = tile_of(f"conv{c // 2}", 2 * (c % 2))
                    if c >= 2:
                        sc.wait_ge(S["conv_in"], 2 * (c - 1))
                    for b, t0, t1 in ((0, 0, LAT), (1, LAT, TOK)):
                        sc.activation(sig2[:, c % 2, t0:t1], ps[:, b, 0:t1 - t0], ACT.Sigmoid).then_inc(S["conv_sig"], 1)
                    if c % 2 == 0:
                        ada_between(f"conv{c // 2}", 0)
                        ada_between(f"conv{c // 2}", 1)
                sc.wait_ge(S["pads_zero"], 1)
                for g in range(BC):
                    ps = tile_of("pool", g)
                    sc.activation(zp[:, g, PPAD:PPAD + LAT], ps[:, 0, :], ACT.Copy).then_inc(S["pool_in"], 1)
                    sc.activation(zp[:, g, PCTX:PCTX + CTX], ps[:, 1, 0:CTX], ACT.Copy).then_inc(S["pool_in"], 1)
                    ada_between("pool", g)
                for g in range(BC):
                    ps = tile_of("u", g)
                    sc.activation(br_sgu[:, g, :].rearrange("p (b t) -> p b t", b=2), ps[:, :, 0:HALF],
                                  ACT.Gelu_apprx_tanh).then_inc(S["u_ready"], 1)
                    ada_between("u", g)
                sc.dma_start(ck, a["ck"][l]).then_inc(S["cache_in"], 16)
                sc.dma_start(cv, a["cv"][l]).then_inc(S["cache_in"], 16)

                def conv_squares(c):
                    sc.wait_ge(S["conv_centred"], 2 * (c + 1))
                    if c >= 2:
                        sc.wait_ge(S["square_used"], KC - 1 + c - 1)
                    for t0, t1 in ((0, LAT), (CCTX, CLEN)):
                        sc.activation(sq2[:, c % 2, t0:t1], br_conv[:, c, t0:t1],
                                      ACT.Square).then_inc(S["squared"], 1)

                for t in range(TT):
                    ps = tile_of("v", t)
                    sc.activation(gv[:, t, :], ps[:, 0, :], ACT.Gelu_apprx_tanh).then_inc(S["zv_ready"], 1)
                    ada_between("v", t)
                    if t == 3:
                        conv_squares(0)
                        conv_squares(1)
                conv_squares(2)
                conv_squares(3)
                root("conv_norm", 2, rstd[:, 0:CLEN])

                def pool_out(g):
                    sc.wait_ge(S["poolw_done"], g + 1)
                    for b, t0, t1 in ((0, 0, LAT), (1, LAT, TOK)):
                        sc.activation(br_pool[:, g, t0:t1], PS[3][:, b, 0:t1 - t0], ACT.Copy,
                                      scale=par("pool_scale", BC)[:, g:g + 1]).then_inc(S["pool_ready"], 1)

                def by_group(phase, m, dst, ctx_dst, scale, name):
                    ps = tile_of(phase, m)
                    sc.activation(group_major(dst), in_rows(ps[:, 0, :]), ACT.Copy, scale=scale).then_inc(S[name], 1)
                    sc.activation(ctx_dst, ps[:, 1, 0:CTX], ACT.Copy, scale=scale).then_inc(S[name], 1)
                    ada_between(phase, m)

                sc.wait_ge(S["x_stored"], 16)
                for m in range(PAIRS):
                    by_group("q", m, qs[:, m, 0:LAT], qs[:, m, LAT:TOK], HD ** -0.5, "q_in")
                    if m == 1:
                        root("var_ready", 2, vroot)
                        for c in range(BC):
                            sc.wait_ge(S["conv_norm"], 2 + c + 1)
                            sc.activation(br_conv[:, c, 0:CLEN], br_conv[:, c, 0:CLEN], ACT.Silu,
                                          scale=par("conv_g", BC)[:, c:c + 1],
                                          bias=par("conv_beta", BC)[:, c:c + 1]).then_inc(S["conv_ready"], 1)
                    pool_out(m)
                for m in range(PAIRS):
                    by_group("k", m, k_rot[:, m, :], kctx[:, m, :], 1.0, "k_in")
                for m in range(PAIRS):
                    by_group("val", m, vT[:, m, 0:LAT], vT[:, m, LAT:TOK], 1.0, "v_in")
                sc.wait_ge(S["k_in"], 2 * PAIRS)
                sc.dma_start(a["new_k"][l], kctx).then_inc(kv_stored, 16)
                units = attention_units()

                def exp_scores(u):
                    sc.wait_ge(S["s_ready"], u + 1)
                    lo = 320 if units[u][1] is None else 64
                    sc.activation(prob[:, u % 2, lo:448], prob[:, u % 2, lo:448], ACT.Exp,
                                  bias=nmax[:, u % 2:u % 2 + 1], accum_out=rsum[:, u % 2:u % 2 + 1]).then_inc(S["p_exp"], 1)

                def copy_turned(u):
                    chunks = key_chunks(units[u][1])
                    sc.wait_ge(S["p_turned"], u + 1)
                    if u:
                        sc.wait_ge(S["o_done"], u)
                    sc.activation(prob_t[:, 0:len(chunks) * P], PS[2][:, 1, 0:len(chunks) * P],
                                  ACT.Copy).then_inc(S["pt_ready"], 1)

                i = 0
                for n in GATE_ORDER:
                    if n == 0:
                        sc.wait_ge(S["o_done"], len(units))
                        sc.wait_ge(kv_stored, l * 32 + 32)
                        sc.wait_ge(S["x_stored"], 16)
                        sc.dma_start(region_m[:, :], a["x_store"]).then_inc(S["x_back"], 16)
                    for m in range(KC):
                        sc.wait_ge(S["gate_done"], i + 1)
                        if i:
                            sc.wait_ge(S["br_used"], i)
                        else:
                            sc.wait_ge(S["roped"], 8)
                        if n == 1:
                            for b, t0, t1 in ((0, 0, LAT), (1, LAT, TOK)):
                                sc.activation(gate[:, t0:t1], PS[0][:, b, 0:t1 - t0],
                                              ACT.Sigmoid).then_inc(S["gate_sig"], 1)
                        else:
                            sc.activation(gate.rearrange("p (b t) -> p b t", b=2), PS[0][:, :, 0:HALF],
                                          ACT.Sigmoid).then_inc(S["gate_sig"], 2)
                        for slot in (2 * i, 2 * i + 1):
                            u = slot - ATT_SLOT
                            if slot == 1:
                                sc.wait_ge(S["v_tok"], TT)
                                sc.dma_start(a["new_v"][l], val[:, 4, :]).then_inc(kv_stored, 16)
                            if n and 0 <= u < len(units):
                                exp_scores(u)
                            if n and 1 <= u < len(units) + 1:
                                copy_turned(u - 1)
                        i += 1
                for k in range(KC):
                    sc.wait_ge(S["x_mixed"], 2 * (k + 1))
                    if k >= 2:
                        sc.wait_ge(S["square_used"], KC - 1 + BC - 1 + k - 1)
                    sc.activation(sq2[:, k % 2, 0:TOK], x[:, k, :], ACT.Square).then_inc(S["squared"], 1)
                sc.dma_start(spread[0:NE, :], a["spread"]).then_inc(S["spread_in"], 16)
                root("var_ready", 3, rstd[:, 0:TOK])
                modulate(1)
                sc.wait_ge(S["logit_sub"], 1)
                sc.activation(aff, aff, ACT.Exp).then_inc(S["aff_exp"], 1)
                for t in range(0, TT, 2):
                    sc.wait_ge(S["h2_turned"], t + 1)
                    sc.activation(h_tok[:, t, :].rearrange("p (b d) -> p b d", b=2), PS[t % 2][:, :, :],
                                  ACT.Copy).then_inc(S["h2_tok_a"], 1)
                sc.wait_ge(S["aff_turned"], 1)
                sc.activation(affT[:, 0:LAT], PS[2][0:NE, 0, :], ACT.Copy).then_inc(S["aff_copied"], 1)
                sc.activation(affT[:, LAT:TOK], PS[2][0:NE, 1, 0:CTX], ACT.Copy).then_inc(S["aff_copied"], 1)
                for q in range(EPAIRS):
                    sc.wait_ge(S["spread_done"], q + 1)
                    if q >= 2:
                        sc.wait_ge(S["put_ready"], 2 * (q - 1))
                    sc.activation(sq2[:, q % 2, 0:LAT], PS[1][:, 0, :], ACT.Copy).then_inc(S["spread_aff"], 1)
                    sc.activation(sq2[0:2 * CROWS, q % 2, LAT:TOK], PS[1][0:2 * CROWS, 1, 0:CTX], ACT.Copy).then_inc(S["spread_aff"], 1)
                sc.wait_ge(S["ctx_gathered"], 1)
                sc.activation(xs_ctx[:, 0:4, :].rearrange("p (b k) s -> p b (k s)", b=2), PS[0][:, :, :],
                              ACT.Copy).then_inc(S["ctx_xs"], 1)
                sc.wait_ge(S["ctx_rows_zero"], 1)

                def chosen(q):
                    sc.wait_ge(S["gathered"], q + 1)
                    for j in range(2):
                        sc.activation(xs[:, j, :, 0:CAPL].rearrange("p (b k) c -> p b k c", b=2),
                                      PS[0][:, :, :].rearrange("p b (k c) -> p b k c", k=4)[:, :, :, j * CAPL:(j + 1) * CAPL],
                                      ACT.Copy).then_inc(S["xs_ready"], 1)

                def expert_pair(q, final):
                    for j in range(2):
                        done = q * 4 + 2 * j
                        for half in range(2):
                            sc.wait_ge(S["a_done"], done + half + 1)
                            sc.activation(act[:, half, :], PS[0][0:CAP, half, :], ACT.Silu).then_inc(S["sil_ready"], 1)
                        if j and not final:
                            chosen(q + 1)
                        for half in range(2):
                            sc.wait_ge(S["y_done"], done + half + 1)
                            cols = slice(half * 512, (half + 1) * 512)
                            sc.activation(y_l[j * CAPL:(j + 1) * CAPL, cols], PS[2][0:CAPL, half, :],
                                          ACT.Copy).then_inc(S["y_ready"], 1)
                            sc.activation(y_c[j * CROWS:j * CROWS + CAPC, cols], PS[2][CAPL:CAP, half, :],
                                          ACT.Copy).then_inc(S["y_ready"], 1)

                chosen(0)
                with sc.Fori(0, EPAIRS - 1) as q:
                    expert_pair(q, False)
                expert_pair(EPAIRS - 1, True)
                sc.drain().then_inc(layer_done, 1)
                sc.wait_ge(layer_go, l + 1)
            for k in range(KC):
                sc.activation(h[:, k, :], x[:, k, :], ACT.Square).then_inc(final_sq, 1)
            sc.wait_ge(final_root, 1)
            sc.activation(rstd[:, 0:TOK], rstd[:, 0:TOK], ACT.Sqrt).then_inc(final_root, 1)

        @block.vector
        def _(v):
            def layer_body(l):
                link = linker(v, "dve_step")
                v.wait_ge(S["params_in"], 16)

                def normalise(norm, n):
                    v.wait_ge(S["norm_sum"], norm + 1)
                    v.tensor_scalar(rstd[:, 0:TOK].rearrange("p (b t) -> p b t", b=2), PS[2][:, :, 0:HALF],
                                    1.0 / D, EPS, ALU.mult, ALU.add).then_inc(S["var_ready"], 1)
                    v.wait_ge(S["root_ready"], n)
                    link(v.reciprocal(rstd[:, 0:TOK], rstd[:, 0:TOK]))
                    for k in range(KC):
                        v.tensor_tensor(h[:, k, :], x[:, k, :], rstd[:, 0:TOK], ALU.mult).then_inc(S["xr_ready"], 1)

                normalise(0, 1)

                def modulation(norm, g):
                    v.wait_ge(S["mod_sum"], ADA_BLOCKS if norm else ADA_FIRST)
                    n0, n1 = (4 * ADA_FIRST, 48) if norm else (0, 4 * ADA_FIRST)
                    link(v.tensor_tensor(mod3[:, n0:n1, :], mod3[:, n0:n1, :],
                                         par("b_ada", 48)[:, n0:n1].unsqueeze(2).broadcast_to([P, n1 - n0, 2]), ALU.add))
                    link(v.scalar_tensor_tensor(msc[:, norm], mod3[:, 24 * norm + 8:24 * norm + 16, :], 1.0,
                                                par(g, KC).unsqueeze(2).broadcast_to([P, KC, 2]), ALU.add, ALU.mult),
                         "mod_ready")

                modulation(0, "g1")
                v.wait_ge(S["pads_zero"], 1)
                for c in range(BC):
                    v.wait_ge(S["conv_sig"], 2 * (c + 1))
                    tile = (f"conv{c // 2}", 2 * (c % 2) + 1)
                    v.wait_ge(S["tile_done"], tile_count(*tile))
                    ps, yp = PS[TILE_AT[tile] % 3], ypad[:, c % 2, :]
                    v.tensor_tensor(yp[:, CPAD:CPAD + LAT], ps[:, 0, :], sig2[:, c % 2, 0:LAT], ALU.mult)\
                        .then_inc(S["conv_in"], 1)
                    v.tensor_tensor(yp[:, 2 * CPAD + LAT:2 * CPAD + TOK], ps[:, 1, 0:CTX], sig2[:, c % 2, LAT:TOK],
                                    ALU.mult).then_inc(S["conv_in"], 1)
                    v.wait_ge(S["conv_in"], 2 * (c + 1))
                    cw = par("conv_w", BC * TAPS)[:, c * TAPS:(c + 1) * TAPS]
                    acc = br_conv[:, c, 0:CLEN]
                    link(v.tensor_scalar(acc, yp[:, 0:CLEN], cw[:, 0:1], par("conv_b", BC)[:, c:c + 1], ALU.mult, ALU.add))
                    for tap in range(1, TAPS):
                        link(v.scalar_tensor_tensor(acc, yp[:, tap:tap + CLEN], cw[:, tap:tap + 1], acc, ALU.mult, ALU.add),
                             "dve_step" if tap < TAPS - 1 else "conv_acc")
                v.wait_ge(S["conv_mean"], 1)
                for c in range(BC):
                    for b, t0, t1 in ((0, 0, LAT), (1, CCTX, CLEN)):
                        v.scalar_tensor_tensor(br_conv[:, c, t0:t1], PS[3][:, b, 0:t1 - t0], -1.0 / BW,
                                               br_conv[:, c, t0:t1], ALU.mult, ALU.add).then_inc(S["conv_centred"], 1)
                v.wait_ge(S["h_ready"], 2 * KC)
                link(v.memset(rstd[:, LAT:CCTX], 1.0))
                v.wait_ge(S["conv_var"], 1)
                for b, t0, t1 in ((0, 0, LAT), (1, CCTX, CLEN)):
                    link(v.tensor_scalar(rstd[:, t0:t1], PS[3][:, b, 0:t1 - t0], 1.0 / BW, EPS, ALU.mult, ALU.add),
                         "conv_norm")
                v.wait_ge(S["root_ready"], 2)
                link(v.reciprocal(rstd[:, 0:CLEN], rstd[:, 0:CLEN]))
                v.wait_ge(S["conv_centred"], 2 * BC)
                for c in range(BC):
                    v.tensor_tensor(br_conv[:, c, 0:CLEN], br_conv[:, c, 0:CLEN], rstd[:, 0:CLEN], ALU.mult)\
                        .then_inc(S["conv_norm"], 1)
                for t in range(TT):
                    v.wait_ge(S["zv_ready"], t + 1)
                    link(v.bn_stats(stats6[:, t, :], gv[:, t, :]))
                    link(v.bn_aggr(stats2[:, t, :], stats6[:, t, :]))
                link(v.tensor_scalar(vroot, stats2[:, :, 1], EPS, None, ALU.add), "var_ready")
                v.wait_ge(S["root_ready"], 3)
                link(v.reciprocal(vroot, vroot))
                for t in range(TT):
                    link(v.tensor_scalar(gv[:, t, :], gv[:, t, :], stats2[:, t, 0:1], vroot[:, t:t + 1],
                                         ALU.subtract, ALU.mult))
                    link(v.tensor_tensor(gv[:, t, :], gv[:, t, :], par("sgu_g", BW), ALU.mult))
                    link(v.tensor_tensor(gv[:, t, :], gv[:, t, :], par("sgu_beta", BW), ALU.add), "sgu_norm")

                def rope(n, src, dst, m, name):
                    v.wait_ge(S[name], 2 * (m + 1))
                    v.wait_ge(S["turned"], n + 1)
                    link(v.tensor_tensor(sig[:, 0:LAT], PS[3][:, n % 2, :], sinT, ALU.mult))
                    link(v.tensor_tensor(dst[:, m, :], src[:, m, 0:LAT], cosT, ALU.mult))
                    link(v.tensor_tensor(dst[:, m, :], dst[:, m, :], sig[:, 0:LAT], ALU.add), "roped")

                for m in range(PAIRS):
                    rope(m, qs, q_rot, m, "q_in")
                for m in range(PAIRS):
                    rope(4 + m, k_rot, k_rot, m, "k_in")
                for t in range(TT):
                    v.wait_ge(S["v_turned"], t + 1)
                    v.tensor_copy(val[:, t, :], PS[3][:, t % 2, :]).then_inc(S["v_tok"], 1)
                modulation(1, "g2")

                def gate_tokens(g):
                    v.wait_ge(S["sgu_mixed"], g + 1)
                    sb_row = par("sgu_b", BW)[:, g * P:(g + 1) * P]
                    v.wait_ge(S["u_ready"], g + 1)
                    link(v.tensor_tensor(mixed[:, 0:LAT].rearrange("p (t q) -> p t q", t=4),
                                         PS[3][:, 0, :].rearrange("p (t q) -> p t q", t=4),
                                         sb_row.unsqueeze(1).broadcast_to([P, 4, P]), ALU.add))
                    link(v.tensor_tensor(mixed[:, LAT:TOK], PS[3][:, 1, 0:CTX], sb_row, ALU.add))
                    link(v.tensor_tensor(br_sgu[:, g, :], br_sgu[:, g, :], mixed, ALU.mult), "sgu_ready")

                units = attention_units()

                def biased(u):
                    head, cb = units[u]
                    v.wait_ge(S["s_done"], u + 1)
                    ps, pr = PS[2][:, 0, :], prob[:, u % 2, :]
                    if u >= 2:
                        v.wait_ge(S["p_turned"], u - 1)
                    if cb is not None:
                        v.wait_ge(S["bias_built"], 3 * (head + 1))
                        var = bias_m[:, head % 2, (0, 1, 1, 2)[cb], :]
                        link(v.tensor_tensor(pr[:, 64:320], ps[:, 0:256], var, ALU.add))
                    link(v.tensor_copy(pr[:, 320:448], ps[:, 256:384]))
                    lo = 320 if cb is None else 64
                    v.tensor_reduce(nmax[:, u % 2:u % 2 + 1], pr[:, lo:448], AX, ALU.max, negate=True)\
                        .then_inc(S["s_ready"], 1)

                def normed(u):
                    lo = 320 if units[u][1] is None else 64
                    v.wait_ge(S["p_exp"], u + 1)
                    link(v.reciprocal(rinv[:, u % 2:u % 2 + 1], rsum[:, u % 2:u % 2 + 1]))
                    v.tensor_scalar(prob[:, u % 2, lo:448], prob[:, u % 2, lo:448], rinv[:, u % 2:u % 2 + 1], None,
                                    ALU.mult).then_inc(S["p_norm"], 1)

                def attended(m):
                    v.wait_ge(S["o_done"], 10 * (m + 1))
                    v.tensor_copy(in_rows(br_att[:, m, 0:LAT]), group_major(PS[3][:, 0, :])).then_inc(S["o_ready"], 1)
                    v.tensor_copy(br_att[:, m, LAT:TOK], PS[3][:, 1, 0:CTX]).then_inc(S["o_ready"], 1)

                def between(slot):
                    if 1 <= slot <= BC:
                        gate_tokens(slot - 1)
                    u = slot - ATT_SLOT
                    if u == 0:
                        v.wait_ge(S["prob_pad"], 1)
                    if 0 <= u < len(units):
                        biased(u)
                        normed(u)
                    if u >= 11 and (u - 11) % 10 == 0 and u <= len(units) + 1:
                        attended((u - 11) // 10)

                i = 0
                for o, n in enumerate(GATE_ORDER):
                    for m in range(KC):
                        if n and i:
                            between(2 * i)
                        v.wait_ge(S["gate_sig"], 2 * (i + 1))
                        v.wait_ge(S["br_done"], i + 1)
                        ps = PS[1]
                        dst = merged[:, m, :] if o == 0 else gate
                        if n == 1:
                            link(v.tensor_tensor(dst[:, 0:LAT], ps[:, 0, :], gate[:, 0:LAT], ALU.mult))
                            link(v.tensor_tensor(dst[:, LAT:TOK], ps[:, 1, 0:CTX], gate[:, LAT:TOK], ALU.mult))
                        else:
                            link(v.tensor_tensor(dst.rearrange("p (b t) -> p b t", b=2), ps[:, :, 0:HALF],
                                                 gate.rearrange("p (b t) -> p b t", b=2), ALU.mult),
                                 "dve_step" if o else "br_used")
                        if o:
                            v.tensor_tensor(merged[:, m, :], merged[:, m, :], gate, ALU.add).then_inc(S["br_used"], 1)
                            v.wait_ge(S["br_used"], i + 1)
                        if n:
                            between(2 * i + 1)
                        i += 1

                def add_gated(m, ps, gate):
                    for g, (b, t0, t1) in enumerate(((0, 0, LAT), (1, LAT, TOK))):
                        yield v.scalar_tensor_tensor(x[:, m, t0:t1], ps[:, b, 0:t1 - t0], mod3[:, gate + m, g:g + 1],
                                                     x[:, m, t0:t1], ALU.mult, ALU.add)

                v.wait_ge(S["x_back"], 16)
                for m in range(KC):
                    v.wait_ge(S["out_done"], m + 1)
                    for ins in add_gated(m, PS[m % 2], 16):
                        link(ins, "x_mixed")
                normalise(1, 4)

                v.wait_ge(S["logits"], 1)
                v.wait_ge(S["xr_ready"], 2 * KC)
                lg = PS[3][:, 0, 0:TT * NE].rearrange("p (t e) -> p t e", t=TT)
                link(v.tensor_reduce(rt_max, lg, AX, ALU.max))
                link(v.tensor_tensor(aff, lg, rt_max.unsqueeze(2).broadcast_to([P, TT, NE]), ALU.subtract), "logit_sub")
                v.wait_ge(S["aff_exp"], 1)
                link(v.tensor_reduce(rt_sum, aff, AX, ALU.add))
                link(v.reciprocal(rt_sum, rt_sum))
                link(v.tensor_tensor(aff, aff, rt_sum.unsqueeze(2).broadcast_to([P, TT, NE]), ALU.mult), "aff_ready")
                for t in range(1, TT, 2):
                    v.wait_ge(S["h2_turned"], t + 1)
                    v.tensor_copy(h_tok[:, t, :].rearrange("p (b d) -> p b d", b=2), PS[t % 2][:, :, :])\
                        .then_inc(S["h2_tok_d"], 1)
                v.wait_ge(S["aff_copied"], 2)
                link(v.tensor_copy(affW, affT))
                best = small[0:NE, 72:80]
                for t0, t1, cap in ((0, LAT, CAPL), (LAT, TOK, CAPC)):
                    for _ in range(cap // 8):
                        link(v.max(best, affW[:, t0:t1]))
                        link(v.match_replace(affW[:, t0:t1], best, affW[:, t0:t1], -1.0))
                link(v.tensor_scalar(selT, affW, 0.0, None, ALU.is_lt))
                for t0, t1 in ((0, LAT), (LAT, TOK)):
                    link(v.tensor_tensor_scan(cumT[:, t0:t1], selT[:, t0:t1], selT[:, t0:t1], 0.0, ALU.add, ALU.max))
                link(v.tensor_tensor(slotT, cumT, selT, ALU.mult))
                link(v.tensor_scalar(slotT, slotT, -1.0, None, ALU.add), "slot_ready")
                v.wait_ge(S["slot_turned"], 1)
                link(v.tensor_copy(slot_tok, PS[3][:, 0, 0:TT * NE].rearrange("p (t e) -> p t e", t=TT)))
                iota = con("iota", CAPL)
                for t in range(TT):
                    cap = CAPL if t < 4 else CAPC
                    v.tensor_tensor(pick_l[:, t, :, :] if t < 4 else pick_c[:, :, :],
                                    slot_tok[:, t, :].unsqueeze(2).broadcast_to([P, NE, cap]),
                                    iota[:, 0:cap].unsqueeze(1).broadcast_to([P, NE, cap]), ALU.is_equal)\
                        .then_inc(S["pick_ready"], 1)
                for q in range(EPAIRS):
                    v.wait_ge(S["spread_aff"], 2 * (q + 1))
                    link(v.scalar_tensor_tensor(put_l[:, q, :], PS[0][:, 0, :], con("row64", 1), sq2[:, q % 2, 0:LAT],
                                                ALU.is_equal, ALU.mult), "put_ready")
                    link(v.scalar_tensor_tensor(put_c[0:2 * CROWS, q, :], PS[0][0:2 * CROWS, 1, 0:CTX],
                                                con("row16", 1)[0:2 * CROWS],
                                                sq2[0:2 * CROWS, q % 2, LAT:TOK], ALU.is_equal, ALU.mult), "put_ready")
                v.wait_ge(S["ctx_gathered"], 1)
                v.tensor_copy(xs_ctx[:, 4:8, :].rearrange("p (b k) s -> p b (k s)", b=2), PS[1][:, :, :])\
                    .then_inc(S["ctx_xs"], 1)
                v.sem_inc(S["c_used"], 1)
                with v.Fori(0, EPAIRS) as q:
                    for half in range(4):
                        v.wait_ge(S["sil_ready"], q * 4 + half + 1)
                        v.wait_ge(S["b_done"], q * 4 + half + 1)
                        v.tensor_tensor(act[:, half % 2, :], PS[1][0:CAP, half % 2, :], act[:, half % 2, :],
                                        ALU.mult).then_inc(S["act_ready"], 1)
                        v.wait_ge(S["act_turned"], q * 4 + half + 1)
                        v.tensor_copy(act_t[:, (half % 2) * 4:(half % 2 + 1) * 4, :],
                                      PS[3][:, 0, 0:4 * CAP].rearrange("p (k c) -> p k c", k=4))\
                            .then_inc(S["act_t_ready"], 1)
                    for k in range(KC):
                        v.wait_ge(S["c_done"], q * KC + k + 1)
                        for g, (ps, t0, t1) in enumerate(((PS[1][:, k % 2, :], 0, LAT), (PS[3][:, k % 2, 0:CTX], LAT, TOK))):
                            second = v.scalar_tensor_tensor(x[:, k, t0:t1], ps, mod3[:, 40 + k, g:g + 1],
                                                            x[:, k, t0:t1], ALU.mult, ALU.add)
                            if g:
                                second.then_inc(S["c_used"], 1)
                            
                    v.wait_ge(S["c_used"], q * KC + KC + 1)
                v.drain().then_inc(layer_done, 1)
                v.wait_ge(layer_go, l + 1)

            v.wait_ge(start_in, 16 * 3)
            with v.Fori(0, LAYERS) as l:
                layer_body(l)
            v.wait_ge(final_sum, 1)
            v.tensor_scalar(rstd[:, 0:TOK].rearrange("p (b t) -> p b t", b=2), PS[0][:, :, 0:HALF],
                            1.0 / D, EPS, ALU.mult, ALU.add).then_inc(final_root, 1)
            v.wait_ge(final_root, 2)
            v.reciprocal(rstd[:, 0:TOK], rstd[:, 0:TOK]).then_inc(final_xr, 1)
            v.wait_ge(final_xr, 1)
            for k in range(KC):
                v.tensor_tensor(h[:, k, :], x[:, k, :], rstd[:, 0:TOK], ALU.mult).then_inc(out_ready, 1)
                v.wait_ge(out_ready, 2 * k + 1)
                v.tensor_scalar(h[:, k, :], h[:, k, :], con("final_g", KC)[:, k:k + 1], None, ALU.mult)\
                    .then_inc(out_ready, 1)

        @block.gpsimd
        def _(g):
            g.wait_ge(start_in, 16 * 3)
            with g.Fori(0, LAYERS) as l:
                link = linker(g, "pool_step")
                link(g.memset(ypad, 0.0))
                g.memset(zp, 0.0).then_inc(S["pads_zero"], 1)

                def ada_sum(n):
                    g.wait_ge(S["ada_part_in"], n + 1)
                    link(g.tensor_tensor(ada_part[:, :, 0:2, :], ada_part[:, :, 0:2, :], ada_part[:, :, 2:4, :], ALU.add),
                         "ada_half")
                    g.tensor_tensor(mod3[:, 4 * n:4 * n + 4, :], ada_part[:, :, 0, :], ada_part[:, :, 1, :],
                                    ALU.add).then_inc(S["mod_sum"], 1)

                for n in range(ADA_FIRST + 2):
                    ada_sum(n)
                for c in range(BC):
                    w = 2 << c
                    if c == 1:
                        ada_sum(ADA_FIRST + 2)
                    g.wait_ge(S["pool_in"], 2 * (c + 1))
                    g.wait_ge(S["pads_zero"], 1)
                    src, width = zp[:, c, :], PLEN
                    for d in range(c + 1):
                        dst = (psum_a, psum_b)[d % 2]
                        width -= 1 << d
                        link(g.tensor_tensor(dst[:, 0:width], src[:, 0:width], src[:, 1 << d:(1 << d) + width], ALU.add))
                        src = dst
                    off = PPAD - w // 2
                    edge = con("edge", 64)[:, c * 16:(c + 1) * 16]
                    for t0, n in ((0, LAT), (PCTX - PPAD, CTX)):
                        for e, at in enumerate((off + t0, off + t0 + n - 8)):
                            link(g.tensor_tensor(src[:, at:at + 8], src[:, at:at + 8], edge[:, e * 8:(e + 1) * 8], ALU.mult))
                    n = PLEN - 2 * PPAD
                    link(g.tensor_scalar(src[:, off:off + n], src[:, off:off + n], 1.0 / w, None, ALU.mult))
                    link(g.tensor_tensor(zp[:, c, PPAD:PPAD + n], src[:, off:off + n], zp[:, c, PPAD:PPAD + n],
                                         ALU.subtract), "pool_d")
                for n in range(ADA_FIRST + 3, ADA_BLOCKS):
                    ada_sum(n)
                g.wait_ge(S["conv_norm"], 2 + BC)
                g.memset(prob[:, :, 0:64], 0.0).then_inc(S["prob_pad"], 1)
                mask = con("mask", 96).rearrange("p (v s) -> p v s", v=3)
                for head in range(HEADS):
                    if head:
                        g.wait_ge(S["bias_built"], 3 * head)
                    g.dma_start(bias_w, a["bias"][l, head]).then_inc(bias_in, 16)
                    g.wait_ge(bias_in, l * (16 * HEADS) + 16 * (head + 1))
                    if head >= 2:
                        g.wait_ge(S["s_ready"], 5 * (head - 1))
                    for var in range(3):
                        at = WIDE // 3 - 8 * var
                        g.tensor_tensor(
                            bias_m[:, head % 2, var, :].rearrange("p (g r j) -> p g r j", g=4, r=ROWS),
                            bias_w[:, :, at:at + 32].rearrange("p r (g j) -> p g r j", g=4),
                            mask[:, var, :].rearrange("p (g j) -> p g j", g=4).unsqueeze(2).broadcast_to([P, 4, ROWS, 8]),
                            ALU.add).then_inc(S["bias_built"], 1)
                g.wait_ge(S["put_ready"], 2 * EPAIRS)
                g.memset(y_c, 0.0).then_inc(S["ctx_rows_zero"], 1)
                g.wait_ge(S["ctx_xs"], 2)
                with g.Fori(0, EPAIRS) as q:
                    g.wait_ge(S["gathered"], q + 1)
                    for j in range(2):
                        g.tensor_copy(xs[:, j, :, CAPL:CAP], xs_ctx[:, :, bass.ds((q * 2 + j) * CAPC, CAPC)])\
                            .then_inc(S["xs_ctx_ready"], 1)
                g.drain().then_inc(layer_done, 1)
                g.wait_ge(layer_done, l * 4 + 4)
                g.sem_inc(all_idle, 1)
                g.sem_clear(range(cleared[0], cleared[-1] + 1))
                g.sem_inc(layer_go, 1)


def span_start(cb):
    return min(max(cb * COLS - COLS // 2, 0), GRID_W - 2 * COLS)


ATT_SLOT = 1 + BC


def attention_units():
    return [(head, cb) for head in range(HEADS) for cb in (0, 1, 2, 3, None)]


def key_chunks(cb):
    if cb is None:
        return [(320, P, 4)]
    if cb in (0, 3):
        first = span_start(cb) // COLS
        return [(64, P, first), (192, P, first + 1), (320, P, "cache")]
    first = (span_start(cb) - 8) // COLS
    return [(0, P, first), (128, P, first + 1), (320, P, "cache"), (256, 64, first + 2)]


def _constants():
    half, nf = HD // 2, HD // 4
    inv = (1.0 / (10000.0 ** (np.arange(nf) / nf))).astype(np.float32)
    tok = np.arange(LAT).reshape(ROWS, 8, 8).transpose(1, 0, 2).reshape(-1)
    out = np.zeros((P, NCON), np.float32)
    cos, sin = np.zeros((HD, LAT), np.float32), np.zeros((HD, LAT), np.float32)
    perm = np.zeros((P, P), np.float32)
    for part, pos in ((0, tok // GRID_W), (1, tok % GRID_W)):
        ang = (pos[:, None].astype(np.float32) * inv[None, :]).astype(np.float32)
        for s in range(2):
            rows = slice(part * half + s * nf, part * half + (s + 1) * nf)
            cos[rows] = np.cos(ang).T
            sin[rows] = np.sin(ang).T * (1 if s else -1)
    for i in range(P):
        perm[i ^ nf, i] = 1
    q = np.arange(P)
    qcol = (q // 64) * 8 + q % 8
    mask = np.zeros((P, 3, 32), np.float32)
    for var, cb in enumerate((0, 1, 3)):
        col = cb * COLS + qcol
        start = np.clip(col - COLS // 2, 0, GRID_W - COLS)
        key = span_start(cb) + np.arange(32)
        ok = (key[None] >= start[:, None]) & (key[None] < start[:, None] + COLS)
        mask[:, var] = np.where(ok, 0.0, NEG)
    edge = np.ones((4, 2, 8), np.float32)
    for g in range(4):
        w = 2 << g
        for t in range(8):
            edge[g, 0, t] = w / (w - max(0, w // 2 - t))
            edge[g, 1, t] = w / (w - max(0, w // 2 - 1 - (7 - t)))
    for name, value in (("cos", np.tile(cos, (2, 1))), ("sin", np.tile(sin, (2, 1))), ("ident", np.eye(P)),
                        ("ones", np.ones((P, P))), ("perm", perm), ("mask", mask.reshape(P, -1)),
                        ("edge", np.broadcast_to(edge.reshape(1, -1), (P, 64))),
                        ("iota", np.broadcast_to(np.arange(CAPL)[None], (P, CAPL))),
                        ("row64", (q % CAPL)[:, None]), ("row16", np.where(q % CROWS < CAPC, q % CROWS, -2)[:, None])):
        out[:, CON[name]:CON[name] + value.shape[1]] = value
    spread = np.zeros((NE, D + EPAIRS * 2 * CROWS), np.float32)
    for e in range(NE):
        pair, j = e // 2, e % 2
        spread[e, pair * P + j * CAPL:pair * P + (j + 1) * CAPL] = 1
        at = D + (pair * 2 + j) * CROWS
        spread[e, at:at + CAPC] = 1
    return out, spread


def _blocks(w, cols=512):
    *lead, k, n = w.shape
    w = w.reshape(*lead, k // P, P, n // cols, cols)
    a = len(lead)
    w = w.transpose(*range(a), a + 2, a + 1, a, a + 3)
    return w.reshape(*lead, n // cols, P, (k // P) * cols)


def _columns(v):
    return np.swapaxes(v.reshape(*v.shape[:-1], -1, P), -1, -2)


def kernel(**inputs):
    import concourse.bacc as bacc
    from concourse.bass_utils import run_bass_kernel_spmd as run

    i = {k: np.asarray(v) for k, v in inputs.items()}
    L = LAYERS
    tokens = np.concatenate([i["x_sample"][0], i["x_prompt"][0]], 0)
    w_in = i["w_in"]
    conv = w_in[:, :, 1536:2560].reshape(L, D, 2, BC, P)[:, :, ::-1].transpose(0, 1, 3, 2, 4).reshape(L, D, 1024)
    parts = [conv, w_in[:, :, 2560:3072], w_in[:, :, 3072:3584], w_in[:, :, 3584:4096], w_in[:, :, 0:1536]]
    ada, into = _blocks(i["w_ada"]), _blocks(np.concatenate(parts, -1))
    blocks = [ada[:, :ADA_FIRST]]
    for n in range(len(PHASES)):
        blocks += [into[:, n:n + 1], ada[:, ADA_FIRST + n:ADA_FIRST + n + 1]]
    for n in GATE_ORDER:
        gate = _blocks(w_in[:, :, 4096 + n * D:4096 + (n + 1) * D])
        branch = _blocks(i["w_branch"][:, n], D)
        blocks += [gate[:, 0:1], branch, gate[:, 1:2]]
    blocks.append(_blocks(i["w_out"]))
    w_mix = np.concatenate(blocks, 1)
    w1, w3, w2 = (_blocks(i[n]) for n in ("w1", "w3", "w2"))
    w_exp = np.concatenate([w1[:, :, 0:1], w3[:, :, 0:1], w1[:, :, 1:2], w3[:, :, 1:2], w2], 2)\
        .reshape(L, EPAIRS, 2 * EXP_BLOCKS, P, 4096)

    params = np.zeros((L, P, NPAR), np.float32)
    row = lambda v: np.broadcast_to(v.reshape(L, 1, -1), (L, P, v[0].size))
    for name, value in (
            ("b_ada", _columns(i["b_ada"])), ("g1", _columns(i["norm1_g"])), ("g2", _columns(i["norm2_g"])),
            ("conv_b", _columns(i["conv_b"])), ("conv_g", _columns(i["conv_ln_g"])),
            ("conv_beta", _columns(i["conv_ln_b"])), ("pool_scale", _columns(i["pool_scale"])),
            ("conv_w", i["conv_w"].reshape(L, TAPS, BC, P).transpose(0, 3, 2, 1).reshape(L, P, -1)),
            ("router", i["w_router"].reshape(L, KC, P, NE).transpose(0, 2, 1, 3).reshape(L, P, -1)),
            ("pool_w", i["pool_w"].transpose(0, 2, 1, 3).reshape(L, P, -1)),
            ("sgu_w", i["sgu_w"].transpose(0, 3, 1, 2).reshape(L, P, -1)),
            ("sgu_g", row(i["sgu_ln_g"])), ("sgu_beta", row(i["sgu_ln_b"])), ("sgu_b", row(i["sgu_b"]))):
        params[:, :, PAR[name]:PAR[name] + value.shape[-1]] = value
    consts, spread = _constants()
    consts[:, CON["final_g"]:CON["final_g"] + KC] = _columns(i["final_g"])

    wide = np.zeros((L, HEADS, 15, 31 + 2 * 24), np.float32)
    wide[..., 24:55] = i["rpb"]
    q = np.arange(P)
    qrow, qcol = (q // 8) % 8, (q // 64) * 8 + q % 8
    at_row = np.arange(ROWS)[None, :] - qrow[:, None] + 7
    at_col = np.arange(WIDE)[None, :] - 16 - qcol[:, None] + 15 + 24
    bias = wide[:, :, at_row[:, :, None], at_col[:, None, :]]

    arrays = {
        "x0": tokens.T.reshape(KC, P, TOK).transpose(1, 0, 2).reshape(P, -1),
        "cond": np.concatenate([np.stack([i["c"][0], i["c_ctx"]], -1).reshape(KC, P, 2).transpose(1, 0, 2)
                                .reshape(P, -1), np.zeros((P, 30), np.float32)], 1),
        "consts": consts, "spread": spread, "params": params, "bias": bias,
        "w_mix": w_mix, "w_exp": w_exp,
        "ck": i["cache_k"][0].reshape(L, PAIRS, 2, P, HD).transpose(0, 2, 4, 1, 3).reshape(L, P, PAIRS, P),
        "cv": i["cache_v"][0].transpose(0, 2, 1, 3).reshape(L, P, BW),
    }
    arrays = {k: np.ascontiguousarray(v) for k, v in arrays.items()}
    nc = bacc.Bacc("TRN2", target_bir_lowering=False, num_devices=1)
    a = {k: nc.dram_tensor(f"in_{k}", v.shape, F32, kind="ExternalInput").ap() for k, v in arrays.items()}
    a["x_store"] = nc.dram_tensor("x_store", (P, KC * TOK), F32, kind="Internal").ap()
    for name, shape in (("y", (P, KC, TOK)), ("new_k", (L, P, PAIRS, CTX)), ("new_v", (L, CTX, BW))):
        a[name] = nc.dram_tensor(f"out_{name}", shape, F32, kind="ExternalOutput").ap()
    step_kernel(nc, a)
    r = run(nc, [{f"in_{k}": v for k, v in arrays.items()}], core_ids=[0]).results[0]
    y = r["out_y"].transpose(1, 0, 2).reshape(D, TOK).T
    new_k = r["out_new_k"].reshape(L, 2, HD, PAIRS, CTX).transpose(0, 3, 1, 4, 2).reshape(1, L, HEADS, CTX, HD)
    new_v = r["out_new_v"].reshape(L, CTX, HEADS, HD).transpose(0, 2, 1, 3)[None]
    return (np.ascontiguousarray(y[LAT:][None]), np.ascontiguousarray(y[:LAT][None]),
            np.ascontiguousarray(new_k), np.ascontiguousarray(new_v))
```

```python
from contextlib import ExitStack

import numpy as np

import concourse.bass as bass
from concourse import mybir

F32 = mybir.dt.float32
ALU = mybir.AluOpType
ACT = mybir.ActivationFunctionType
AX = mybir.AxisListType.X

P = 128
LAYERS = 2
D = 1024
KC = D // P
LAT, CTX = 512, 128
TOK = LAT + CTX
HALF = TOK // 2
TT = TOK // P
HEADS, HD = 8, 64
PAIRS = HEADS // 2
GRID_W, ROWS, COLS = 64, LAT // 64, 16
BW = 512
BC = BW // P
TAPS = 31
CPAD = TAPS // 2
CLEN = LAT + CPAD + CTX
CCTX = LAT + CPAD
PPAD = 8
PLEN = PPAD + LAT + PPAD + CTX + PPAD
PCTX = PPAD + LAT + PPAD
NE = 16
CAPL, CAPC = 2 * LAT // NE, 2 * CTX // NE
CAP = CAPL + CAPC
EPAIRS = NE // 2
CROWS = 32
EPS = 1e-6
NEG = -1e30
SLOTS = 3
WIDE = 48

ADA_BLOCKS, ADA_FIRST = 12, 4
PHASES = ("conv0", "conv1", "pool", "u", "v", "q", "k", "val")
IN_BLOCK = {name: ADA_FIRST + 2 * i for i, name in enumerate(PHASES)}


def ada_block(n):
    return n if n < ADA_FIRST else 2 * n - ADA_FIRST + 1


TILES = []
for _i, _name in enumerate(PHASES):
    TILES += [(_name, 0), ("ada", ADA_FIRST + _i)] + [(_name, _m) for _m in range(1, 5 if _name == "v" else 4)]
TILE_AT = {_t: _n for _n, _t in enumerate(TILES)}
GATE_ORDER = (2, 3, 1, 0)
OUT_BLOCK = 32
MIX_BLOCKS = 34
EXP_BLOCKS = 6


def tile_count(phase, m):
    return sum(name != "ada" for name, _ in TILES[:TILE_AT[phase, m] + 1])


def first_in_slot(n):
    return n // SLOTS


def per_layer(s):
    mixer = len(range(s, MIX_BLOCKS, SLOTS))
    return mixer + EXP_BLOCKS * NE // SLOTS


def _layout(parts):
    at, out = 0, {}
    for name, n in parts:
        out[name] = at
        at += n
    return out, at


PAR, NPAR = _layout([("b_ada", 48), ("g1", KC), ("g2", KC), ("conv_b", BC), ("conv_g", BC),
                     ("conv_beta", BC), ("pool_scale", BC), ("conv_w", BC * TAPS), ("router", KC * NE),
                     ("pool_w", BW), ("sgu_w", BW), ("sgu_g", BW), ("sgu_beta", BW), ("sgu_b", BW)])
CON, NCON = _layout([("cos", LAT), ("sin", LAT), ("ident", P), ("ones", P), ("perm", P),
                     ("mask", 3 * 32), ("edge", 4 * 2 * 8), ("iota", CAPL), ("row64", 1), ("row16", 1),
                     ("final_g", KC)])


def group_major(ap):
    return ap.rearrange("p (g r j) -> p r g j", g=8, r=ROWS)


def in_rows(ap):
    return ap.rearrange("p (r g j) -> p r g j", g=8, r=ROWS)


def step_kernel(nc, a):
    with ExitStack() as ctx:
        def sb(name, n):
            return ctx.enter_context(nc.sbuf_tensor(name, [P, n], F32))

        def sem(name):
            return ctx.enter_context(nc.semaphore(name))

        ring = sb("ring", SLOTS * 4096)
        region_x = sb("region_x", KC * TOK)
        hT = sb("hT", KC * TOK)
        region_m = sb("region_m", KC * TOK)
        region_b = sb("region_b", 3 * BC * TOK + BC * 656)
        region_r = sb("region_r", 7168)
        params = sb("params", NPAR)
        consts = sb("consts", NCON)
        sq = sb("sq", 2 * 656)
        sig = sb("sig", 2 * TOK)
        rstd = sb("rstd", 656)
        mod = sb("mod", 96)
        mscale = sb("mscale", 2 * 2 * KC)
        cond = sb("cond", 2 * KC + 30)
        small = sb("small", 112)
        PS = [ctx.enter_context(nc.psum_tensor(f"ps{i}", [P, 2, 512], F32)) for i in range(4)]

        def par(name, n):
            return params[:, PAR[name]:PAR[name] + n]

        def con(name, n):
            return consts[:, CON[name]:CON[name] + n]

        x = region_m[:, :].rearrange("p (k t) -> p k t", k=KC)
        h = hT[:, :].rearrange("p (k t) -> p k t", k=KC)
        ones, ident, perm = con("ones", P), con("ident", P), con("perm", P)
        cosT, sinT = con("cos", LAT), con("sin", LAT)
        mod3 = mod[:, :].rearrange("p (c g) -> p c g", g=2)
        msc = mscale[:, :].rearrange("p (n k g) -> p n k g", n=2, g=2)
        sq2 = sq[:, :].rearrange("p (b t) -> p b t", b=2)
        sig2 = sig[:, :].rearrange("p (b t) -> p b t", b=2)
        br_att = region_b[:, 0:2560].rearrange("p (c t) -> p c t", c=BC)
        br_pool = region_b[:, 2560:5120].rearrange("p (c t) -> p c t", c=BC)
        br_sgu = region_b[:, 5120:7680].rearrange("p (c t) -> p c t", c=BC)
        br_conv = region_b[:, 7680:7680 + BC * 656].rearrange("p (c t) -> p c t", c=BC)
        YP = CPAD + LAT + CPAD + CTX + CPAD
        ypad = region_b[:, 0:BC * YP].rearrange("p (b t) -> p b t", b=BC)
        vT = br_att
        ada_row = region_x[:, 0:1024].rearrange("p (b n) -> p b n", b=2)
        ada_part = small[:, 80:112].rearrange("p (m g c) -> p m g c", m=4, g=4)
        zp = region_r[:, 0:4 * PLEN].rearrange("p (c t) -> p c t", c=BC)
        psum_a = region_r[:, 4 * PLEN:5 * PLEN]
        psum_b = region_r[:, 5 * PLEN:6 * PLEN]
        qs = region_m[:, 0:2560].rearrange("p (c t) -> p c t", c=PAIRS)
        q_rot = region_m[:, 2560:4608].rearrange("p (c t) -> p c t", c=PAIRS)
        kctx = region_m[:, 4608:5120].rearrange("p (c t) -> p c t", c=PAIRS)
        k_rot = region_r[:, 0:2048].rearrange("p (c t) -> p c t", c=PAIRS)
        val = region_r[:, 2048:4608].rearrange("p (t c) -> p t c", t=TT)
        ck = region_r[:, 4608:5120].rearrange("p (c t) -> p c t", c=PAIRS)
        cv = region_r[:, 5120:5632]
        bias_m = region_r[:, 5632:7168].rearrange("p (b v s) -> p b v s", b=2, v=3)
        bias_w = rstd[:, 0:ROWS * WIDE].rearrange("p (r s) -> p r s", r=ROWS)
        prob = sq[:, 0:2 * 448].rearrange("p (b s) -> p b s", b=2)
        prob_t = sig[:, TOK:TOK + 512]
        gate = sig[:, 0:TOK]
        gv = region_x[:, 2560:5120].rearrange("p (t c) -> p t c", t=TT)
        mixed = region_x[:, 1920:2560]
        nmax, rsum, rinv = small[:, 0:2], small[:, 2:4], small[:, 4:6]
        stats6 = small[:, 8:38].rearrange("p (t s) -> p t s", t=TT)
        stats2 = small[:, 38:48].rearrange("p (t s) -> p t s", t=TT)
        vroot = small[:, 48:53]
        merged = region_x[:, :].rearrange("p (k t) -> p k t", k=KC)
        h_tok = region_x[:, :].rearrange("p (t d) -> p t d", t=TT)
        pick_l = region_b[:, 0:4096].rearrange("p (t e c) -> p t e c", t=4, e=NE)
        pick_c = region_b[:, 4096:4352].rearrange("p (e c) -> p e c", e=NE)
        put_l = region_b[:, 4352:4864]
        put_c = region_b[:, 4864:4992]
        spread = region_b[0:NE, 5120:7168]
        slotT = region_b[0:NE, 7168:7808]
        affT = region_b[0:NE, 7808:8448]
        spread_now = region_b[0:NE, 8448:8704]
        y_c = region_b[:, 8704:9728]
        xs = region_r[:, 0:2 * KC * CAP].rearrange("p (b k c) -> p b k c", b=2, k=KC)
        xs_ctx = region_r[:, 2560:4608].rearrange("p (k s) -> p k s", k=KC)
        act = region_r[:, 4608:5632].rearrange("p (h f) -> p h f", h=2)
        y_l = region_r[:, 5632:6656]
        logit_row = region_r[:, 2560:3200].rearrange("p (b t) -> p b t", b=2)
        act_t = sig[:, 0:KC * P].rearrange("p (k c) -> p k c", k=KC)
        affW = region_r[0:NE, 640:1280]
        selT = region_r[0:NE, 1280:1920]
        cumT = region_r[0:NE, 1920:2560]
        aff = rstd[:, 0:80].rearrange("p (t e) -> p t e", t=TT)
        slot_tok = rstd[:, 80:160].rearrange("p (t e) -> p t e", t=TT)
        rt_max, rt_sum = small[:, 56:61], small[:, 61:66]

        slot_loaded = [sem(f"slot_loaded{i}") for i in range(SLOTS)]
        slot_used = [sem(f"slot_used{i}") for i in range(SLOTS)]
        start_in, cond_in, cond_ready = sem("start_in"), sem("cond_in"), sem("cond_ready")
        layer_done, all_idle, layer_go = sem("layer_done"), sem("all_idle"), sem("layer_go")
        stored, kv_stored, bias_in = sem("stored"), sem("kv_stored"), sem("bias_in")
        out_ready, final_sq, final_add, final_sum, final_root, final_xr = (
            sem(n) for n in ("out_ready", "final_sq", "final_add", "final_sum", "final_root", "final_xr"))
        names = """x_stored x_back params_in cache_in spread_in dve_step pool_step
            squared square_used norm_sum var_ready root_ready xr_ready h_ready ada_rows ada_row_in ada_turned ada_part_in ada_half mod_sum mod_ready
            tile_done conv_sig conv_in pool_in u_ready zv_ready q_in k_in v_in
            pads_zero conv_acc conv_summed conv_mean conv_centred conv_var conv_norm conv_ready
            pool_d poolw_done pool_ready sgu_norm sgu_mixed sgu_ready turned roped
            v_turned v_tok prob_pad bias_built bias_read
            s_done s_ready p_exp p_norm p_turned pt_ready o_done o_ready
            gate_done gate_sig br_done br_used out_done x_mixed
            logits logit_rows logit_turned logit_sub aff_exp aff_ready aff_turned aff_copied slot_ready slot_turned spread_turn spread_done
            put_slot put_ready h2_turned h2_tok pick_ready
            ctx_gathered ctx_xs act_zero gathered xs_ready xs_ctx_ready a_done b_done sil_ready act_ready
            act_turned act_t_ready y_done y_ready c_done c_used""".split()
        S = {n: sem(n) for n in names}
        cleared = [S[n].num for n in names]
        assert cleared == list(range(cleared[0], cleared[0] + len(cleared)))

        block = ctx.enter_context(nc.Block())

        def linker(eng, own):
            n = {}

            def link(ins, name=own):
                n[name] = n.get(name, 0) + 1
                ins.then_inc(S[name], 1)
                eng.wait_ge(S[name], n[name])
            return link

        @block.sync
        def _(sp):
            def load(slot, before, src):
                sp.wait_ge(slot_used[slot], before + 1)
                sp.dma_start(ring[:, slot * 4096:(slot + 1) * 4096], src).then_inc(slot_loaded[slot], 16)

            sp.dma_start(region_m[:, :], a["x0"]).then_inc(start_in, 16)
            for slot in range(SLOTS):
                sp.sem_inc(slot_used[slot], 1)
            with sp.Fori(0, LAYERS) as l:
                for n in range(MIX_BLOCKS):
                    s = n % SLOTS
                    load(s, l * per_layer(s) + first_in_slot(n), a["w_mix"][l, n])
                with sp.Fori(0, EPAIRS) as q:
                    for b in range(2 * EXP_BLOCKS):
                        s = (MIX_BLOCKS + b) % SLOTS
                        load(s, l * per_layer(s) + q * (2 * EXP_BLOCKS // SLOTS)
                             + first_in_slot(MIX_BLOCKS + b),
                             a["w_exp"][l, q, b])
            for k in range(KC):
                sp.wait_ge(out_ready, 2 * (k + 1))
                sp.dma_start(a["y"][:, k, :], h[:, k, :]).then_inc(stored, 16)
            sp.wait_ge(stored, 16 * KC)
            sp.wait_ge(kv_stored, 2 * 16 * LAYERS)

        @block.tensor
        def _(pe):
            pending = []

            def mm(*args, **kw):
                ins = pe.matmul(*args, **kw)
                if pending:
                    ins.then_inc(slot_used[pending.pop(0)], 1)
                return ins

            def weights(l, n, more=0):
                s = n % SLOTS
                pe.wait_ge(slot_loaded[s], (l * per_layer(s) + more) * 16 + 16 * (first_in_slot(n) + 1))
                return ring[:, s * 4096:(s + 1) * 4096].rearrange("p (k n) -> p k n", k=KC)

            def read(n):
                pending.append(n % SLOTS)

            def evacuated(name, m):
                if name == "ada":
                    return "ada_part_in", m + 1
                if name in ("conv0", "conv1"):
                    c = 2 * int(name[-1]) + m // 2
                    return ("conv_in" if m % 2 else "conv_sig"), 2 * (c + 1)
                signal, each = {"pool": ("pool_in", 2), "u": ("u_ready", 1), "v": ("zv_ready", 1), "q": ("q_in", 2),
                                "k": ("k_in", 2), "val": ("v_in", 2)}[name]
                return signal, each * (m + 1)

            tile = [0]

            def tile_slot():
                n = tile[0]
                tile[0] += 1
                if n >= 3:
                    name, v = evacuated(*TILES[n - 3])
                    pe.wait_ge(S[name], v)
                return PS[n % 3]

            def columns(split):
                return ((0, 0, HALF), (1, HALF, TOK)) if split == "half" else ((0, 0, LAT), (1, LAT, TOK))

            def project(w, m, split):
                ps = tile_slot()
                for k in range(KC):
                    if tile[0] == 1:
                        pe.wait_ge(S["h_ready"], 2 * (k + 1))
                    for b, t0, t1 in columns(split):
                        args = dict(start=k == 0, stop=k == KC - 1)
                        at = (ps[:, b, 0:t1 - t0], w[:, k, m * P:(m + 1) * P], h[:, k, t0:t1])
                        last = (pe.matmul if (k, b) == (KC - 1, 1) else mm)(*at, **args)
                last.then_inc(S["tile_done"], 1)

            def over_partitions(ps, total, ranges, done):
                for b, t0, t1 in ranges:
                    last = (pe.matmul if b else mm)(ps[:, b, 0:t1 - t0], ones, total[:, t0:t1], start=True, stop=True)
                last.then_inc(done, 1)

            def norm_sum(adds):
                pe.wait_ge(S["square_used"], adds)
                over_partitions(PS[2], rstd, columns("half"), S["norm_sum"])

            pe.wait_ge(cond_ready, 1)
            with pe.Fori(0, LAYERS) as l:
                tile[0] = 0

                def ada_rows(n, ps):
                    w = weights(l, ada_block(n))
                    if n >= 2:
                        pe.wait_ge(S["ada_part_in"], n - 1)
                    for k in range(KC):
                        g = k % 4
                        last = (pe.matmul if k == KC - 1 else mm)(
                            ps[32 * g:32 * (g + 1), 0, :], cond[:, 2 * k:2 * k + 32], w[:, k, :], start=k < 4,
                            stop=k >= 4, tile_position=(0, 32 * g))
                    last.then_inc(S["ada_rows"], 1)
                    read(ada_block(n))

                def ada_turn(n, ps):
                    pe.wait_ge(S["ada_row_in"], n + 1)
                    for m in range(4):
                        last = pe.transpose(ps[:, 1, m * P:(m + 1) * P], ada_row[:, n % 2, m * P:(m + 1) * P], ident)
                    last.then_inc(S["ada_turned"], 1)

                def ada_tile(phase):
                    n = ADA_FIRST + PHASES.index(phase)
                    ada_rows(n, tile_slot())

                def ada_tile_turn(phase):
                    n = ADA_FIRST + PHASES.index(phase)
                    ada_turn(n, PS[TILE_AT["ada", n] % 3])

                ada_rows(0, PS[0])
                pe.wait_ge(start_in, 16 * 2)
                norm_sum(KC - 1)
                ada_turn(0, PS[0])
                ada_rows(1, PS[1])
                ada_rows(2, PS[0])
                ada_turn(1, PS[1])
                ada_turn(2, PS[0])
                ada_rows(3, PS[1])
                ada_turn(3, PS[1])
                pe.wait_ge(S["ada_part_in"], 4)
                for phase, split in (("conv0", "group"), ("conv1", "group"), ("pool", "group"), ("u", "half")):
                    w = weights(l, IN_BLOCK[phase])
                    for m in range(4):
                        project(w, m, split)
                        if m == 0:
                            ada_tile(phase)
                        if m == 1:
                            ada_tile_turn(phase)
                    read(IN_BLOCK[phase])

                def conv_sum(name, n, done):
                    pe.wait_ge(S[name], n)
                    over_partitions(PS[3], rstd, ((0, 0, LAT), (1, CCTX, CLEN)), S[done])

                w = weights(l, IN_BLOCK["v"])
                for t in range(TT):
                    ps = tile_slot()
                    for k in range(KC):
                        last = (pe.matmul if k == KC - 1 else mm)(
                            ps[:, 0, :], h[:, k, t * P:(t + 1) * P], w[:, k, :], start=k == 0, stop=k == KC - 1)
                    last.then_inc(S["tile_done"], 1)
                    if t == 0:
                        ada_tile("v")
                    if t == 1:
                        ada_tile_turn("v")
                    if t == 2:
                        conv_sum("conv_summed", 1, "conv_mean")
                read(IN_BLOCK["v"])
                conv_sum("square_used", KC - 1 + BC - 1, "conv_var")

                def pool_product(g):
                    pe.wait_ge(S["pool_d"], g + 1)
                    if g:
                        pe.wait_ge(S["pool_ready"], 2 * g)
                    else:
                        pe.wait_ge(S["conv_norm"], 2)
                    pw = par("pool_w", BW)[:, g * P:(g + 1) * P]
                    pe.matmul(PS[3][:, 0, :], pw, zp[:, g, PPAD:PPAD + LAT], start=True, stop=True)
                    pe.matmul(PS[3][:, 1, 0:CTX], pw, zp[:, g, PCTX:PCTX + CTX], start=True,
                              stop=True).then_inc(S["poolw_done"], 1)

                def turn(name, src, m, n):
                    pe.wait_ge(S[name], 2 * (m + 1))
                    if n >= 2:
                        pe.wait_ge(S["roped"], n - 1)
                    else:
                        pe.wait_ge(S["pool_ready"], 2 * BC)
                    pe.matmul(PS[3][:, n % 2, :], perm, src[:, m, 0:LAT], start=True,
                              stop=True).then_inc(S["turned"], 1)

                def turn_values():
                    pe.wait_ge(S["v_in"], 2 * PAIRS)
                    for t in range(TT):
                        if t < 2:
                            pe.wait_ge(S["roped"], 8)
                        else:
                            pe.wait_ge(S["v_tok"], t - 1)
                        for m in range(PAIRS):
                            last = pe.transpose(PS[3][:, t % 2, m * P:(m + 1) * P], vT[:, m, t * P:(t + 1) * P], ident)
                        last.then_inc(S["v_turned"], 1)

                def mix_tokens(g):
                    if g == 0:
                        pe.wait_ge(S["v_tok"], TT)
                        pe.wait_ge(S["sgu_norm"], TT)
                    else:
                        pe.wait_ge(S["sgu_ready"], g)
                    for t in range(TT):
                        last = pe.matmul(PS[3][:, t // 4, (t % 4) * P:(t % 4 + 1) * P],
                                         gv[:, t, g * P:(g + 1) * P], par("sgu_w", BW)[:, g * P:(g + 1) * P],
                                         start=True, stop=True)
                    last.then_inc(S["sgu_mixed"], 1)

                for phase in ("q", "k", "val"):
                    w = weights(l, IN_BLOCK[phase])
                    for m in range(PAIRS):
                        project(w, m, "group")
                        if m == 0:
                            ada_tile(phase)
                        if m == 1:
                            ada_tile_turn(phase)
                        if phase == "q":
                            pool_product(m)
                        elif phase == "k":
                            turn("q_in", qs, m, m)
                        else:
                            turn("k_in", k_rot, m, 4 + m)
                    read(IN_BLOCK[phase])

                units = attention_units()

                def scores(u):
                    head, cb = units[u]
                    hb, m = (head % 2) * HD, head // 2
                    if u:
                        pe.wait_ge(S["s_ready"], u)
                    else:
                        pe.wait_ge(S["cache_in"], 32)
                    ps = PS[2][:, 0, :]
                    if cb is None:
                        pe.matmul(ps[:, 256:384], qs[hb:hb + HD, m, LAT:TOK], kctx[hb:hb + HD, m, :],
                                  start=True, stop=True).then_inc(S["s_done"], 1)
                        return
                    s0 = span_start(cb) * ROWS
                    pe.matmul(ps[:, 0:256], q_rot[hb:hb + HD, m, cb * P:(cb + 1) * P],
                              k_rot[hb:hb + HD, m, s0:s0 + 256], start=True, stop=True)
                    pe.matmul(ps[:, 256:384], qs[hb:hb + HD, m, cb * P:(cb + 1) * P], ck[hb:hb + HD, m, :],
                              start=True, stop=True).then_inc(S["s_done"], 1)

                def turn_probs(u):
                    pe.wait_ge(S["p_norm"], u + 1)
                    if u:
                        pe.wait_ge(S["pt_ready"], u)
                    for i, (c0, _, _) in enumerate(key_chunks(units[u][1])):
                        last = pe.transpose(PS[2][:, 1, i * P:(i + 1) * P], prob[:, u % 2, c0:c0 + P], ident)
                    last.then_inc(S["p_turned"], 1)

                def weigh_values(u):
                    head, cb = units[u]
                    hb, m = (head % 2) * HD, head // 2
                    pe.wait_ge(S["pt_ready"], u + 1)
                    if u == 0:
                        pe.wait_ge(S["sgu_ready"], BC)
                    elif hb == 0 and cb == 0:
                        pe.wait_ge(S["o_ready"], 2 * m)
                    chunks = key_chunks(cb)
                    out = PS[3][hb:hb + HD, 1, 0:P] if cb is None else \
                        PS[3][hb:hb + HD, 0, cb * P:(cb + 1) * P]
                    for i, (_, n, src) in enumerate(chunks):
                        v = val[0:n, src, head * HD:(head + 1) * HD] if src != "cache" else \
                            cv[:, head * HD:(head + 1) * HD]
                        last = pe.matmul(out, v, prob_t[0:n, i * P:(i + 1) * P], start=i == 0,
                                         stop=i == len(chunks) - 1)
                    last.then_inc(S["o_done"], 1)

                def between(slot):
                    if slot == 0:
                        turn_values()
                    elif slot <= BC:
                        mix_tokens(slot - 1)
                    else:
                        u = slot - ATT_SLOT
                        if u < len(units):
                            scores(u)
                        if 2 <= u < len(units) + 2:
                            weigh_values(u - 2)
                        if 1 <= u < len(units) + 1:
                            turn_probs(u - 1)

                i = 0
                for o, n in enumerate(GATE_ORDER):
                    base = 20 + 3 * o
                    split = "group" if n == 1 else "half"
                    src = {0: br_att, 1: br_conv, 2: br_pool, 3: br_sgu}[n]
                    pe.wait_ge(*{0: (S["o_ready"], 2 * PAIRS), 1: (S["conv_ready"], BC),
                                 2: (S["pool_ready"], 2 * BC), 3: (S["sgu_ready"], BC)}[n])
                    for m in range(KC):
                        if m % 4 == 0:
                            wg = weights(l, base + (2 if m else 0))
                        if i:
                            pe.wait_ge(S["gate_sig"], 2 * i)
                        else:
                            pe.wait_ge(S["v_in"], 2 * PAIRS - 2)
                        for k in range(KC):
                            for b, t0, t1 in columns(split):
                                last = (pe.matmul if (k, b) == (KC - 1, 1) else mm)(
                                    PS[0][:, b, 0:t1 - t0], wg[:, k, (m % 4) * P:(m % 4 + 1) * P],
                                    h[:, k, t0:t1], start=k == 0, stop=k == KC - 1)
                        last.then_inc(S["gate_done"], 1)
                        if n:
                            between(2 * i)
                        if m == 0:
                            weights(l, base + 1)
                            s = (base + 1) % SLOTS
                            wb = ring[:, s * 4096:(s + 1) * 4096].rearrange("p (k n) -> p k n", k=BC)
                        if i:
                            pe.wait_ge(S["br_used"], i)
                        else:
                            pe.wait_ge(S["v_in"], 2 * PAIRS)
                        for k in range(BC):
                            for b, t0, t1 in columns(split):
                                rhs = src[:, k, CCTX:CLEN] if n == 1 and b else src[:, k, t0:t1]
                                last = (pe.matmul if (k, b) == (BC - 1, 1) else mm)(
                                    PS[1][:, b, 0:t1 - t0], wb[:, k, m * P:(m + 1) * P],
                                    rhs, start=k == 0, stop=k == BC - 1)
                        last.then_inc(S["br_done"], 1)
                        if n:
                            between(2 * i + 1)
                        i += 1
                        if m == 3:
                            read(base)
                    read(base + 1)
                    read(base + 2)
                pe.wait_ge(S["br_used"], i)
                for m in range(KC):
                    w = weights(l, OUT_BLOCK + m // 4)
                    if m >= 2:
                        pe.wait_ge(S["x_mixed"], 2 * (m - 1))
                    for k in range(KC):
                        for b, t0, t1 in columns("group"):
                            last = (pe.matmul if (k, b) == (KC - 1, 1) else mm)(
                                PS[m % 2][:, b, 0:t1 - t0], w[:, k, (m % 4) * P:(m % 4 + 1) * P],
                                merged[:, k, t0:t1], start=k == 0, stop=k == KC - 1)
                    last.then_inc(S["out_done"], 1)
                    if m % 4 == 3:
                        read(OUT_BLOCK + m // 4)
                norm_sum(2 * (KC - 1) + BC - 1)

                for k in range(KC):
                    pe.wait_ge(S["h_ready"], 2 * (KC + k + 1))
                    at = PAR["router"] + k * NE
                    grp = slice(32 * (k % 4), 32 * (k % 4) + 32)
                    for b, t0, t1 in columns("half"):
                        last = (mm if (k, b) < (KC - 1, 1) else pe.matmul)(
                            PS[3][grp, b, 0:HALF], params[:, at:at + 32], h[:, k, t0:t1], start=k < 4, stop=k >= 4,
                            tile_position=(0, grp.start))
                last.then_inc(S["logits"], 1)

                def turn_h2(t):
                    if t >= 2:
                        pe.wait_ge(S["h2_tok"], t - 1)
                    for k in range(KC):
                        last = pe.transpose(PS[t % 2][:, k // 4, (k % 4) * P:(k % 4 + 1) * P],
                                            h[:, k, t * P:(t + 1) * P], ident)
                    last.then_inc(S["h2_turned"], 1)

                turn_h2(0)
                turn_h2(1)
                pe.wait_ge(S["logit_rows"], 1)
                for t in range(TT):
                    last = pe.transpose(PS[2][:, t // 4, (t % 4) * P:(t % 4 + 1) * P],
                                        logit_row.rearrange("p b t -> p (b t)")[:, t * P:(t + 1) * P], ident)
                last.then_inc(S["logit_turned"], 1)
                pe.wait_ge(S["aff_ready"], 1)
                for t in range(TT):
                    last = pe.transpose(PS[2][0:NE, t // 4, (t % 4) * P:(t % 4 + 1) * P], aff[:, t, :], ident)
                last.then_inc(S["aff_turned"], 1)
                for t in range(2, TT):
                    turn_h2(t)
                pe.wait_ge(S["slot_ready"], 1)
                for t in range(TT):
                    last = pe.transpose(PS[3][:, 0, t * NE:(t + 1) * NE], slotT[:, t * P:(t + 1) * P],
                                        ident[0:NE, 0:NE])
                last.then_inc(S["slot_turned"], 1)
                pe.wait_ge(S["h2_tok"], TT)
                pe.wait_ge(S["pick_ready"], 5)
                for k in range(KC):
                    last = pe.matmul(PS[1 + k // 4][:, (k // 2) % 2, (k % 2) * 256:(k % 2 + 1) * 256],
                                     h_tok[:, 4, k * P:(k + 1) * P], pick_c.rearrange("p e c -> p (e c)"),
                                     start=True, stop=True)
                last.then_inc(S["ctx_gathered"], 1)

                def gather(q):
                    for k in range(KC):
                        for t in range(4):
                            last = pe.matmul(PS[0][:, k // 4, (k % 4) * P:(k % 4 + 1) * P],
                                             h_tok[:, t, k * P:(k + 1) * P],
                                             pick_l[:, t, :, :].rearrange("p e c -> p (e c)")[:, bass.ds(q * P, P)],
                                             start=t == 0, stop=t == 3)
                            if pending:
                                last.then_inc(slot_used[pending.pop(0)], 1)
                    last.then_inc(S["gathered"], 1)

                def expert_pair(q, final):
                    for j in range(2):
                        first = MIX_BLOCKS + EXP_BLOCKS * j
                        done = q * 4 + 2 * j

                        def block(n, rows):
                            w = weights(l, first + n, q * (2 * EXP_BLOCKS // SLOTS))
                            return w.rearrange("p (r k) n -> p r (k n)", r=rows)

                        def part(ps, at, half, lhs, rhs, start, stop, signal=None):
                            m = lhs.shape[-1]
                            ins = (pe.matmul if signal else mm)(ps[at:at + m, half, :], lhs, rhs, start=start, stop=stop,
                                                                tile_position=(0, at))
                            if signal:
                                ins.then_inc(S[signal], 1)

                        lat = [xs[:, j, k, 0:CAPL] for k in range(KC)]
                        cont = [region_r[:, (j * KC + k) * CAP + CAPL:(j * KC + k) * CAP + CAPL + CROWS] for k in range(KC)]

                        def turn_act(half):
                            pe.wait_ge(S["act_ready"], (done + half + 1) * 2)
                            for k in range(4):
                                last = pe.transpose(PS[3][:, 0, k * P:(k + 1) * P],
                                                    act[:, half, k * P:(k + 1) * P], ident)
                            last.then_inc(S["act_turned"], 1)

                        if j == 0:
                            pe.wait_ge(S["xs_ready"], q * 2 + 2)
                            pe.wait_ge(S["xs_ctx_ready"], q * 2 + 2)
                        for b in range(4):
                            if (j, b) == (0, 2):
                                pe.wait_ge(S["spread_turn"], q + 1)
                                pe.wait_ge(S["c_used"], q * KC + 1)
                                el, ec = spread_now[:, 0:P], spread_now[:, P:2 * P]
                                mm(PS[2][:, 0, :], el, slotT[:, 0:LAT], start=True, stop=True)
                                pe.matmul(PS[2][:, 1, :], el, affT[:, 0:LAT], start=True, stop=True)
                                pe.matmul(PS[3][:, 1, 0:CTX], ec, slotT[:, LAT:TOK], start=True, stop=True)
                                pe.matmul(PS[3][:, 1, CTX:2 * CTX], ec, affT[:, LAT:TOK], start=True,
                                          stop=True).then_inc(S["spread_done"], 1)
                            w = block(b, 2)
                            w1 = [w[:, :, 0:512], w[:, :, 512:1024]]
                            w3 = [w[:, :, 1024:1536], w[:, :, 1536:2048]]
                            ks = [(r, 2 * b + r, b + r == 0, b + r == 4) for r in range(2)]
                            for r, k, a, z in ks:
                                part(PS[0], 0, 0, lat[k], w1[0][:, r, :], a, z)
                                part(PS[0], 64, 0, cont[k], w1[0][:, r, :], a, z, "a_done" if z else None)
                                part(PS[1], 96, 0, cont[k], w3[0][:, r, :], a, z)
                            for r, k, a, z in ks:
                                part(PS[0], 64, 1, lat[k], w1[1][:, r, :], a, z)
                                part(PS[1], 0, 0, lat[k], w3[0][:, r, :], a, z, "b_done" if z else None)
                            for r, k, a, z in ks:
                                part(PS[1], 64, 1, lat[k], w3[1][:, r, :], a, z)
                                part(PS[0], 0, 1, cont[k], w1[1][:, r, :], a, z, "a_done" if z else None)
                                part(PS[1], 32, 1, cont[k], w3[1][:, r, :], a, z, "b_done" if z else None)
                                if k == KC - 2:
                                    turn_act(0)
                            read(first + b)
                        if j:
                            if not final:
                                pe.wait_ge(S["sil_ready"], (done + 2) * 2)
                                pe.wait_ge(S["pick_ready"], 9)
                                gather(q + 1)
                            pe.wait_ge(S["y_ready"], q * 8 + 4)
                        else:
                            pe.wait_ge(S["put_ready"], q * 2 + 2)
                        pe.wait_ge(S["act_t_ready"], done + 1)
                        for s in range(2):
                            w = block(4 + s, 4)
                            if s:
                                pe.wait_ge(S["act_t_ready"], done + 2)
                            lat_at, ctx_at = ((0, 96), (64, 32))[s]
                            for i in range(4):
                                k = 4 * s + i
                                for half in range(2):
                                    z = (k, half) == (KC - 1, 1)
                                    part(PS[2], 64 * half, 0, act_t[:, k, lat_at:lat_at + CAPL],
                                         w[:, i, 512 * half:512 * half + 512], k == 0, k == KC - 1, "y_done" if z else None)
                            if s == 0:
                                turn_act(1)
                            for i in (0, 2):
                                for half in range(2):
                                    for odd in range(2):
                                        k = 4 * s + i + odd
                                        z = (k, half) == (KC - 1, 1)
                                        part(PS[2], 64 * half + 32 * odd, 1, act_t[:, k, ctx_at:ctx_at + CROWS],
                                             w[:, i + odd, 512 * half:512 * half + 512], k < 2, k >= KC - 2,
                                             "y_done" if z else None)
                            read(first + 4 + s)
                    for k in range(KC):
                        if k == 0:
                            pe.wait_ge(S["y_ready"], q * 8 + 6)
                        if k >= 2:
                            pe.wait_ge(S["c_used"], q * KC + k)
                        mm(PS[2][:, k % 2, :], y_l[:, k * P:(k + 1) * P], put_l, start=True, stop=True)
                        if k == 0:
                            pe.wait_ge(S["y_ready"], q * 8 + 8)
                        pe.matmul(PS[3][:, k % 2, 0:CTX], y_c[:, k * P:(k + 1) * P], put_c,
                                  start=True, stop=True).then_inc(S["c_done"], 1)

                gather(0)
                with pe.Fori(0, EPAIRS - 1) as q:
                    expert_pair(q, False)
                expert_pair(EPAIRS - 1, True)
                assert not pending
                pe.drain().then_inc(layer_done, 1)
                pe.wait_ge(layer_go, l + 1)
            pe.wait_ge(final_add, KC - 1)
            over_partitions(PS[0], rstd, columns("half"), final_sum)

        @block.scalar
        def _(sc):
            sc.dma_start(cond[:, :], a["cond"]).then_inc(cond_in, 16)
            sc.dma_start(consts[:, :], a["consts"]).then_inc(start_in, 16)
            sc.wait_ge(cond_in, 16)
            sc.activation(cond[:, :], cond[:, :], ACT.Silu).then_inc(cond_ready, 1)
            sc.wait_ge(start_in, 16 * 2)

            def square(k, src, n, adds):
                if k >= 3:
                    sc.wait_ge(S["square_used"], adds + k - 2)
                dst = sq2[:, k % 2, 0:n] if k else rstd[:, 0:n]
                sc.activation(dst, src, ACT.Square).then_inc(S["squared"], 1)

            def root(name, n, ap):
                sc.wait_ge(S[name], n)
                sc.activation(ap, ap, ACT.Sqrt).then_inc(S["root_ready"], 1)

            def modulate(norm):
                sc.wait_ge(S["mod_ready"], 2 if norm else 1)
                for k in range(KC):
                    sc.wait_ge(S["xr_ready"], KC * norm + k + 1)
                    for g, (t0, t1) in enumerate(((0, LAT), (LAT, TOK))):
                        sc.activation(h[:, k, t0:t1], h[:, k, t0:t1], ACT.Identity,
                                      scale=msc[:, norm, k, g:g + 1],
                                      bias=mod3[:, 24 * norm + k, g:g + 1]).then_inc(S["h_ready"], 1)

            def tile_of(phase, m):
                sc.wait_ge(S["tile_done"], tile_count(phase, m))
                return PS[TILE_AT[phase, m] % 3]

            def ada_rows_in(n, ps):
                sc.wait_ge(S["ada_rows"], n + 1)
                sc.activation(ada_row[:, n % 2, :], ps[:, 0, :], ACT.Copy).then_inc(S["ada_row_in"], 1)

            def ada_parts_in(n, ps):
                sc.wait_ge(S["ada_turned"], n + 1)
                if n:
                    sc.wait_ge(S["mod_sum"], n)
                sc.activation(ada_part, ps[:, 1, :].rearrange("p (m g c) -> p m g c", m=4, g=4)[:, :, :, 0:2],
                              ACT.Copy).then_inc(S["ada_part_in"], 1)

            def ada_between(phase, m):
                n = ADA_FIRST + PHASES.index(phase)
                if m < 2:
                    (ada_rows_in, ada_parts_in)[m](n, PS[TILE_AT["ada", n] % 3])

            with sc.Fori(0, LAYERS) as l:
                sc.dma_start(params[:, :], a["params"][l]).then_inc(S["params_in"], 16)
                for k in range(KC):
                    square(k, x[:, k, :], TOK, 0)
                    if k == 2:
                        ada_rows_in(0, PS[0])
                ada_parts_in(0, PS[0])
                root("var_ready", 1, rstd[:, 0:TOK])
                ada_rows_in(1, PS[1])
                ada_rows_in(2, PS[0])
                ada_parts_in(1, PS[1])
                ada_parts_in(2, PS[0])
                ada_rows_in(3, PS[1])
                ada_parts_in(3, PS[1])
                modulate(0)
                sc.dma_start(a["x_store"], region_m[:, :]).then_inc(S["x_stored"], 16)
                sc.wait_ge(S["params_in"], 16)
                for c in range(BC):
                    ps = tile_of(f"conv{c // 2}", 2 * (c % 2))
                    if c >= 2:
                        sc.wait_ge(S["conv_in"], 2 * (c - 1))
                    for b, t0, t1 in ((0, 0, LAT), (1, LAT, TOK)):
                        sc.activation(sig2[:, c % 2, t0:t1], ps[:, b, 0:t1 - t0], ACT.Sigmoid).then_inc(S["conv_sig"], 1)
                    if c % 2 == 0:
                        ada_between(f"conv{c // 2}", 0)
                        ada_between(f"conv{c // 2}", 1)
                sc.wait_ge(S["pads_zero"], 1)
                for g in range(BC):
                    ps = tile_of("pool", g)
                    sc.activation(zp[:, g, PPAD:PPAD + LAT], ps[:, 0, :], ACT.Copy).then_inc(S["pool_in"], 1)
                    sc.activation(zp[:, g, PCTX:PCTX + CTX], ps[:, 1, 0:CTX], ACT.Copy).then_inc(S["pool_in"], 1)
                    ada_between("pool", g)
                for g in range(BC):
                    ps = tile_of("u", g)
                    sc.activation(br_sgu[:, g, :].rearrange("p (b t) -> p b t", b=2), ps[:, :, 0:HALF],
                                  ACT.Gelu_apprx_tanh).then_inc(S["u_ready"], 1)
                    ada_between("u", g)
                sc.dma_start(ck, a["ck"][l]).then_inc(S["cache_in"], 16)
                sc.dma_start(cv, a["cv"][l]).then_inc(S["cache_in"], 16)

                def conv_squares(c):
                    sc.wait_ge(S["conv_centred"], 2 * (c + 1))
                    square(c, br_conv[:, c, 0:CLEN], CLEN, KC - 1)

                for t in range(TT):
                    ps = tile_of("v", t)
                    sc.activation(gv[:, t, :], ps[:, 0, :], ACT.Gelu_apprx_tanh).then_inc(S["zv_ready"], 1)
                    ada_between("v", t)
                    if t == 3:
                        conv_squares(0)
                        conv_squares(1)
                conv_squares(2)
                conv_squares(3)
                root("conv_norm", 2, rstd[:, 0:CLEN])

                def pool_out(g):
                    sc.wait_ge(S["poolw_done"], g + 1)
                    for b, t0, t1 in ((0, 0, LAT), (1, LAT, TOK)):
                        sc.activation(br_pool[:, g, t0:t1], PS[3][:, b, 0:t1 - t0], ACT.Copy,
                                      scale=par("pool_scale", BC)[:, g:g + 1]).then_inc(S["pool_ready"], 1)

                def by_group(phase, m, dst, ctx_dst, scale, name):
                    ps = tile_of(phase, m)
                    sc.activation(group_major(dst), in_rows(ps[:, 0, :]), ACT.Copy, scale=scale).then_inc(S[name], 1)
                    sc.activation(ctx_dst, ps[:, 1, 0:CTX], ACT.Copy, scale=scale).then_inc(S[name], 1)
                    ada_between(phase, m)

                sc.wait_ge(S["x_stored"], 16)
                for m in range(PAIRS):
                    by_group("q", m, qs[:, m, 0:LAT], qs[:, m, LAT:TOK], HD ** -0.5, "q_in")
                    if m == 1:
                        root("var_ready", 2, vroot)
                        for c in range(BC):
                            sc.wait_ge(S["conv_norm"], 2 + c + 1)
                            sc.activation(br_conv[:, c, 0:CLEN], br_conv[:, c, 0:CLEN], ACT.Silu,
                                          scale=par("conv_g", BC)[:, c:c + 1],
                                          bias=par("conv_beta", BC)[:, c:c + 1]).then_inc(S["conv_ready"], 1)
                    pool_out(m)
                for m in range(PAIRS):
                    by_group("k", m, k_rot[:, m, :], kctx[:, m, :], 1.0, "k_in")
                for m in range(PAIRS):
                    by_group("val", m, vT[:, m, 0:LAT], vT[:, m, LAT:TOK], 1.0, "v_in")
                sc.wait_ge(S["k_in"], 2 * PAIRS)
                sc.dma_start(a["new_k"][l], kctx).then_inc(kv_stored, 16)
                units = attention_units()

                def exp_scores(u):
                    sc.wait_ge(S["s_ready"], u + 1)
                    lo = 320 if units[u][1] is None else 64
                    sc.activation(prob[:, u % 2, lo:448], prob[:, u % 2, lo:448], ACT.Exp,
                                  bias=nmax[:, u % 2:u % 2 + 1], accum_out=rsum[:, u % 2:u % 2 + 1]).then_inc(S["p_exp"], 1)

                def copy_turned(u):
                    chunks = key_chunks(units[u][1])
                    sc.wait_ge(S["p_turned"], u + 1)
                    if u:
                        sc.wait_ge(S["o_done"], u)
                    sc.activation(prob_t[:, 0:len(chunks) * P], PS[2][:, 1, 0:len(chunks) * P],
                                  ACT.Copy).then_inc(S["pt_ready"], 1)

                i = 0
                for n in GATE_ORDER:
                    if n == 0:
                        sc.wait_ge(S["o_done"], len(units))
                        sc.wait_ge(kv_stored, l * 32 + 32)
                        sc.wait_ge(S["x_stored"], 16)
                        sc.dma_start(region_m[:, :], a["x_store"]).then_inc(S["x_back"], 16)
                    for m in range(KC):
                        sc.wait_ge(S["gate_done"], i + 1)
                        if i:
                            sc.wait_ge(S["br_used"], i)
                        else:
                            sc.wait_ge(S["roped"], 8)
                        if n == 1:
                            for b, t0, t1 in ((0, 0, LAT), (1, LAT, TOK)):
                                sc.activation(gate[:, t0:t1], PS[0][:, b, 0:t1 - t0],
                                              ACT.Sigmoid).then_inc(S["gate_sig"], 1)
                        else:
                            sc.activation(gate.rearrange("p (b t) -> p b t", b=2), PS[0][:, :, 0:HALF],
                                          ACT.Sigmoid).then_inc(S["gate_sig"], 2)
                        for slot in (2 * i, 2 * i + 1):
                            u = slot - ATT_SLOT
                            if slot == 1:
                                sc.wait_ge(S["v_tok"], TT)
                                sc.dma_start(a["new_v"][l], val[:, 4, :]).then_inc(kv_stored, 16)
                            if n and 0 <= u < len(units):
                                exp_scores(u)
                            if n and 1 <= u < len(units) + 1:
                                copy_turned(u - 1)
                        i += 1
                for k in range(KC):
                    sc.wait_ge(S["x_mixed"], 2 * (k + 1))
                    square(k, x[:, k, :], TOK, KC - 1 + BC - 1)
                sc.dma_start(spread, a["spread"]).then_inc(S["spread_in"], 16)
                root("var_ready", 3, rstd[:, 0:TOK])
                modulate(1)
                sc.wait_ge(S["logits"], 1)
                sc.activation(logit_row, PS[3][:, :, 0:HALF], ACT.Copy).then_inc(S["logit_rows"], 1)
                sc.wait_ge(S["logit_sub"], 1)
                sc.activation(aff, aff, ACT.Exp).then_inc(S["aff_exp"], 1)
                sc.wait_ge(S["aff_turned"], 1)
                sc.activation(affT[:, 0:LAT], PS[2][0:NE, 0, :], ACT.Copy).then_inc(S["aff_copied"], 1)
                sc.activation(affT[:, LAT:TOK], PS[2][0:NE, 1, 0:CTX], ACT.Copy).then_inc(S["aff_copied"], 1)
                for t in range(TT):
                    sc.wait_ge(S["h2_turned"], t + 1)
                    sc.activation(h_tok[:, t, :].rearrange("p (b d) -> p b d", b=2), PS[t % 2][:, :, :],
                                  ACT.Copy).then_inc(S["h2_tok"], 1)
                sc.wait_ge(S["ctx_gathered"], 1)
                for half in range(2):
                    sc.activation(xs_ctx[:, 4 * half:4 * half + 4, :].rearrange("p (b k) s -> p b (k s)", b=2),
                                  PS[1 + half][:, :, :], ACT.Copy).then_inc(S["ctx_xs"], 1)
                sc.wait_ge(S["act_zero"], 1)

                def chosen(q):
                    sc.wait_ge(S["gathered"], q + 1)
                    for j in range(2):
                        sc.activation(xs[:, j, :, 0:CAPL].rearrange("p (b k) c -> p b k c", b=2),
                                      PS[0][:, :, :].rearrange("p b (k c) -> p b k c", k=4)[:, :, :, j * CAPL:(j + 1) * CAPL],
                                      ACT.Copy).then_inc(S["xs_ready"], 1)

                def expert_pair(q, final):
                    for j in range(2):
                        done = q * 4 + 2 * j
                        for half, rows, src, dst in ((0, CAPL, 0, 0), (0, CROWS, 64, 96), (1, CAPL, 64, 64), (1, CROWS, 0, 32)):
                            sc.wait_ge(S["a_done"], done + half + 1)
                            sc.activation(act[dst:dst + rows, half, :], PS[0][src:src + rows, half, :],
                                          ACT.Silu).then_inc(S["sil_ready"], 1)
                        if j and not final:
                            chosen(q + 1)
                        for bank, dst in enumerate((y_l, y_c)):
                            sc.wait_ge(S["y_done"], done + bank + 1)
                            for half in range(2):
                                sc.activation(dst[j * CAPL:(j + 1) * CAPL, half * 512:(half + 1) * 512],
                                              PS[2][half * 64:(half + 1) * 64, bank, :], ACT.Copy).then_inc(S["y_ready"], 1)

                chosen(0)
                with sc.Fori(0, EPAIRS - 1) as q:
                    expert_pair(q, False)
                expert_pair(EPAIRS - 1, True)
                sc.drain().then_inc(layer_done, 1)
                sc.wait_ge(layer_go, l + 1)
            for k in range(KC):
                sc.activation(h[:, k, :] if k else rstd[:, 0:TOK], x[:, k, :], ACT.Square).then_inc(final_sq, 1)
            sc.wait_ge(final_root, 1)
            sc.activation(rstd[:, 0:TOK], rstd[:, 0:TOK], ACT.Sqrt).then_inc(final_root, 1)

        @block.vector
        def _(v):
            def layer_body(l):
                link = linker(v, "dve_step")

                def add_square(k, n, squares):
                    v.wait_ge(S["squared"], squares + k + 1)
                    link(v.tensor_tensor(rstd[:, 0:n], rstd[:, 0:n], sq2[:, k % 2, 0:n], ALU.add), "square_used")

                def normalise(norm, n):
                    v.wait_ge(S["norm_sum"], norm + 1)
                    v.tensor_scalar(rstd[:, 0:TOK].rearrange("p (b t) -> p b t", b=2), PS[2][:, :, 0:HALF],
                                    1.0 / D, EPS, ALU.mult, ALU.add).then_inc(S["var_ready"], 1)
                    v.wait_ge(S["root_ready"], n)
                    link(v.reciprocal(rstd[:, 0:TOK], rstd[:, 0:TOK]))
                    for k in range(KC):
                        v.tensor_tensor(h[:, k, :], x[:, k, :], rstd[:, 0:TOK], ALU.mult).then_inc(S["xr_ready"], 1)

                for k in range(1, KC):
                    add_square(k, TOK, 0)
                normalise(0, 1)
                v.wait_ge(S["params_in"], 16)

                def modulation(norm, g):
                    v.wait_ge(S["mod_sum"], ADA_BLOCKS if norm else ADA_FIRST)
                    n0, n1 = (4 * ADA_FIRST, 48) if norm else (0, 4 * ADA_FIRST)
                    link(v.tensor_tensor(mod3[:, n0:n1, :], mod3[:, n0:n1, :],
                                         par("b_ada", 48)[:, n0:n1].unsqueeze(2).broadcast_to([P, n1 - n0, 2]), ALU.add))
                    link(v.scalar_tensor_tensor(msc[:, norm], mod3[:, 24 * norm + 8:24 * norm + 16, :], 1.0,
                                                par(g, KC).unsqueeze(2).broadcast_to([P, KC, 2]), ALU.add, ALU.mult),
                         "mod_ready")

                modulation(0, "g1")
                v.wait_ge(S["pads_zero"], 1)

                def conv_input(c):
                    v.wait_ge(S["conv_sig"], 2 * (c + 1))
                    tile = (f"conv{c // 2}", 2 * (c % 2) + 1)
                    v.wait_ge(S["tile_done"], tile_count(*tile))
                    ps, yp = PS[TILE_AT[tile] % 3], ypad[:, c, :]
                    v.tensor_tensor(yp[:, CPAD:CPAD + LAT], ps[:, 0, :], sig2[:, c % 2, 0:LAT], ALU.mult)\
                        .then_inc(S["conv_in"], 1)
                    v.tensor_tensor(yp[:, 2 * CPAD + LAT:2 * CPAD + TOK], ps[:, 1, 0:CTX], sig2[:, c % 2, LAT:TOK],
                                    ALU.mult).then_inc(S["conv_in"], 1)
                    v.wait_ge(S["conv_in"], 2 * (c + 1))

                conv_input(0)
                for c in range(BC):
                    cw = par("conv_w", BC * TAPS)[:, c * TAPS:(c + 1) * TAPS]
                    yp, acc = ypad[:, c, :], br_conv[:, c, 0:CLEN]
                    link(v.tensor_scalar(acc, yp[:, 0:CLEN], cw[:, 0:1], par("conv_b", BC)[:, c:c + 1], ALU.mult, ALU.add))
                    for tap in range(1, TAPS):
                        if c < BC - 1 and tap == (TAPS - 1, TAPS // 2, TAPS // 3)[c]:
                            conv_input(c + 1)
                        link(v.scalar_tensor_tensor(acc, yp[:, tap:tap + CLEN], cw[:, tap:tap + 1], acc, ALU.mult, ALU.add),
                             "dve_step" if tap < TAPS - 1 else "conv_acc")
                link(v.tensor_tensor(rstd[:, 0:CLEN], br_conv[:, 0, 0:CLEN], br_conv[:, 1, 0:CLEN], ALU.add))
                link(v.tensor_tensor(rstd[:, 0:CLEN], rstd[:, 0:CLEN], br_conv[:, 2, 0:CLEN], ALU.add))
                link(v.tensor_tensor(rstd[:, 0:CLEN], rstd[:, 0:CLEN], br_conv[:, 3, 0:CLEN], ALU.add), "conv_summed")
                v.wait_ge(S["conv_mean"], 1)
                for c in range(BC):
                    for b, t0, t1 in ((0, 0, LAT), (1, CCTX, CLEN)):
                        v.scalar_tensor_tensor(br_conv[:, c, t0:t1], PS[3][:, b, 0:t1 - t0], -1.0 / BW,
                                               br_conv[:, c, t0:t1], ALU.mult, ALU.add).then_inc(S["conv_centred"], 1)
                for c in range(1, BC):
                    add_square(c, CLEN, KC)
                v.wait_ge(S["conv_var"], 1)
                link(v.memset(rstd[:, LAT:CCTX], 1.0))
                for b, t0, t1 in ((0, 0, LAT), (1, CCTX, CLEN)):
                    link(v.tensor_scalar(rstd[:, t0:t1], PS[3][:, b, 0:t1 - t0], 1.0 / BW, EPS, ALU.mult, ALU.add),
                         "conv_norm")
                v.wait_ge(S["root_ready"], 2)
                link(v.reciprocal(rstd[:, 0:CLEN], rstd[:, 0:CLEN]))
                v.wait_ge(S["conv_centred"], 2 * BC)
                for c in range(BC):
                    v.tensor_tensor(br_conv[:, c, 0:CLEN], br_conv[:, c, 0:CLEN], rstd[:, 0:CLEN], ALU.mult)\
                        .then_inc(S["conv_norm"], 1)
                for t in range(TT):
                    v.wait_ge(S["zv_ready"], t + 1)
                    link(v.bn_stats(stats6[:, t, :], gv[:, t, :]))
                    link(v.bn_aggr(stats2[:, t, :], stats6[:, t, :]))
                link(v.tensor_scalar(vroot, stats2[:, :, 1], EPS, None, ALU.add), "var_ready")
                v.wait_ge(S["root_ready"], 3)
                link(v.reciprocal(vroot, vroot))
                for t in range(TT):
                    link(v.tensor_scalar(gv[:, t, :], gv[:, t, :], stats2[:, t, 0:1], vroot[:, t:t + 1],
                                         ALU.subtract, ALU.mult))
                    link(v.tensor_tensor(gv[:, t, :], gv[:, t, :], par("sgu_g", BW), ALU.mult))
                    link(v.tensor_tensor(gv[:, t, :], gv[:, t, :], par("sgu_beta", BW), ALU.add), "sgu_norm")

                def rope(n, src, dst, m, name):
                    v.wait_ge(S[name], 2 * (m + 1))
                    v.wait_ge(S["turned"], n + 1)
                    link(v.tensor_tensor(sig[:, 0:LAT], PS[3][:, n % 2, :], sinT, ALU.mult))
                    link(v.tensor_tensor(dst[:, m, :], src[:, m, 0:LAT], cosT, ALU.mult))
                    link(v.tensor_tensor(dst[:, m, :], dst[:, m, :], sig[:, 0:LAT], ALU.add), "roped")

                for m in range(PAIRS):
                    rope(m, qs, q_rot, m, "q_in")
                for m in range(PAIRS):
                    rope(4 + m, k_rot, k_rot, m, "k_in")
                for t in range(TT):
                    v.wait_ge(S["v_turned"], t + 1)
                    v.tensor_copy(val[:, t, :], PS[3][:, t % 2, :]).then_inc(S["v_tok"], 1)
                modulation(1, "g2")

                def gate_tokens(g):
                    v.wait_ge(S["sgu_mixed"], g + 1)
                    sb_row = par("sgu_b", BW)[:, g * P:(g + 1) * P]
                    v.wait_ge(S["u_ready"], g + 1)
                    link(v.tensor_tensor(mixed[:, 0:LAT].rearrange("p (t q) -> p t q", t=4),
                                         PS[3][:, 0, :].rearrange("p (t q) -> p t q", t=4),
                                         sb_row.unsqueeze(1).broadcast_to([P, 4, P]), ALU.add))
                    link(v.tensor_tensor(mixed[:, LAT:TOK], PS[3][:, 1, 0:CTX], sb_row, ALU.add))
                    link(v.tensor_tensor(br_sgu[:, g, :], br_sgu[:, g, :], mixed, ALU.mult), "sgu_ready")

                units = attention_units()

                def biased(u):
                    head, cb = units[u]
                    v.wait_ge(S["s_done"], u + 1)
                    ps, pr = PS[2][:, 0, :], prob[:, u % 2, :]
                    if u >= 2:
                        v.wait_ge(S["p_turned"], u - 1)
                    if cb is not None:
                        v.wait_ge(S["bias_built"], 3 * (head + 1))
                        var = bias_m[:, head % 2, (0, 1, 1, 2)[cb], :]
                        link(v.tensor_tensor(pr[:, 64:320], ps[:, 0:256], var, ALU.add))
                    link(v.tensor_copy(pr[:, 320:448], ps[:, 256:384]))
                    lo = 320 if cb is None else 64
                    v.tensor_reduce(nmax[:, u % 2:u % 2 + 1], pr[:, lo:448], AX, ALU.max, negate=True)\
                        .then_inc(S["s_ready"], 1)

                def normed(u):
                    lo = 320 if units[u][1] is None else 64
                    v.wait_ge(S["p_exp"], u + 1)
                    link(v.reciprocal(rinv[:, u % 2:u % 2 + 1], rsum[:, u % 2:u % 2 + 1]))
                    v.tensor_scalar(prob[:, u % 2, lo:448], prob[:, u % 2, lo:448], rinv[:, u % 2:u % 2 + 1], None,
                                    ALU.mult).then_inc(S["p_norm"], 1)

                def attended(m):
                    v.wait_ge(S["o_done"], 10 * (m + 1))
                    v.tensor_copy(in_rows(br_att[:, m, 0:LAT]), group_major(PS[3][:, 0, :])).then_inc(S["o_ready"], 1)
                    v.tensor_copy(br_att[:, m, LAT:TOK], PS[3][:, 1, 0:CTX]).then_inc(S["o_ready"], 1)

                def between(slot):
                    if 1 <= slot <= BC:
                        gate_tokens(slot - 1)
                    u = slot - ATT_SLOT
                    if u == 0:
                        v.wait_ge(S["prob_pad"], 1)
                    if 0 <= u < len(units):
                        biased(u)
                        normed(u)
                    if u >= 11 and (u - 11) % 10 == 0 and u <= len(units) + 1:
                        attended((u - 11) // 10)

                i = 0
                for o, n in enumerate(GATE_ORDER):
                    for m in range(KC):
                        if n and i:
                            between(2 * i)
                        v.wait_ge(S["gate_sig"], 2 * (i + 1))
                        v.wait_ge(S["br_done"], i + 1)
                        ps = PS[1]
                        dst = merged[:, m, :] if o == 0 else gate
                        if n == 1:
                            link(v.tensor_tensor(dst[:, 0:LAT], ps[:, 0, :], gate[:, 0:LAT], ALU.mult))
                            link(v.tensor_tensor(dst[:, LAT:TOK], ps[:, 1, 0:CTX], gate[:, LAT:TOK], ALU.mult))
                        else:
                            link(v.tensor_tensor(dst.rearrange("p (b t) -> p b t", b=2), ps[:, :, 0:HALF],
                                                 gate.rearrange("p (b t) -> p b t", b=2), ALU.mult),
                                 "dve_step" if o else "br_used")
                        if o:
                            v.tensor_tensor(merged[:, m, :], merged[:, m, :], gate, ALU.add).then_inc(S["br_used"], 1)
                            v.wait_ge(S["br_used"], i + 1)
                        if n:
                            between(2 * i + 1)
                        i += 1

                def add_gated(m, ps, gate):
                    for g, (b, t0, t1) in enumerate(((0, 0, LAT), (1, LAT, TOK))):
                        yield v.scalar_tensor_tensor(x[:, m, t0:t1], ps[:, b, 0:t1 - t0], mod3[:, gate + m, g:g + 1],
                                                     x[:, m, t0:t1], ALU.mult, ALU.add)

                v.wait_ge(S["x_back"], 16)
                for m in range(KC):
                    v.wait_ge(S["out_done"], m + 1)
                    for ins in add_gated(m, PS[m % 2], 16):
                        link(ins, "x_mixed")
                    if m >= 2:
                        add_square(m - 1, TOK, KC + BC)
                add_square(KC - 1, TOK, KC + BC)
                normalise(1, 4)

                v.wait_ge(S["logit_turned"], 1)
                v.wait_ge(S["xr_ready"], 2 * KC)
                by_grp = PS[2][:, :, :].rearrange("p b n -> p (b n)")[:, 0:TOK]\
                    .rearrange("p (t g s) -> p t s g", t=TT, g=4)[:, :, 0:NE, :]
                link(v.tensor_reduce(aff, by_grp, AX, ALU.add))
                link(v.tensor_reduce(rt_max, aff, AX, ALU.max))
                link(v.tensor_tensor(aff, aff, rt_max.unsqueeze(2).broadcast_to([P, TT, NE]), ALU.subtract), "logit_sub")
                v.wait_ge(S["aff_exp"], 1)
                link(v.tensor_reduce(rt_sum, aff, AX, ALU.add))
                link(v.reciprocal(rt_sum, rt_sum))
                link(v.tensor_tensor(aff, aff, rt_sum.unsqueeze(2).broadcast_to([P, TT, NE]), ALU.mult), "aff_ready")
                v.wait_ge(S["aff_copied"], 2)
                link(v.tensor_copy(affW, affT))
                best = small[0:NE, 72:80]
                for t0, t1, cap in ((0, LAT, CAPL), (LAT, TOK, CAPC)):
                    for _ in range(cap // 8):
                        link(v.max(best, affW[:, t0:t1]))
                        link(v.match_replace(affW[:, t0:t1], best, affW[:, t0:t1], -1.0))
                link(v.tensor_scalar(selT, affW, 0.0, None, ALU.is_lt))
                for t0, t1 in ((0, LAT), (LAT, TOK)):
                    link(v.tensor_tensor_scan(cumT[:, t0:t1], selT[:, t0:t1], selT[:, t0:t1], 0.0, ALU.add, ALU.max))
                link(v.tensor_tensor(slotT, cumT, selT, ALU.mult))
                link(v.tensor_scalar(slotT, slotT, -1.0, None, ALU.add), "slot_ready")
                v.wait_ge(S["slot_turned"], 1)
                link(v.tensor_copy(slot_tok, PS[3][:, 0, 0:TT * NE].rearrange("p (t e) -> p t e", t=TT)))
                iota = con("iota", CAPL)
                for t, e0, e1 in [(4, 0, NE)] + [(t, 0, 2) for t in range(4)] + [(t, 2, NE) for t in range(4)]:
                    cap = CAPL if t < 4 else CAPC
                    v.tensor_tensor(pick_l[:, t, e0:e1, :] if t < 4 else pick_c[:, :, :],
                                    slot_tok[:, t, e0:e1].unsqueeze(2).broadcast_to([P, e1 - e0, cap]),
                                    iota[:, 0:cap].unsqueeze(1).broadcast_to([P, e1 - e0, cap]), ALU.is_equal)\
                        .then_inc(S["pick_ready"], 1)
                v.sem_inc(S["c_used"], 1)
                with v.Fori(0, EPAIRS) as q:
                    for half in range(4):
                        if half == 0:
                            v.wait_ge(S["spread_done"], q + 1)
                            v.tensor_scalar(put_l, PS[2][:, 0, :], con("row64", 1), None,
                                            ALU.is_equal).then_inc(S["put_slot"], 1)
                            v.tensor_scalar(put_c, PS[3][:, 1, 0:CTX], con("row16", 1), None,
                                            ALU.is_equal).then_inc(S["put_slot"], 1)
                            v.wait_ge(S["put_slot"], q * 2 + 2)
                            v.tensor_tensor(put_l, PS[2][:, 1, :], put_l, ALU.mult).then_inc(S["put_ready"], 1)
                            v.tensor_tensor(put_c, PS[3][:, 1, CTX:2 * CTX], put_c,
                                            ALU.mult).then_inc(S["put_ready"], 1)
                        v.wait_ge(S["sil_ready"], (q * 4 + half + 1) * 2)
                        v.wait_ge(S["b_done"], q * 4 + half + 1)
                        for at, rows in ((64, CAPL), (32, CROWS)) if half % 2 else ((0, CAPL), (96, CROWS)):
                            v.tensor_tensor(act[at:at + rows, half % 2, :], PS[1][at:at + rows, half % 2, :],
                                            act[at:at + rows, half % 2, :], ALU.mult).then_inc(S["act_ready"], 1)
                        v.wait_ge(S["act_turned"], q * 4 + half + 1)
                        v.tensor_copy(act_t[:, (half % 2) * 4:(half % 2 + 1) * 4, :],
                                      PS[3][:, 0, :].rearrange("p (k c) -> p k c", k=4))\
                            .then_inc(S["act_t_ready"], 1)
                    for k in range(KC):
                        v.wait_ge(S["c_done"], q * KC + k + 1)
                        for g, (ps, t0, t1) in enumerate(((PS[2][:, k % 2, :], 0, LAT), (PS[3][:, k % 2, 0:CTX], LAT, TOK))):
                            second = v.scalar_tensor_tensor(x[:, k, t0:t1], ps, mod3[:, 40 + k, g:g + 1],
                                                            x[:, k, t0:t1], ALU.mult, ALU.add)
                            if g:
                                second.then_inc(S["c_used"], 1)
                            
                    v.wait_ge(S["c_used"], q * KC + KC + 1)
                v.drain().then_inc(layer_done, 1)
                v.wait_ge(layer_go, l + 1)

            v.wait_ge(start_in, 16 * 2)
            with v.Fori(0, LAYERS) as l:
                layer_body(l)
            for k in range(1, KC):
                v.wait_ge(final_sq, k + 1)
                v.tensor_tensor(rstd[:, 0:TOK], rstd[:, 0:TOK], h[:, k, :], ALU.add).then_inc(final_add, 1)
                v.wait_ge(final_add, k)
            v.wait_ge(final_sum, 1)
            v.tensor_scalar(rstd[:, 0:TOK].rearrange("p (b t) -> p b t", b=2), PS[0][:, :, 0:HALF],
                            1.0 / D, EPS, ALU.mult, ALU.add).then_inc(final_root, 1)
            v.wait_ge(final_root, 2)
            v.reciprocal(rstd[:, 0:TOK], rstd[:, 0:TOK]).then_inc(final_xr, 1)
            v.wait_ge(final_xr, 1)
            for k in range(KC):
                v.tensor_tensor(h[:, k, :], x[:, k, :], rstd[:, 0:TOK], ALU.mult).then_inc(out_ready, 1)
                v.wait_ge(out_ready, 2 * k + 1)
                v.tensor_scalar(h[:, k, :], h[:, k, :], con("final_g", KC)[:, k:k + 1], None, ALU.mult)\
                    .then_inc(out_ready, 1)

        @block.gpsimd
        def _(g):
            g.wait_ge(start_in, 16 * 2)
            with g.Fori(0, LAYERS) as l:
                link = linker(g, "pool_step")
                link(g.memset(ypad, 0.0))
                g.memset(zp, 0.0).then_inc(S["pads_zero"], 1)

                def ada_sum(n):
                    g.wait_ge(S["ada_part_in"], n + 1)
                    link(g.tensor_tensor(ada_part[:, :, 0:2, :], ada_part[:, :, 0:2, :], ada_part[:, :, 2:4, :], ALU.add),
                         "ada_half")
                    g.tensor_tensor(mod3[:, 4 * n:4 * n + 4, :], ada_part[:, :, 0, :], ada_part[:, :, 1, :],
                                    ALU.add).then_inc(S["mod_sum"], 1)

                for n in range(ADA_FIRST + 2):
                    ada_sum(n)
                for c in range(BC):
                    w = 2 << c
                    if c == 1:
                        ada_sum(ADA_FIRST + 2)
                    g.wait_ge(S["pool_in"], 2 * (c + 1))
                    g.wait_ge(S["pads_zero"], 1)
                    src, width = zp[:, c, :], PLEN
                    for d in range(c + 1):
                        dst = (psum_a, psum_b)[d % 2]
                        width -= 1 << d
                        link(g.tensor_tensor(dst[:, 0:width], src[:, 0:width], src[:, 1 << d:(1 << d) + width], ALU.add))
                        src = dst
                    off = PPAD - w // 2
                    edge = con("edge", 64)[:, c * 16:(c + 1) * 16]
                    for t0, n in ((0, LAT), (PCTX - PPAD, CTX)):
                        for e, at in enumerate((off + t0, off + t0 + n - 8)):
                            link(g.tensor_tensor(src[:, at:at + 8], src[:, at:at + 8], edge[:, e * 8:(e + 1) * 8], ALU.mult))
                    n = PLEN - 2 * PPAD
                    link(g.tensor_scalar(src[:, off:off + n], src[:, off:off + n], 1.0 / w, None, ALU.mult))
                    link(g.tensor_tensor(zp[:, c, PPAD:PPAD + n], src[:, off:off + n], zp[:, c, PPAD:PPAD + n],
                                         ALU.subtract), "pool_d")
                for n in range(ADA_FIRST + 3, ADA_BLOCKS):
                    ada_sum(n)
                g.wait_ge(S["conv_norm"], 2 + BC)
                g.memset(prob[:, :, 0:64], 0.0).then_inc(S["prob_pad"], 1)
                mask = con("mask", 96).rearrange("p (v s) -> p v s", v=3)
                for head in range(HEADS):
                    if head:
                        g.wait_ge(S["bias_built"], 3 * head)
                    g.dma_start(bias_w, a["bias"][l, head]).then_inc(bias_in, 16)
                    g.wait_ge(bias_in, l * (16 * HEADS) + 16 * (head + 1))
                    if head >= 2:
                        g.wait_ge(S["s_ready"], 5 * (head - 1))
                    for var in range(3):
                        at = WIDE // 3 - 8 * var
                        g.tensor_tensor(
                            bias_m[:, head % 2, var, :].rearrange("p (g r j) -> p g r j", g=4, r=ROWS),
                            bias_w[:, :, at:at + 32].rearrange("p r (g j) -> p g r j", g=4),
                            mask[:, var, :].rearrange("p (g j) -> p g j", g=4).unsqueeze(2).broadcast_to([P, 4, ROWS, 8]),
                            ALU.add).then_inc(S["bias_built"], 1)
                g.wait_ge(S["h2_turned"], 1)
                g.memset(region_r[:, 4608:5632], 0.0).then_inc(S["act_zero"], 1)
                g.wait_ge(S["ctx_xs"], 2)
                g.wait_ge(S["spread_in"], 16)
                with g.Fori(0, EPAIRS) as q:
                    g.wait_ge(S["gathered"], q + 1)
                    g.tensor_copy(spread_now, spread[:, bass.ds(q * 2 * P, 2 * P)])\
                        .then_inc(S["spread_turn"], 1)
                    for j in range(2):
                        g.tensor_copy(xs[:, j, :, CAPL:CAP], xs_ctx[:, :, bass.ds((q * 2 + j) * CAPC, CAPC)])\
                            .then_inc(S["xs_ctx_ready"], 1)
                g.drain().then_inc(layer_done, 1)
                g.wait_ge(layer_done, l * 4 + 4)
                g.sem_inc(all_idle, 1)
                g.sem_clear(range(cleared[0], cleared[-1] + 1))
                g.sem_inc(layer_go, 1)


def span_start(cb):
    return min(max(cb * COLS - COLS // 2, 0), GRID_W - 2 * COLS)


ATT_SLOT = 1 + BC


def attention_units():
    return [(head, cb) for head in range(HEADS) for cb in (0, 1, 2, 3, None)]


def key_chunks(cb):
    if cb is None:
        return [(320, P, 4)]
    if cb in (0, 3):
        first = span_start(cb) // COLS
        return [(64, P, first), (192, P, first + 1), (320, P, "cache")]
    first = (span_start(cb) - 8) // COLS
    return [(0, P, first), (128, P, first + 1), (320, P, "cache"), (256, 64, first + 2)]


def _constants():
    half, nf = HD // 2, HD // 4
    inv = (1.0 / (10000.0 ** (np.arange(nf) / nf))).astype(np.float32)
    tok = np.arange(LAT).reshape(ROWS, 8, 8).transpose(1, 0, 2).reshape(-1)
    out = np.zeros((P, NCON), np.float32)
    cos, sin = np.zeros((HD, LAT), np.float32), np.zeros((HD, LAT), np.float32)
    perm = np.zeros((P, P), np.float32)
    for part, pos in ((0, tok // GRID_W), (1, tok % GRID_W)):
        ang = (pos[:, None].astype(np.float32) * inv[None, :]).astype(np.float32)
        for s in range(2):
            rows = slice(part * half + s * nf, part * half + (s + 1) * nf)
            cos[rows] = np.cos(ang).T
            sin[rows] = np.sin(ang).T * (1 if s else -1)
    for i in range(P):
        perm[i ^ nf, i] = 1
    q = np.arange(P)
    qcol = (q // 64) * 8 + q % 8
    mask = np.zeros((P, 3, 32), np.float32)
    for var, cb in enumerate((0, 1, 3)):
        col = cb * COLS + qcol
        start = np.clip(col - COLS // 2, 0, GRID_W - COLS)
        key = span_start(cb) + np.arange(32)
        ok = (key[None] >= start[:, None]) & (key[None] < start[:, None] + COLS)
        mask[:, var] = np.where(ok, 0.0, NEG)
    edge = np.ones((4, 2, 8), np.float32)
    for g in range(4):
        w = 2 << g
        for t in range(8):
            edge[g, 0, t] = w / (w - max(0, w // 2 - t))
            edge[g, 1, t] = w / (w - max(0, w // 2 - 1 - (7 - t)))
    for name, value in (("cos", np.tile(cos, (2, 1))), ("sin", np.tile(sin, (2, 1))), ("ident", np.eye(P)),
                        ("ones", np.ones((P, P))), ("perm", perm), ("mask", mask.reshape(P, -1)),
                        ("edge", np.broadcast_to(edge.reshape(1, -1), (P, 64))),
                        ("iota", np.broadcast_to(np.arange(CAPL)[None], (P, CAPL))),
                        ("row64", (q % CAPL)[:, None]), ("row16", np.where(q % CROWS < CAPC, q % CROWS, -2)[:, None])):
        out[:, CON[name]:CON[name] + value.shape[1]] = value
    spread = np.zeros((NE, EPAIRS * 2 * P), np.float32)
    for e in range(NE):
        at, j = e // 2 * 2 * P, e % 2
        spread[e, at + j * CAPL:at + (j + 1) * CAPL] = 1
        for half in range(2):
            row = at + P + (j * 2 + half) * CROWS
            spread[e, row:row + CAPC] = 1
    return out, spread


def _blocks(w, cols=512):
    *lead, k, n = w.shape
    w = w.reshape(*lead, k // P, P, n // cols, cols)
    a = len(lead)
    w = w.transpose(*range(a), a + 2, a + 1, a, a + 3)
    return w.reshape(*lead, n // cols, P, (k // P) * cols)


def _columns(v):
    return np.swapaxes(v.reshape(*v.shape[:-1], -1, P), -1, -2)


def kernel(**inputs):
    import concourse.bacc as bacc
    from concourse.bass_utils import run_bass_kernel_spmd as run

    i = {k: np.asarray(v) for k, v in inputs.items()}
    L = LAYERS
    tokens = np.concatenate([i["x_sample"][0], i["x_prompt"][0]], 0)
    w_in = i["w_in"]
    conv = w_in[:, :, 1536:2560].reshape(L, D, 2, BC, P)[:, :, ::-1].transpose(0, 1, 3, 2, 4).reshape(L, D, 1024)
    parts = [conv, w_in[:, :, 2560:3072], w_in[:, :, 3072:3584], w_in[:, :, 3584:4096], w_in[:, :, 0:1536]]
    ada, into = _blocks(i["w_ada"]), _blocks(np.concatenate(parts, -1))
    blocks = [ada[:, :ADA_FIRST]]
    for n in range(len(PHASES)):
        blocks += [into[:, n:n + 1], ada[:, ADA_FIRST + n:ADA_FIRST + n + 1]]
    for n in GATE_ORDER:
        gate = _blocks(w_in[:, :, 4096 + n * D:4096 + (n + 1) * D])
        branch = _blocks(i["w_branch"][:, n], D)
        blocks += [gate[:, 0:1], branch, gate[:, 1:2]]
    blocks.append(_blocks(i["w_out"]))
    w_mix = np.concatenate(blocks, 1)
    w13 = np.concatenate([i["w1"], i["w3"]], -1).reshape(L, NE, 4, 2, P, 2 * D).transpose(0, 1, 2, 4, 3, 5)
    w13 = w13.reshape(L, NE, 4, P, 4 * D)
    w2 = i["w2"].reshape(L, NE, 2, 4, P, D).transpose(0, 1, 2, 4, 3, 5).reshape(L, NE, 2, P, 4 * D)
    w_exp = np.concatenate([w13, w2], 2)\
        .reshape(L, EPAIRS, 2 * EXP_BLOCKS, P, 4096)

    params = np.zeros((L, P, NPAR), np.float32)
    row = lambda v: np.broadcast_to(v.reshape(L, 1, -1), (L, P, v[0].size))
    for name, value in (
            ("b_ada", _columns(i["b_ada"])), ("g1", _columns(i["norm1_g"])), ("g2", _columns(i["norm2_g"])),
            ("conv_b", _columns(i["conv_b"])), ("conv_g", _columns(i["conv_ln_g"])),
            ("conv_beta", _columns(i["conv_ln_b"])), ("pool_scale", _columns(i["pool_scale"])),
            ("conv_w", i["conv_w"].reshape(L, TAPS, BC, P).transpose(0, 3, 2, 1).reshape(L, P, -1)),
            ("router", i["w_router"].reshape(L, KC, P, NE).transpose(0, 2, 1, 3).reshape(L, P, -1)),
            ("pool_w", i["pool_w"].transpose(0, 2, 1, 3).reshape(L, P, -1)),
            ("sgu_w", i["sgu_w"].transpose(0, 3, 1, 2).reshape(L, P, -1)),
            ("sgu_g", row(i["sgu_ln_g"])), ("sgu_beta", row(i["sgu_ln_b"])), ("sgu_b", row(i["sgu_b"]))):
        params[:, :, PAR[name]:PAR[name] + value.shape[-1]] = value
    consts, spread = _constants()
    consts[:, CON["final_g"]:CON["final_g"] + KC] = _columns(i["final_g"])

    wide = np.zeros((L, HEADS, 15, 31 + 2 * 24), np.float32)
    wide[..., 24:55] = i["rpb"]
    q = np.arange(P)
    qrow, qcol = (q // 8) % 8, (q // 64) * 8 + q % 8
    at_row = np.arange(ROWS)[None, :] - qrow[:, None] + 7
    at_col = np.arange(WIDE)[None, :] - 16 - qcol[:, None] + 15 + 24
    bias = wide[:, :, at_row[:, :, None], at_col[:, None, :]]

    arrays = {
        "x0": tokens.T.reshape(KC, P, TOK).transpose(1, 0, 2).reshape(P, -1),
        "cond": np.concatenate([np.stack([i["c"][0], i["c_ctx"]], -1).reshape(KC, P, 2).transpose(1, 0, 2)
                                .reshape(P, -1), np.zeros((P, 30), np.float32)], 1),
        "consts": consts, "spread": spread, "params": params, "bias": bias,
        "w_mix": w_mix, "w_exp": w_exp,
        "ck": i["cache_k"][0].reshape(L, PAIRS, 2, P, HD).transpose(0, 2, 4, 1, 3).reshape(L, P, PAIRS, P),
        "cv": i["cache_v"][0].transpose(0, 2, 1, 3).reshape(L, P, BW),
    }
    arrays = {k: np.ascontiguousarray(v) for k, v in arrays.items()}
    nc = bacc.Bacc("TRN2", target_bir_lowering=False, num_devices=1)
    a = {k: nc.dram_tensor(f"in_{k}", v.shape, F32, kind="ExternalInput").ap() for k, v in arrays.items()}
    a["x_store"] = nc.dram_tensor("x_store", (P, KC * TOK), F32, kind="Internal").ap()
    for name, shape in (("y", (P, KC, TOK)), ("new_k", (L, P, PAIRS, CTX)), ("new_v", (L, CTX, BW))):
        a[name] = nc.dram_tensor(f"out_{name}", shape, F32, kind="ExternalOutput").ap()
    step_kernel(nc, a)
    r = run(nc, [{f"in_{k}": v for k, v in arrays.items()}], core_ids=[0]).results[0]
    y = r["out_y"].transpose(1, 0, 2).reshape(D, TOK).T
    new_k = r["out_new_k"].reshape(L, 2, HD, PAIRS, CTX).transpose(0, 3, 1, 4, 2).reshape(1, L, HEADS, CTX, HD)
    new_v = r["out_new_v"].reshape(L, CTX, HEADS, HD).transpose(0, 2, 1, 3)[None]
    return (np.ascontiguousarray(y[LAT:][None]), np.ascontiguousarray(y[:LAT][None]),
            np.ascontiguousarray(new_k), np.ascontiguousarray(new_v))
```
